# Optimizing a Trainium2 kernel written in Bass

```python
import jax, jax.numpy as jnp
from jax import lax
import numpy as np

D_MODEL = 1024
BATCH = 1
SEQ = 1024
DEPTH = 1
DEC_BATCH = 8
DEC_SEQ = 1
PAST_LEN = 2048
PAGE_SIZE = 128

HEAD_DIM = 64
N_Q_HEADS = 8
N_KV_HEADS = 2
GQA_GROUP = N_Q_HEADS // N_KV_HEADS
ATTN_WIDTH = N_Q_HEADS * HEAD_DIM
KV_WIDTH = N_KV_HEADS * HEAD_DIM
WINDOW = 128
ROT_DIM = HEAD_DIM // 4
ROPE_THETA = 500000.0
N_REC_HEADS = 4
REC_DK = 128
REC_DV = 128
REC_WIDTH = N_REC_HEADS * REC_DK
REC_VWIDTH = N_REC_HEADS * REC_DV
REC_CHUNK = 64
MIX_WIDTH = ATTN_WIDTH + REC_VWIDTH
IN_SIZES = (ATTN_WIDTH, KV_WIDTH, KV_WIDTH, REC_WIDTH, REC_WIDTH, REC_VWIDTH, REC_VWIDTH)
IN_WIDTH = sum(IN_SIZES)
SPLIT_POINTS = tuple(int(s) for s in np.cumsum(IN_SIZES)[:-1])
D_FF = -(-8 * D_MODEL // (3 * 256)) * 256
EPS = 1e-6

kernel_name = 'hymba_swa_sink_hgrn2_decode_step'

F32 = jnp.float32

def _rmsnorm(x, g):
    xf = x.astype(F32)
    y = xf * lax.rsqrt(jnp.mean(xf * xf, axis=-1, keepdims=True) + EPS)
    return (y * g.astype(F32)).astype(x.dtype)

def _rope(x, pos):
    half = ROT_DIM // 2
    inv_freq = jnp.exp(-jnp.log(jnp.asarray(ROPE_THETA, F32)) * jnp.arange(half, dtype=F32) * (2.0 / ROT_DIM))
    ang = pos[:, None] * inv_freq[None, :]
    cos = jnp.cos(ang)[None, :, None, :]
    sin = jnp.sin(ang)[None, :, None, :]
    x1 = x[..., :half]
    x2 = x[..., half:ROT_DIM]
    return jnp.concatenate([x1 * cos - x2 * sin, x2 * cos + x1 * sin, x[..., ROT_DIM:]], axis=-1)

def _sink_probs(s, sink):
    m = jnp.maximum(jnp.max(s, axis=-1, keepdims=True), sink)
    p = jnp.exp(s - m)
    return p / (jnp.sum(p, axis=-1, keepdims=True) + jnp.exp(sink - m))

def _swa_prompt(q, k, v, sinks):
    B, T = q.shape[:2]
    nb = -(-T // WINDOW)
    pad = nb * WINDOW - T
    if pad:
        cfg = ((0, 0), (0, pad), (0, 0), (0, 0))
        q, k, v = jnp.pad(q, cfg), jnp.pad(k, cfg), jnp.pad(v, cfg)
    qb = q.reshape(B, nb, WINDOW, N_KV_HEADS, GQA_GROUP, HEAD_DIM)
    kb = k.reshape(B, nb, WINDOW, N_KV_HEADS, HEAD_DIM)
    vb = v.reshape(B, nb, WINDOW, N_KV_HEADS, HEAD_DIM)
    kk = jnp.concatenate([jnp.concatenate([jnp.zeros_like(kb[:, :1]), kb[:, :-1]], axis=1), kb], axis=2)
    vv = jnp.concatenate([jnp.concatenate([jnp.zeros_like(vb[:, :1]), vb[:, :-1]], axis=1), vb], axis=2)
    s = jnp.einsum('bnqhgd,bnkhd->bnhgqk', qb, kk) * (HEAD_DIM ** -0.5)
    qi = WINDOW + jnp.arange(WINDOW)
    ki = jnp.arange(2 * WINDOW)
    band = (ki[None, :] <= qi[:, None]) & (qi[:, None] - ki[None, :] < WINDOW)
    no_prev = (jnp.arange(nb)[:, None, None] == 0) & (ki < WINDOW)[None, None, :]
    valid = band[None] & ~no_prev
    s = jnp.where(valid[None, :, None, None], s, -jnp.inf)
    p = _sink_probs(s, sinks.reshape(1, 1, N_KV_HEADS, GQA_GROUP, 1, 1))
    o = jnp.einsum('bnhgqk,bnkhd->bnqhgd', p, vv)
    return o.reshape(B, nb * WINDOW, ATTN_WIDTH)[:, :T]

def _swa_sample(q, k, v, k_buf, v_buf, sinks, pos0):
    B, T = q.shape[:2]
    w_keep = k_buf.shape[1]
    kk = jnp.concatenate([k_buf.astype(F32), k], axis=1)
    vv = jnp.concatenate([v_buf.astype(F32), v], axis=1)
    qpos = pos0 + jnp.arange(T)
    kpos = pos0 - w_keep + jnp.arange(w_keep + T)
    valid = (kpos[None, :] <= qpos[:, None]) & (qpos[:, None] - kpos[None, :] < WINDOW)
    qg = q.reshape(B, T, N_KV_HEADS, GQA_GROUP, HEAD_DIM)
    s = jnp.einsum('bqhgd,bkhd->bhgqk', qg, kk) * (HEAD_DIM ** -0.5)
    s = jnp.where(valid[None, None, None], s, -jnp.inf)
    p = _sink_probs(s, sinks.reshape(1, N_KV_HEADS, GQA_GROUP, 1, 1))
    o = jnp.einsum('bhgqk,bkhd->bqhgd', p, vv).reshape(B, T, ATTN_WIDTH)
    return o, kk[:, -w_keep:], vv[:, -w_keep:]

def _hgrn2_scan(q, log_f, k, i, S0):
    B, T = q.shape[:2]
    C = min(REC_CHUNK, T)
    nc = -(-T // C)
    pad = nc * C - T
    if pad:
        cfg = ((0, 0), (0, pad), (0, 0), (0, 0))
        q, log_f, k, i = jnp.pad(q, cfg), jnp.pad(log_f, cfg), jnp.pad(k, cfg), jnp.pad(i, cfg)

    def to_chunks(a):
        return a.reshape(B, nc, C, *a.shape[2:]).swapaxes(0, 1)

    tri = jnp.tril(jnp.ones((C, C), dtype=bool))[None, :, :, None, None]

    def step(S, inp):
        qc, lc, kc, ic = inp
        b = jnp.cumsum(lc, axis=1)
        inter = jnp.einsum('bthk,bhkv->bthv', qc * jnp.exp(b), S)
        decay = jnp.exp(jnp.where(tri, b[:, :, None] - b[:, None, :], -jnp.inf))
        scores = jnp.einsum('btshk,bthk,bshk->btsh', decay, qc, kc)
        intra = jnp.einsum('btsh,bshv->bthv', scores, ic)
        b_last = b[:, -1]
        S_new = jnp.exp(b_last)[..., None] * S + jnp.einsum('bshk,bshv->bhkv', kc * jnp.exp(b_last[:, None] - b), ic)
        return S_new, inter + intra

    S_fin, o = lax.scan(step, S0, (to_chunks(q), to_chunks(log_f), to_chunks(k), to_chunks(i)))
    o = o.swapaxes(0, 1).reshape(B, nc * C, N_REC_HEADS, REC_DV)[:, :T]
    return o, S_fin

def _layer(x, pos0, w_in, w_out, w_gate, w_up, w_down, g_pre_mix, g_post_mix, g_pre_ffn, g_post_ffn,
           sinks, lb, rec_norm, k_buf, v_buf, S0):
    B, T, _ = x.shape
    h = _rmsnorm(x, g_pre_mix)
    aq, ak, av, rq, rf, ri, rg = jnp.split(h @ w_in, SPLIT_POINTS, axis=-1)
    pos = pos0 + jnp.arange(T, dtype=F32)
    q = _rope(aq.astype(F32).reshape(B, T, N_Q_HEADS, HEAD_DIM), pos)
    k = _rope(ak.astype(F32).reshape(B, T, N_KV_HEADS, HEAD_DIM), pos)
    v = av.astype(F32).reshape(B, T, N_KV_HEADS, HEAD_DIM)
    sinks = sinks.astype(F32)
    if k_buf is None:
        a = _swa_prompt(q, k, v, sinks)
        keep = min(WINDOW, T)
        k_new, v_new = k[:, -keep:], v[:, -keep:]
    else:
        a, k_new, v_new = _swa_sample(q, k, v, k_buf, v_buf, sinks, pos0)
    f = lb + (1.0 - lb) * jax.nn.sigmoid(rf.astype(F32))
    log_f = jnp.log(f).reshape(B, T, N_REC_HEADS, REC_DK)
    kr = (1.0 - f).reshape(B, T, N_REC_HEADS, REC_DK)
    qr = jax.nn.silu(rq.astype(F32)).reshape(B, T, N_REC_HEADS, REC_DK)
    ir = ri.astype(F32).reshape(B, T, N_REC_HEADS, REC_DV)
    o, S_new = _hgrn2_scan(qr, log_f, kr, ir, S0)
    o = o * lax.rsqrt(jnp.mean(o * o, axis=-1, keepdims=True) + EPS) * rec_norm.astype(F32)
    o = o.reshape(B, T, REC_VWIDTH) * jax.nn.silu(rg.astype(F32))
    mix = jnp.concatenate([a, o], axis=-1).astype(x.dtype) @ w_out
    x = x + _rmsnorm(mix, g_post_mix)
    h2 = _rmsnorm(x, g_pre_ffn)
    ffn = (jax.nn.silu(h2 @ w_gate) * (h2 @ w_up)) @ w_down
    x = x + _rmsnorm(ffn, g_post_ffn)
    return x, k_new, v_new, S_new

def setup_inputs(seed: int = 0) -> dict:
    key = jax.random.key(seed)
    ks = jax.random.split(key, 20)
    w_keep = min(WINDOW, PAST_LEN)
    nrm = jax.random.normal
    return {
        'x_prompt': nrm(ks[0], (BATCH, SEQ, D_MODEL), F32),
        'x_sample': nrm(ks[1], (DEC_BATCH, DEC_SEQ, D_MODEL), F32),
        'cache_k_win': nrm(ks[2], (DEPTH, DEC_BATCH, w_keep, N_KV_HEADS, HEAD_DIM), F32),
        'cache_v_win': nrm(ks[3], (DEPTH, DEC_BATCH, w_keep, N_KV_HEADS, HEAD_DIM), F32),
        'state_hgrn': 0.5 * nrm(ks[4], (DEPTH, DEC_BATCH, N_REC_HEADS, REC_DK, REC_DV), F32),
        'w_in': nrm(ks[5], (DEPTH, D_MODEL, IN_WIDTH), F32) * D_MODEL ** -0.5,
        'w_out': nrm(ks[6], (DEPTH, MIX_WIDTH, D_MODEL), F32) * MIX_WIDTH ** -0.5,
        'w_gate': nrm(ks[7], (DEPTH, D_MODEL, D_FF), F32) * D_MODEL ** -0.5,
        'w_up': nrm(ks[8], (DEPTH, D_MODEL, D_FF), F32) * D_MODEL ** -0.5,
        'w_down': nrm(ks[9], (DEPTH, D_FF, D_MODEL), F32) * D_FF ** -0.5,
        'norm_pre_mix': 1.0 + 0.02 * nrm(ks[10], (DEPTH, D_MODEL), F32),
        'norm_post_mix': 1.0 + 0.02 * nrm(ks[11], (DEPTH, D_MODEL), F32),
        'norm_pre_ffn': 1.0 + 0.02 * nrm(ks[12], (DEPTH, D_MODEL), F32),
        'norm_post_ffn': 1.0 + 0.02 * nrm(ks[13], (DEPTH, D_MODEL), F32),
        'attn_sinks': nrm(ks[14], (DEPTH, N_Q_HEADS), F32),
        'rec_lb': 0.5 * nrm(ks[15], (DEPTH + 1, REC_WIDTH), F32),
        'rec_out_norm': 1.0 + 0.02 * nrm(ks[16], (DEPTH, N_REC_HEADS, REC_DV), F32),
    }

def reference(x_prompt, x_sample, cache_k_win, cache_v_win, state_hgrn, w_in, w_out, w_gate, w_up, w_down,
              norm_pre_mix, norm_post_mix, norm_pre_ffn, norm_post_ffn, attn_sinks, rec_lb, rec_out_norm):
    lbs = jnp.cumsum(jax.nn.softmax(rec_lb.astype(F32), axis=0), axis=0)
    yp, ys = x_prompt, x_sample
    kp_l, vp_l, sp_l, ks_l, vs_l, ss_l = [], [], [], [], [], []
    for l in range(DEPTH):
        shared = (w_in[l], w_out[l], w_gate[l], w_up[l], w_down[l], norm_pre_mix[l], norm_post_mix[l],
                  norm_pre_ffn[l], norm_post_ffn[l], attn_sinks[l], lbs[l], rec_out_norm[l])
        S0 = jnp.zeros((yp.shape[0], N_REC_HEADS, REC_DK, REC_DV), F32)
        yp, kp, vp, sp = _layer(yp, 0, *shared, None, None, S0)
        ys, kn, vn, sn = _layer(ys, PAST_LEN, *shared, cache_k_win[l], cache_v_win[l], state_hgrn[l].astype(F32))
        kp_l.append(kp.astype(cache_k_win.dtype)); vp_l.append(vp.astype(cache_v_win.dtype)); sp_l.append(sp.astype(state_hgrn.dtype))
        ks_l.append(kn.astype(cache_k_win.dtype)); vs_l.append(vn.astype(cache_v_win.dtype)); ss_l.append(sn.astype(state_hgrn.dtype))
    new_k_win_prompt = jnp.stack(kp_l)
    new_v_win_prompt = jnp.stack(vp_l)
    new_state_prompt = jnp.stack(sp_l)
    new_k_win_sample = jnp.stack(ks_l)
    new_v_win_sample = jnp.stack(vs_l)
    new_state_sample = jnp.stack(ss_l)
    return (yp, ys, new_k_win_prompt, new_v_win_prompt, new_state_prompt, new_k_win_sample, new_v_win_sample, new_state_sample)


_drawn_inputs = setup_inputs


def setup_inputs(seed=0):
    import zlib

    import numpy as np

    out = dict(_drawn_inputs(seed))
    spreads = {}
    factors = {'norm_post_mix': 3.39,
     'norm_pre_ffn': 3.478,
     'norm_post_ffn': 4.751,
     'attn_sinks': 3.609,
     'rec_out_norm': 3.352}
    for name, (base, spread) in spreads.items():
        noise = np.random.default_rng([zlib.crc32(name.encode()), seed]).standard_normal(out[name].shape)
        drawn = base * np.exp(spread * noise) if base else spread * noise
        out[name] = __import__('jax').numpy.asarray(drawn.astype(out[name].dtype))
    for name, factor in factors.items():
        out[name] = (out[name] * factor).astype(out[name].dtype)
    return out
```

```python
import math

import numpy as np

import concourse.bass as bass
from concourse import mybir

F32 = mybir.dt.float32
F32R = mybir.dt.float32r
U8 = mybir.dt.uint8
ALU = mybir.AluOpType
ACT = mybir.ActivationFunctionType
AX = mybir.AxisListType

P = 128
DM = 1024
SEQ, DECB = 1024, 8
ROWS = SEQ + DECB
KT = DM // P
HD, NQ, NKV = 64, 8, 2
GRP = NQ // NKV
WIN = 128
NREC, RD = 4, 128
DFF = 2816
FT = DFF // P
CH = 3
CW = ROWS // CH
NBLK = SEQ // P
RT = NBLK + 1
LEVELS = 7
PAST = 2048
ROT = HD // 4
THETA = 500000.0
EPS = 1e-6
SCALE = HD ** -0.5
NEG = -1.0e30

CQ, CK, CV = 0, NQ * HD, NQ * HD + NKV * HD
CRQ = CV + NKV * HD
CRF, CRI, CRG = CRQ + NREC * RD, CRQ + 2 * NREC * RD, CRQ + 3 * NREC * RD

TILES = [("k", 0), ("v", 0)] + [("q", t) for t in range(4)]
for _h in range(NREC):
    TILES += [("rq", _h), ("ri", _h), ("rf", _h)]
TILES += [("rg", h) for h in range(NREC)]
NIN = len(TILES)
NOUT = DM // P
N12 = NIN + NOUT
UNITS = NIN * CH
TICKS = 2 * UNITS
AT0 = 22
NITEM = 4 * NBLK
HG0, HGS = 55, 18
SA0 = 94
SR0, SRS = 102, 5
GROUPS = FT // 2


def rows_of(i):
    return (P * i, P if i < NBLK else DECB)


def shape_constants():
    ident = np.eye(P, dtype=np.float32)
    perm = np.zeros((P, P), np.float32)
    half = ROT // 2
    for b in range(0, P, HD):
        for d in range(half):
            perm[b + d + half, b + d] = -1.0
            perm[b + d, b + d + half] = 1.0
    q = WIN + np.arange(WIN)[:, None]
    k = np.arange(2 * WIN)[None, :]
    band = (k <= q) & (q - k < WIN)
    amask = np.where(band, 0.0, NEG).astype(np.float32)
    s, t = np.arange(P)[:, None], np.arange(P)[None, :]
    lmask = np.stack([(s // (2 * h) == t // (2 * h)) & (s // h % 2 == 0) & (t // h % 2 == 1)
                      for h in (2 ** n for n in range(LEVELS))], axis=1).astype(np.float32)
    pos = np.concatenate([np.arange(SEQ), np.full(DECB, PAST)]).astype(np.float32)
    inv = np.exp(-np.log(np.float32(THETA)) * np.arange(half, dtype=np.float32) * np.float32(2.0 / ROT))
    ang = (pos[None, :] * inv.astype(np.float32)[:, None]).astype(np.float32)
    cos, sin = np.ones((P, ROWS), np.float32), np.zeros((P, ROWS), np.float32)
    for b in range(0, P, HD):
        for d in range(ROT):
            cos[b + d], sin[b + d] = np.cos(ang[d % half]), np.sin(ang[d % half])
    return {"c_ident": ident, "c_perm": perm, "c_amask": amask, "c_lmask": lmask, "c_cos": cos, "c_sin": sin}


def build(nc, t_in, t_out):
    base = (nc.sbuf_base + 31) // 32 * 32
    end = nc.sbuf_top // 32 * 32

    def at(name, shape, dt, offset):
        size = math.prod(shape[1:]) * (1 if dt == U8 else 4)
        assert offset + size <= end, (name, offset + size - end)
        return nc.alloc_sbuf_tensor_at(name, shape, dt, offset=offset), (offset + size + 31) // 32 * 32

    o = base
    act_hi, o = at("act_hi", [P, KT, ROWS], F32R, o)
    act_lo, o = at("act_lo", [P, KT, ROWS], F32R, o)
    mix, o = at("mix", [P, KT, ROWS], F32, o)
    w_hi, o = at("w_hi", [P, 4, KT, P], F32R, o)
    w_lo, o = at("w_lo", [P, 4, KT, P], F32R, o)
    raw, o = at("raw", [P, 2, KT, P], F32, o)
    ident, o = at("ident", [P, P], F32, o)
    small_from = o

    def small(name, shape):
        nonlocal o
        x, o = at(name, shape, F32, o)
        return x

    eps = small("eps", [P, 1])
    ss = small("ss", [P, 2, RT])
    std = small("std", [P, 2, RT])
    rstd = small("rstd", [P, 2, RT])
    lbl = small("lbl", [P, 2, NREC])
    lbt = small("lbt", [P, 8, NREC])
    rnorm = small("rnorm", [P, NREC])
    sink = small("sink", [P, NQ])
    nsink = small("nsink", [P, NQ])
    mx = small("mx", [P, 2, 2])
    negm = small("negm", [P, 2, 2])
    tsum = small("tsum", [P, 2, 2])
    esk = small("esk", [P, 2, 2])
    den = small("den", [P, 2, 2])
    rden = small("rden", [P, 2, 2])
    oss = small("oss", [P, NBLK])
    ostd = small("ostd", [P, NBLK])
    orstd = small("orstd", [P, NBLK])
    q_s = small("q_s", [P, NREC, DECB])
    f_s = small("f_s", [P, NREC, DECB])
    i_s = small("i_s", [P, NREC, DECB])
    k_s = small("k_s", [P, NREC, DECB])
    g_s = small("g_s", [P, NREC, DECB])
    o_s = small("o_s", [P, NREC, DECB])
    kn_s = small("kn_s", [DECB, P])
    qp = small("qp", [P, DECB, NQ])
    stx = small("stx", [P, DECB * NQ])
    ptx = small("ptx", [P, DECB * NQ])
    sinkc = small("sinkc", [DECB * NQ, 1])
    sst = small("sst", [P, 8])
    assert o - small_from <= 4096, o - small_from
    region = small_from + 4096

    o = region
    kt2, o = at("kt2", [P, NKV, ROWS], F32, o)
    vrow, o = at("vrow", [P, RT, P], F32, o)
    at_in = o
    r_i, o = at("r_i", [P, ROWS], F32, o)
    r_q, o = at("r_q", [P, ROWS], F32, o)
    r_f, o = at("r_f", [P, ROWS], F32, o)
    th, o = at("th", [P, 2, CW], F32, o)
    at_att = o
    sm, o = at("sm", [P, 2, 2 * WIN], F32, o)
    prob, o = at("prob", [P, 2, 2, 2 * WIN], F32, o)
    pt, o = at("pt", [P, 4, P], F32, o)
    orow, o = at("orow", [P, 2, HD], F32, o)
    amask, o = at("amask", [P, 2 * WIN], F32, o)
    lmask, o = at("lmask", [P, LEVELS, P], U8, o)
    hq, o = at("hq", [P, SEQ], F32, o)
    hk, o = at("hk", [P, SEQ], F32, o)
    hg, o = at("hg", [P, 1016], F32, o)
    ast, o = at("ast", [P, NBLK, P], F32, o)
    irow, o = at("irow", [P, NBLK, P], F32, o)
    at_krow = o
    krow, o = at("krow", [P, NBLK, P], F32, o)
    states, o = at("states", [P, NBLK + 1, P], F32, o)
    cos, oo = at("cos", [P, ROWS], F32, at_krow)
    sin, oo = at("sin", [P, ROWS], F32, oo)
    perm, _ = at("perm", [P, P], F32, at_krow - 2 * 4096 - 4064)
    kwin, _ = at("kwin", [P, P], F32, at_krow - 2 * 4096)
    lmask32, _ = at("lmask32", [P, LEVELS, P], F32, at_krow - 4096)
    kraw = r_f
    vt = r_i
    xr0, oo = at("xr0", [P, 2, DM], F32, at_in)
    hr0, oo = at("hr0", [P, 2, DM], F32, oo)
    gb0, oo = at("gb0", [P, DM], F32, oo)
    assert oo <= at_krow - 2 * 4096 - 4064
    ks, oo = at("ks", [P, DECB, P], F32, at_att)
    vs, oo = at("vs", [P, DECB, P], F32, oo)
    px, oo = at("px", [DECB * NQ, P], F32, oo)
    ki, oo = at("ki", [DECB, 2, P], F32, oo)
    kst, oo = at("kst", [P, DECB, P], F32, region)
    st, oo = at("st", [P, DECB, P], F32, oo)
    ib, _ = at("ib", [DECB, DECB, P], F32, region + 8256)
    orn = hk
    o = region
    h_hi, o = at("h_hi", [P, 2, ROWS], F32R, o)
    h_lo, o = at("h_lo", [P, 2, ROWS], F32R, o)
    sg, o = at("sg", [P, 2, CW], F32, o)
    hf, o = at("hf", [P, 2, CW], F32, o)
    free = o
    o = end - 6 * 4096
    d_hi, o = at("d_hi", [P, 2, DM], F32R, o)
    d_lo, o = at("d_lo", [P, 2, DM], F32R, o)
    draw, o = at("draw", [P, 2, DM], F32, o)
    o = free
    xr, o = at("xr", [P, 2, DM], F32, o)
    tr, o = at("tr", [P, 2, DM], F32, o)
    gbl, o = at("gbl", [P, DM], F32, o)
    assert o <= end - 6 * 4096
    gb2, o = at("gb2", [P, DM], F32, end - 6 * 4096)
    x2r, o = at("x2r", [P, 2, DM], F32, o)
    assert o <= end - 2 * 4096

    x2d = nc.dram_tensor("x2_scratch", (ROWS, DM), F32).ap()

    pair = [nc.alloc_psum_tensor(f"pair{i}", [P, 2, 512], F32) for i in range(4)]
    bank = [pair[i // 2][:, i % 2, :] for i in range(8)]
    J = [bank[0], bank[1]]
    BS, BP, BO, BR = bank[2], bank[3], bank[4], bank[5]
    BL = [bank[6], bank[7]]

    sems = {}

    def sem(name):
        if name not in sems:
            sems[name] = nc.alloc_semaphore(name)
        return sems[name]

    xp = t_in["x_prompt"].rearrange("b s d -> (b s) d")
    xs = t_in["x_sample"].rearrange("b s d -> (b s) d")
    w_in = t_in["w_in"][0]
    w_out = t_in["w_out"][0]
    yp = t_out["y_prompt"].rearrange("b s d -> (b s) d")
    ys = t_out["y_sample"].rearrange("b s d -> (b s) d")

    def x_rows(i):
        return xp[P * i:P * i + P, :] if i < NBLK else xs

    def y_rows(i):
        return yp[P * i:P * i + P, :] if i < NBLK else ys

    def gain(name):
        return t_in[name].partition_broadcast(P).rearrange("p o d -> p (o d)")

    def cols(c):
        return slice(CW * c, CW * c + CW)

    def bc(ap, shape):
        return ap.broadcast_to(shape)

    def g_level(n):
        off = sum(SEQ >> m for m in range(1, n))
        return hg[:, off:off + (SEQ >> n)]

    def weight_parts(n):
        dst = raw[:, n % 2]
        if n < NIN:
            kind, m = TILES[n]
            if kind == "q":
                return [(dst[:, :, HD * g:HD * g + HD],
                         w_in[:, CQ + HD * (m + GRP * g):CQ + HD * (m + GRP * g) + HD].rearrange("(k p) n -> p k n", p=P))
                        for g in range(NKV)]
            c = {"k": CK, "v": CV, "rq": CRQ, "rf": CRF, "ri": CRI, "rg": CRG}[kind] + P * m
            return [(dst, w_in[:, c:c + P].rearrange("(k p) n -> p k n", p=P))]
        c = P * (n - NIN)
        part = [(dst[HD * g:HD * g + HD, 0:4, :],
                 w_out[HD * GRP * g:HD * GRP * (g + 1), c:c + P].rearrange("(t p) n -> p t n", p=HD)) for g in range(NKV)]
        return part + [(dst[:, 4:8, :], w_out[4 * P:8 * P, c:c + P].rearrange("(k p) n -> p k n", p=P))]

    raw_count = []
    slot_total = [0, 0]
    for n in range(N12):
        slot_total[n % 2] += 16 * len(weight_parts(n))
        raw_count.append(slot_total[n % 2])
    for n in range(N12, N12 + 4):
        raw_count.append(slot_total[n % 2] + 16 * ((n - N12) // 2 + 1))

    def units_before(kinds, u):
        return sum(TILES[v // CH][0] in kinds for v in range(min(u, UNITS)))

    SILU = ("rq", "rg", "rf")
    ROPE = ("k", "q")
    WIN_LOADS = 2 * (1 + DECB) * 16
    NCONST = 8 * 16 + DECB * 16 + 16

    def attention_steps(tick):
        d = tick - AT0
        out = []
        if d % 2 == 0:
            for step, i in (("PT", d // 2 - 1), ("OT", d // 2 - 2), ("S", d // 2)):
                if 0 <= i < NITEM:
                    out.append((step, i))
        elif 0 <= (d - 3) // 2 < NITEM:
            out.append(("PV", (d - 3) // 2))
        return out

    def recurrence_steps(tick):
        out = []
        for h in range(NREC):
            d = tick - (HG0 + HGS * h)
            if d in (-4, -1):
                out.append(("it" + "ab"[d == -1], h))
            if d == -1:
                out.append(("prep", h))
            if d == 0:
                out.append(("diag", h))
            if 1 <= d <= LEVELS:
                out.append(("level", h, d - 1))
            out += [(s, h) for s, v in (("kta", 9), ("ktb", 10), ("u", 11), ("o", 13), ("ota", 15), ("otb", 16)) if d == v]
        return out

    def br_uses():
        out = []
        for tick in range(TICKS):
            out += rot_steps(tick)
            out += [("br", s) for s in recurrence_steps(tick) if s[0] in ("ita", "itb", "kta", "ktb", "ota", "otb")]
        return out

    ROPE_UNITS = [u for u in range(UNITS) if TILES[u // CH][0] in ROPE]

    def rot_steps(tick):
        out = []
        if tick % 2 == 1 and (tick - 3) // 2 in ROPE_UNITS and tick >= 3:
            out.append(("rot", ROPE_UNITS.index((tick - 3) // 2)))
        if tick in (12, 14, 16):
            out.append(("vt", (tick - 12) // 2))
        if tick == 10:
            out.append(("kw", 0))
        return out

    def sample_steps(tick):
        out = []
        d = tick - SA0
        out += [(s,) for s, v in (("ks_t", 0), ("s_score", 2), ("s_turn", 4), ("s_back", 6), ("s_out", 7)) if d == v]
        for h in range(NREC):
            d = tick - (SR0 + SRS * h)
            out += [(s, h) for s, v in (("r_turn", 0), ("r_outer", 1), ("r_o", 3)) if d == v]
        d = tick - (SR0 + SRS * NREC)
        out += [(s,) for s, v in (("r_rows", 0), ("r_cols", 2)) if d == v]
        return out

    V_GROUPS = [(0, 4), (4, 4), (8, 1)]

    block = nc.Block()
    blk = block.__enter__()

    @blk.sync
    def _(sp):
        def load_x(i, buf, free_sem, free_val):
            if i >= 2:
                sp.wait_ge(sem(free_sem), free_val)
            r, w = rows_of(i)
            sp.dma_start(buf[0:w, i % 2, :], x_rows(i)).then_inc(sem(f"x_in{i % 2}"), 16)

        def load_weight(n):
            if n >= 2:
                sp.wait_ge(sem("w_split"), n - 1)
            for dst, src in weight_parts(n):
                sp.dma_start(dst, src).then_inc(sem(f"raw_in{n % 2}"), 16)

        load_x(0, xr0, "", 0)
        sp.dma_start(gb0[:], gain("norm_pre_mix")).then_inc(sem("g_in"), 16)
        sp.dma_start(ident[:], t_in["c_ident"]).then_inc(sem("id_in"), 16)
        load_x(1, xr0, "", 0)
        load_weight(0)
        load_weight(1)
        for dst, src in ((perm[:], t_in["c_perm"]), (amask[:], t_in["c_amask"]), (lmask32[:], t_in["c_lmask"]),
                         (cos[:], t_in["c_cos"]), (sin[:], t_in["c_sin"]),
                         (sink[:], t_in["attn_sinks"].partition_broadcast(P).rearrange("p o h -> p (o h)"))):
            sp.dma_start(dst, src).then_inc(sem("const_in"), 16)
        for l in range(2):
            sp.dma_start(lbl[:, l, :], t_in["rec_lb"][l].rearrange("(h p) -> p h", p=P), allow_slow_non_contiguous=True).then_inc(sem("const_in"), 16)
        sp.dma_start(rnorm[:], t_in["rec_out_norm"][0].rearrange("h v -> v h"), allow_slow_non_contiguous=True).then_inc(sem("const_in"), 16)
        for b in range(DECB):
            sp.dma_start(sinkc[NQ * b:NQ * b + NQ, :], t_in["attn_sinks"].rearrange("o h -> h o"), allow_slow_non_contiguous=True).then_inc(sem("const_in"), 16)
        for i in range(2, RT):
            load_x(i, xr0, "h_rows", i - 1)
        stores = 0
        for tick in range(TICKS):
            if tick % 6 == 1 and tick // 6 + 2 < N12:
                load_weight(tick // 6 + 2)
            if tick == 12:
                sp.wait_ge(sem("kw_out"), 1)
                sp.dma_start(t_out["k_p"].rearrange("o b w n d -> (o b w) (n d)"), kwin[:]).then_inc(sem("stored"), 16)
            if tick == 18:
                sp.wait_ge(sem("v_rows"), 3)
                sp.dma_start(t_out["v_p"].rearrange("o b w n d -> (o b w) (n d)"), vrow[:, NBLK - 1, :]).then_inc(sem("stored"), 16)
            if tick == AT0 + 2 * NITEM + 6:
                sp.wait_ge(sem("at_out"), NITEM)
                sp.wait_ge(sem("kw_out"), 1)
                for dst, cache, new in ((ks, "cache_k_win", kn_s), (vs, "cache_v_win", vrow[:, NBLK, :])):
                    sp.dma_start(dst[0:P - 1, :, :], t_in[cache][0, :, 1:WIN].rearrange("b w n d -> w b (n d)"))\
                      .then_inc(sem("win_in"), 16)
                    for b in range(DECB):
                        sp.dma_start(dst[P - 1:P, b, :], new[b:b + 1, :]).then_inc(sem("win_in"), 16)
            if tick == SA0:
                sp.wait_ge(sem("win_in"), WIN_LOADS)
                for src, dst in ((ks, "k_s"), (vs, "v_s")):
                    sp.dma_start(t_out[dst][0].rearrange("b w n d -> w b (n d)"), src[:]).then_inc(sem("stored"), 16)
            for step in sample_steps(tick + 1):
                if step[0] == "r_turn":
                    h = step[1]
                    if h:
                        sp.wait_ge(sem("s_o"), h)
                        sp.wait_ge(sem("st_out"), 16 * h)
                    else:
                        sp.wait_ge(sem("at_out"), NITEM)
                    sp.dma_start(st[:], t_in["state_hgrn"][0, :, h].rearrange("b k v -> k b v")).then_inc(sem("st_in"), 16)
            for step in sample_steps(tick):
                if step[0] == "r_o":
                    h = step[1]
                    sp.wait_ge(sem("s_state"), 2 * h + 2)
                    sp.dma_start(t_out["st_s"][0, :, h].rearrange("b k v -> k b v"), st[:]).then_inc(sem("st_out"), 16)
            for step in recurrence_steps(tick):
                if step[0] == "o":
                    sp.wait_ge(sem("chain"), NBLK * (step[1] + 1))
                    sp.dma_start(t_out["st_p"][0, 0, step[1]], states[:, NBLK, :]).then_inc(sem("stp_out"), 16)
        for n in range(NIN + 1, N12 - 1):
            load_weight(n + 1)
        sp.wait_ge(sem("stored"), 64)
        sp.wait_ge(sem("st_out"), 16 * NREC)
        sp.wait_ge(sem("stp_out"), 16 * NREC)
        sp.wait_ge(sem("mix_lo"), KT)
        sp.dma_start(gbl[:], gain("norm_post_mix")).then_inc(sem("g_in"), 16)
        sp.dma_start(gb2[:], gain("norm_pre_ffn")).then_inc(sem("g_in"), 16)

        def ffn_raw(g, j, k):
            w = t_in["w_gate" if k == 0 else "w_up"][0]
            n = N12 + 4 * g + 2 * j + k
            sp.wait_ge(sem("w_split"), n - 1)
            sp.dma_start(raw[:, k], w[:, bass.ds(2 * P * g + P * j, P)].rearrange("(k p) n -> p k n", p=P))\
              .then_inc(sem(f"raw_in{k}"), 16)

        def load_row(i, buf, src, free_sem, free_val):
            if free_val > 0:
                sp.wait_ge(sem(free_sem), free_val)
            r, w = rows_of(i)
            sp.dma_start(buf[0:w, i % 2, :], src).then_inc(sem(f"x_in{i % 2}"), 16)

        load_row(0, xr, x_rows(0), "", 0)
        load_row(1, xr, x_rows(1), "", 0)
        for j in range(2):
            for k in range(2):
                ffn_raw(0, j, k)
        for i in range(RT):
            if i + 2 < RT:
                load_row(i + 2, xr, x_rows(i + 2), "x2", i + 1)
            sp.wait_ge(sem("x2"), i + 1)
            r, w = rows_of(i)
            sp.dma_start(x2d[r:r + w, :], x2r[0:w, i % 2, :]).then_inc(sem(f"x2_out{i % 2}"), 16)
        sp.wait_ge(sem("x2_out0"), 16 * 5)
        sp.wait_ge(sem("x2_out1"), 16 * 4)

        def ffn_down(g):
            for j in range(2):
                if not isinstance(g, int) or g > 0:
                    sp.wait_ge(sem("d_split"), 2 * g + j - 1)
                sp.dma_start(draw[:, j, :], t_in["w_down"][0, bass.ds(2 * P * g + P * j, P), :]).then_inc(sem(f"draw_in{j}"), 16)

        def ffn_loads(g):
            ffn_down(g)
            for j in range(2):
                for k in range(2):
                    ffn_raw(g + 1, j, k)

        ffn_loads(0)
        with sp.Fori(1, GROUPS - 1) as g:
            ffn_loads(g)
        ffn_down(GROUPS - 1)
        sp.dma_start(gbl[:], gain("norm_post_ffn")).then_inc(sem("g_in"), 16)
        load_row(0, xr, x2d[0:P, :], "", 0)
        load_row(1, xr, x2d[P:2 * P, :], "", 0)
        for i in range(RT):
            r, w = rows_of(i)
            sp.wait_ge(sem("y"), i + 1)
            sp.dma_start(y_rows(i), tr[0:w, i % 2, :]).then_inc(sem(f"y_out{i % 2}"), 16)
            if i + 2 < RT:
                r, w = rows_of(i + 2)
                load_row(i + 2, xr, x2d[r:r + w, :], "y", i + 1)
        sp.wait_ge(sem("y_out0"), 16 * 5)
        sp.wait_ge(sem("y_out1"), 16 * 4)

    @blk.gpsimd
    def _(pool):
        def weight_lo(n, slot=None):
            slot = n % 4 if slot is None else slot
            pool.wait_ge(sem("w_hi_done"), n + 1)
            pool.tensor_tensor(w_lo[:, slot], raw[:, slot % 2], w_hi[:, slot].bitcast(F32), ALU.subtract)\
                .then_inc(sem("w_split"), 1)

        pool.memset(kt2[:], 0.0).then_inc(sem("kt2_zero"), 1)
        pool.memset(qp[:], 0.0).then_inc(sem("qp_zero"), 1)
        pool.wait_ge(sem("const_in"), NCONST)
        pool.tensor_copy(lmask[:], lmask32[:]).then_inc(sem("lmask_done"), 1)
        for n in range(2):
            weight_lo(n)
        for tick in range(TICKS):
            for step in recurrence_steps(tick):
                if step[0] == "prep":
                    h = step[1]
                    pool.wait_ge(sem("f_done"), h + 1)
                    if h:
                        pool.wait_ge(sem("chain"), NBLK * h)
                    for n in range(1, LEVELS + 1):
                        src = r_f[:, 0:SEQ] if n == 1 else g_level(n - 1)
                        if n > 1:
                            pool.wait_ge(sem("g_prod"), LEVELS * h + n - 1)
                        v = src.rearrange("p (b e) -> p b e", e=2)
                        pool.tensor_tensor(g_level(n), v[:, :, 0], v[:, :, 1], ALU.mult).then_inc(sem("g_prod"), 1)
            if tick % 6 == 1 and tick // 6 + 2 < NIN + 2:
                weight_lo(tick // 6 + 2)
        for n in range(NIN + 2, N12):
            weight_lo(n)
        for n in range(N12, N12 + 2):
            weight_lo(n, n % 4)
        for i in range(RT):
            r, w = rows_of(i)
            pool.wait_ge(sem("p_t"), i + 1)
            pool.wait_ge(sem(f"x_in{i % 2}"), 16 * (5 if i % 2 == 0 else 4) + 16 * (i // 2 + 1))
            if i >= 2:
                pool.wait_ge(sem(f"x2_out{i % 2}"), 16 * (i // 2))
                pool.wait_ge(sem("h2_rows"), i - 1)
            pool.tensor_tensor(x2r[0:w, i % 2, :], tr[0:w, i % 2, :], xr[0:w, i % 2, :], ALU.add).then_inc(sem("x2"), 1)
            if i in (3, 5):
                weight_lo(N12 + 2 + (i - 3) // 2, (N12 + 2 + (i - 3) // 2) % 4)

        def hidden_lo(g, j, c):
            q = 6 * g + 3 * j + c
            pool.wait_ge(sem("h_hi_done"), q + 1)
            pool.tensor_tensor(h_lo[:, j, cols(c)], hf[:, (3 * j + c) % 2, :], h_hi[:, j, cols(c)].bitcast(F32), ALU.subtract)\
                .then_inc(sem("h_lo_done"), 1)

        def ffn(g, more):
            for j in range(2):
                pool.wait_ge(sem("d_hi_done"), 2 * g + j + 1)
                pool.tensor_tensor(d_lo[:, j, :], draw[:, j, :], d_hi[:, j, :].bitcast(F32), ALU.subtract)\
                    .then_inc(sem("d_split"), 1)
            for j in range(2):
                for c in range(CH):
                    hidden_lo(g, j, c)
                if more:
                    for k in range(2):
                        weight_lo(4 * g + (N12 + 4 + 2 * j + k), (N12 + 2 * j + k) % 4)

        ffn(0, True)
        with pool.Fori(1, GROUPS - 1) as g:
            ffn(g, True)
        ffn(GROUPS - 1, False)
        for i in range(RT):
            r, w = rows_of(i)
            pool.wait_ge(sem("y_t"), i + 1)
            pool.wait_ge(sem(f"x_in{i % 2}"), 2 * 16 * (5 if i % 2 == 0 else 4) + 16 * (i // 2 + 1))
            pool.tensor_tensor(tr[0:w, i % 2, :], tr[0:w, i % 2, :], xr[0:w, i % 2, :], ALU.add).then_inc(sem("y"), 1)

    @blk.scalar
    def _(act):
        def copy(out, in_):
            return act.activation(out, in_, ACT.Copy)

        def weight_hi(n, slot=None, count=None, used=None):
            slot = n % 4 if slot is None else slot
            act.wait_ge(sem(f"raw_in{slot % 2}"), raw_count[n] if count is None else count)
            if used is not None:
                act.wait_ge(sem(used[0]), used[1])
            elif n >= 4:
                act.wait_ge(sem("unit"), CH * (n - 3))
            copy(w_hi[:, slot], raw[:, slot % 2]).then_inc(sem("w_hi_done"), 1)

        def root(out, in_, scale, done, value):
            act.wait_ge(sem(done), value)
            return act.activation(out, in_, ACT.Sqrt, bias=eps[0:out.shape[0], :], scale=scale)

        def squares(i):
            r, w = rows_of(i)
            act.wait_ge(sem(f"x_in{i % 2}"), 16 * (i // 2 + 1))
            if i >= 2:
                act.wait_ge(sem("n_tr"), 2 * (i - 1))
            act.activation(hr0[0:w, i % 2, :], xr0[0:w, i % 2, :], ACT.Square, accum_out=ss[0:w, 0, i:i + 1]).then_inc(sem("n_ss"), 1)
            root(std[0:w, 0, i:i + 1], ss[0:w, 0, i:i + 1], 1.0 / DM, "n_ss", i + 1).then_inc(sem("n_std"), 1)

        def high(i, tr_sem, hi_sem, first_bank):
            r, w = rows_of(i)
            for kk in range(2):
                q = 2 * i + kk
                act.wait_ge(sem(tr_sem), q + 1)
                copy(act_hi[:, 4 * kk:4 * kk + 4, r:r + w],
                     bank[first_bank + q % 4].rearrange("p (k r) -> p k r", k=4)[:, :, 0:w]).then_inc(sem(hi_sem), 1)

        act.wait_ge(sem("eps_set"), 1)
        squares(0)
        for i in range(RT):
            if i + 1 < RT:
                squares(i + 1)
            high(i, "n_tr", "n_hi", 0)
            if i in (3, 5):
                weight_hi((i - 3) // 2)
        act.wait_ge(sem("lb_in"), 1)
        act.activation(lbt[:, 2:4, :], lbt[:, 0:2, :], ACT.Exp).then_inc(sem("lb_exp"), 1)

        def unit_read(u):
            kind, m = TILES[u // CH]
            c = u % CH
            act.wait_ge(sem("unit"), u + 1)
            src = J[u % 2][:, 0:CW]
            if kind == "k":
                copy(kraw[:, cols(c)], src).then_inc(sem("unit_act"), 1)
            elif kind == "v":
                copy(vt[:, cols(c)], src).then_inc(sem("unit_act"), 1)
            elif kind == "q":
                copy(mix[:, m, cols(c)], src).then_inc(sem("unit_act"), 1)
            elif kind == "ri":
                if m:
                    act.wait_ge(sem("i_turned"), 2 * m)
                    act.wait_ge(sem("s_saved"), m)
                else:
                    act.wait_ge(sem("v_turned"), 3)
                copy(r_i[:, cols(c)], src).then_inc(sem("unit_act"), 1)
            else:
                s = units_before(SILU, u)
                if s >= 2:
                    act.wait_ge(sem("th_read"), s - 1)
                act.activation(th[:, s % 2, :], src, ACT.Tanh, scale=0.5).then_inc(sem("unit_act"), 1)

        for tick in range(TICKS):
            if tick % 6 == 1 and tick // 6 + 2 < NIN + 2:
                weight_hi(tick // 6 + 2)
            for step in rot_steps(tick):
                if step[0] == "vt":
                    act.wait_ge(sem("v_turned"), step[1] + 1)
                    b0, n = V_GROUPS[step[1]]
                    if n == 4:
                        copy(vrow[:, b0:b0 + 4, :], BR.rearrange("p (b d) -> p b d", b=4)).then_inc(sem("v_rows"), 1)
                    else:
                        copy(vrow[0:DECB, b0, :], BR[0:DECB, 0:P]).then_inc(sem("v_rows"), 1)
                if step[0] == "kw":
                    act.wait_ge(sem("kw_mm"), 1)
                    copy(kn_s[:, :], BR[0:DECB, P:2 * P])
                    copy(kwin[:], BR[:, 0:P]).then_inc(sem("kw_out"), 1)
            for step, i in attention_steps(tick):
                t, j, e = i // NBLK, i % NBLK, i % 2
                k0 = WIN if j == 0 else 0
                if step == "S":
                    act.wait_ge(sem("at_max"), i + 1)
                    if i >= 2:
                        act.wait_ge(sem("at_pt"), i - 1)
                    for g in range(NKV):
                        act.activation(prob[:, e, g, k0:], sm[:, g, k0:], ACT.Exp, bias=negm[:, e, g:g + 1], scale=SCALE,
                                       accum_out=den[:, e, g:g + 1])
                    act.activation(esk[:, e, :], tsum[:, e, :], ACT.Exp).then_inc(sem("at_exp"), 1)
                elif step == "PT":
                    act.wait_ge(sem("at_pt"), i + 1)
                    if i >= 1:
                        act.wait_ge(sem("at_pv"), i)
                    kb = 1 if j == 0 else 0
                    pv = pt[:].rearrange("p (g b) q -> p g b q", g=2)
                    bv = BP.rearrange("p (g b q) -> p g b q", g=2, b=2)
                    copy(pv[:, :, kb:, :], bv[:, :, kb:, :]).then_inc(sem("at_ptc"), 1)
                elif step == "OT":
                    act.wait_ge(sem("at_ot"), i + 1)
                    copy(mix[:, t, P * j:P * j + P], BO[:, P:2 * P]).then_inc(sem("at_out"), 1)
            for step in recurrence_steps(tick):
                h = step[1]
                if step[0] in ("ita", "itb"):
                    a = step[0] == "itb"
                    act.wait_ge(sem("i_turned"), 2 * h + a + 1)
                    if h and not a:
                        act.wait_ge(sem("o_mm"), h)
                    copy(irow[:, 4 * a:4 * a + 4, :], BR.rearrange("p (b d) -> p b d", b=4)).then_inc(sem("i_rows"), 1)
                if step[0] in ("kta", "ktb"):
                    a = step[0] == "ktb"
                    act.wait_ge(sem("k_turned"), 2 * h + a + 1)
                    copy(krow[:, 4 * a:4 * a + 4, :], BR.rearrange("p (b d) -> p b d", b=4)).then_inc(sem("k_rows"), 1)
                if step[0] == "o":
                    act.wait_ge(sem("o_mm"), h + 1)
                    for c in range(NBLK):
                        ins = act.activation(ast[:, c, :], BL[c // 4][:, P * (c % 4):P * (c % 4) + P], ACT.Square,
                                             accum_out=oss[:, c:c + 1])
                    ins.then_inc(sem("o_ss"), 1)
                    root(ostd[:], oss[:], 1.0 / (4 * RD), "o_ss", h + 1).then_inc(sem("o_std"), 1)
            for step in sample_steps(tick):
                if step[0] == "ks_t":
                    for a, b in ((0, BS), (1, BP)):
                        act.wait_ge(sem("ks_turned"), a + 1)
                        copy(kst[:, 4 * a:4 * a + 4, :], b.rearrange("p (b d) -> p b d", b=4)).then_inc(sem("ks_cols"), 1)
                if step[0] == "s_score":
                    act.wait_ge(sem("s_score"), 1)
                    copy(stx[:], BO[:, 0:DECB * NQ]).then_inc(sem("s_scored"), 1)
                if step[0] == "s_turn":
                    act.wait_ge(sem("s_max"), 1)
                    n = DECB * NQ
                    act.activation(px[:], BP[0:n, 0:P], ACT.Exp, bias=sst[0:n, 1:2], scale=SCALE, accum_out=sst[0:n, 3:4])
                    act.activation(sst[0:n, 4:5], sst[0:n, 2:3], ACT.Exp).then_inc(sem("s_exp"), 1)
                if step[0] == "s_back":
                    act.wait_ge(sem("s_back"), 1)
                    copy(ptx[:], BP[:, 0:DECB * NQ]).then_inc(sem("s_pt"), 1)
                if step[0] == "r_turn":
                    act.wait_ge(sem("s_turned"), step[1] + 1)
                    if step[1]:
                        act.wait_ge(sem("s_outer"), step[1])
                    copy(ki[:], BP[0:DECB, 0:2 * P].rearrange("p (a d) -> p a d", a=2)).then_inc(sem("s_ki"), 1)
                if step[0] == "r_rows":
                    n = NREC * DECB
                    act.wait_ge(sem("so_turned"), 1)
                    act.activation(px[0:n, :], BP[0:n, 0:P], ACT.Square, accum_out=sst[0:n, 5:6]).then_inc(sem("so_ss"), 1)
                    root(sst[0:n, 6:7], sst[0:n, 5:6], 1.0 / (4 * RD), "so_ss", 1).then_inc(sem("so_std"), 1)
            if tick % 2:
                unit_read(tick // 2)
        act.wait_ge(sem("mix_done"), 1)
        for k in range(KT):
            copy(act_hi[:, k, :], mix[:, k, :]).then_inc(sem("mix_hi"), 1)
        for m in range(NOUT):
            if NIN + 2 + m < N12 + 2:
                n = NIN + 2 + m
                weight_hi(n)
            if m == 0:
                act.wait_ge(sem("mix_lo"), KT)
            for c in range(CH):
                u = UNITS + CH * m + c
                act.wait_ge(sem("unit"), u + 1)
                copy(mix[:, m, cols(c)], J[u % 2][:, 0:CW]).then_inc(sem("unit_act"), 1)

        def post_squares(i):
            r, w = rows_of(i)
            act.wait_ge(sem("p_tr"), i + 1)
            if i >= 2:
                act.wait_ge(sem("h2_tr"), 2 * (i - 1))
            act.activation(tr[0:w, i % 2, :].rearrange("p (a b) -> p a b", a=2), pair[i % 2][0:w, :, :], ACT.Square,
                           accum_out=ss[0:w, 0, i:i + 1]).then_inc(sem("p_ss"), 1)
            root(std[0:w, 0, i:i + 1], ss[0:w, 0, i:i + 1], 1.0 / DM, "p_ss", i + 1).then_inc(sem("p_std"), 1)

        def pre_squares(i):
            r, w = rows_of(i)
            act.wait_ge(sem("x2"), i + 1)
            act.activation(tr[0:w, i % 2, :], x2r[0:w, i % 2, :], ACT.Square, accum_out=ss[0:w, 1, i:i + 1]).then_inc(sem("q_ss"), 1)
            root(std[0:w, 1, i:i + 1], ss[0:w, 1, i:i + 1], 1.0 / DM, "q_ss", i + 1).then_inc(sem("q_std"), 1)

        post_squares(0)
        for i in range(RT):
            if i + 1 < RT:
                post_squares(i + 1)
            pre_squares(i)
            if i >= 1:
                high(i - 1, "h2_tr", "h2_hi", 4)
            if i in (3, 5):
                weight_hi(N12 + 2 + (i - 3) // 2)
        high(RT - 1, "h2_tr", "h2_hi", 4)

        def gate(g, j, c):
            q = 6 * g + 3 * j + c
            e = (3 * j + c) % 2
            act.wait_ge(sem("gate_mm"), q + 1)
            if not (isinstance(g, int) and q < 2):
                act.wait_ge(sem("hf_done"), q - 1)
            act.activation(sg[:, e, :], bank[e][:, 0:CW], ACT.Silu).then_inc(sem("gate_done"), 1)

        def hidden_hi(g, j, c):
            q = 6 * g + 3 * j + c
            act.wait_ge(sem("hf_done"), q + 1)
            copy(h_hi[:, j, cols(c)], hf[:, (3 * j + c) % 2, :]).then_inc(sem("h_hi_done"), 1)

        def ffn(g, more):
            for j in range(2):
                act.wait_ge(sem(f"draw_in{j}"), 16 * g + 16)
                if not (isinstance(g, int) and g == 0):
                    act.wait_ge(sem("down_mm"), 24 * g)
                copy(d_hi[:, j, :], draw[:, j, :]).then_inc(sem("d_hi_done"), 1)
            for j in range(2):
                for c in range(CH):
                    gate(g, j, c)
                    hidden_hi(g, j, c)
                if more:
                    for k in range(2):
                        n = 4 * g + (N12 + 4 + 2 * j + k)
                        weight_hi(n, (N12 + 2 * j + k) % 4, slot_total[k] + 16 * (2 + j + 1) + 32 * g,
                                  (("gate_mm", "up_mm")[k], 6 * g + (3 * j + 3)))

        ffn(0, True)
        with act.Fori(1, GROUPS - 1) as g:
            ffn(g, True)
        ffn(GROUPS - 1, False)

        for i in range(RT):
            r, w = rows_of(i)
            act.wait_ge(sem("y_tr"), i + 1)
            if i >= 2:
                act.wait_ge(sem(f"y_out{i % 2}"), 16 * (i // 2))
            act.activation(tr[0:w, i % 2, :].rearrange("p (a b) -> p a b", a=2), pair[i % 2][0:w, :, :], ACT.Square,
                           accum_out=ss[0:w, 1, i:i + 1]).then_inc(sem("y_ss"), 1)
            root(std[0:w, 1, i:i + 1], ss[0:w, 1, i:i + 1], 1.0 / DM, "y_ss", i + 1).then_inc(sem("y_std"), 1)

    @blk.tensor
    def _(pe):
        def rows_to_cols(src, i, b0, q_sem, free_sem, first):
            r, w = rows_of(i)
            for kk in range(2):
                q = 2 * i + kk
                if q >= 4:
                    pe.wait_ge(sem(free_sem), q - 3)
                for k in range(4):
                    mm = pe.transpose(bank[b0 + q % 4][:, P * k:P * k + w], src[0:w, i % 2, P * (4 * kk + k):P * (4 * kk + k) + P],
                                      ident[0:w, 0:w])
                mm.then_inc(sem(q_sem), 1)

        pe.wait_ge(sem("id_in"), 16)
        for i in range(RT):
            pe.wait_ge(sem("h_rows"), i + 1)
            rows_to_cols(hr0, i, 0, "n_tr", "n_lo", True)

        def products(out, slot, c, lo, hi):
            for k in range(lo, hi):
                for s, (a, b) in enumerate(((w_hi, act_hi), (w_hi, act_lo), (w_lo, act_hi))):
                    mm = pe.matmul(out, a[:, slot, k, :], b[:, k, cols(c)], start=(k == 0 and s == 0), stop=(k == KT - 1 and s == 2))
            return mm

        br_free = None

        def take_br(sem_name, value):
            nonlocal br_free
            if br_free is not None:
                pe.wait_ge(sem(br_free[0]), br_free[1])
            br_free = (sem_name, value)

        bl_free = None

        def take_bl(sem_name, value):
            nonlocal bl_free
            if bl_free is not None:
                pe.wait_ge(sem(bl_free[0]), bl_free[1])
            bl_free = (sem_name, value)

        pe.wait_ge(sem("n_lo"), 2 * RT)
        for tick in range(TICKS):
            u, half = tick // 2, tick % 2
            n = u // CH
            if half == 0:
                if u % CH == 0:
                    pe.wait_ge(sem("w_split"), n + 1)
                if u >= 2:
                    pe.wait_ge(sem("unit_act"), u - 1)
                    s = units_before(SILU, u - 1)
                    if TILES[(u - 2) // CH][0] in ("rq", "rg"):
                        pe.wait_ge(sem("th_read"), s)
            mm = products(J[u % 2][:, 0:CW], n % 4, u % CH, 4 * half, 4 * half + 4)
            if half:
                mm.then_inc(sem("unit"), 1)
            for step in rot_steps(tick):
                if step[0] == "rot":
                    r = step[1]
                    if r == 0:
                        pe.wait_ge(sem("const_in"), NCONST - 0)
                    v = ROPE_UNITS[r]
                    kind, m = TILES[v // CH]
                    pe.wait_ge(sem("unit_act"), v + 1)
                    src = kraw[:, cols(v % CH)] if kind == "k" else mix[:, m, cols(v % CH)]
                    take_br("rot_read", r + 1)
                    pe.matmul(BR[:, 0:CW], perm[:], src, start=True, stop=True).then_inc(sem("rot_mm"), 1)
                if step[0] == "vt":
                    b0, nb = V_GROUPS[step[1]]
                    pe.wait_ge(sem("unit_act"), 6)
                    take_br("v_rows", step[1] + 1)
                    for b in range(nb):
                        r, w = rows_of(b0 + b)
                        mm = pe.transpose(BR[0:w, P * b:P * b + P], vt[:, r:r + w], ident[:])
                    mm.then_inc(sem("v_turned"), 1)
                if step[0] == "kw":
                    pe.wait_ge(sem("rope"), CH)
                    take_br("kw_out", 1)
                    for (r, w), c in ((rows_of(NBLK - 1), 0), (rows_of(NBLK), P)):
                        for g in range(NKV):
                            mm = pe.matmul(BR[0:w, c:c + P], kt2[:, g, r:r + w], ident[:], start=(g == 0), stop=(g == NKV - 1))
                    mm.then_inc(sem("kw_mm"), 1)
            for step, i in attention_steps(tick):
                t, j, e = i // NBLK, i % NBLK, i % 2
                kbs = (1,) if j == 0 else (0, 1)
                if step == "S":
                    pe.wait_ge(sem("rope"), CH * (t + 2))
                    if i:
                        pe.wait_ge(sem("at_max"), i)
                    out = BS.rearrange("p (g k) -> p g k", g=2)
                    if j == 0:
                        pe.matmul(out[:, :, WIN:], mix[:, t, 0:P], kt2[:, :, 0:P], start=True, stop=True).then_inc(sem("at_s"), 1)
                    else:
                        pe.matmul(out, mix[:, t, P * j:P * j + P], kt2[:, :, P * (j - 1):P * (j + 1)],
                                  start=True, stop=True).then_inc(sem("at_s"), 1)
                elif step == "PT":
                    pe.wait_ge(sem("at_exp"), i + 1)
                    if i:
                        pe.wait_ge(sem("at_ptc"), i)
                    for g in range(NKV):
                        for kb in kbs:
                            mm = pe.transpose(BP[:, P * (2 * g + kb):P * (2 * g + kb) + P], prob[:, e, g, P * kb:P * kb + P], ident[:])
                    mm.then_inc(sem("at_pt"), 1)
                elif step == "PV":
                    pe.wait_ge(sem("at_ptc"), i + 1)
                    pe.wait_ge(sem("v_rows"), 3)
                    if i:
                        pe.wait_ge(sem("at_out"), i)
                    for g in range(NKV):
                        for kb in kbs:
                            mm = pe.matmul(BO[:, HD * g:HD * g + HD], pt[:, 2 * g + kb, :], vrow[:, j - 1 + kb, HD * g:HD * g + HD],
                                           start=(kb == kbs[0]), stop=(kb == 1))
                    mm.then_inc(sem("at_pv"), 1)
                elif step == "OT":
                    pe.wait_ge(sem("at_or"), i + 1)
                    pe.transpose(BO[:, P:2 * P], orow[:].rearrange("p g d -> p (g d)"), ident[:]).then_inc(sem("at_ot"), 1)
            for step in recurrence_steps(tick):
                h = step[1]
                if step[0] in ("ita", "itb"):
                    a = step[0] == "itb"
                    if not a:
                        pe.wait_ge(sem("unit_act"), CH * (8 + 3 * h))
                    take_br("i_rows", 2 * h + a + 1)
                    for b in range(4):
                        c = 4 * a + b
                        mm = pe.transpose(BR[:, P * b:P * b + P], r_i[:, P * c:P * c + P], ident[:])
                    mm.then_inc(sem("i_turned"), 1)
                if step[0] == "diag":
                    pe.wait_ge(sem("hq_prep"), h + 1)
                    take_bl("diag_read", h + 1)
                    for c in range(NBLK):
                        mm = pe.matmul(BL[c // 4][:, P * (c % 4):P * (c % 4) + P], hk[:, P * c:P * c + P], r_q[:, P * c:P * c + P],
                                       start=True, stop=True)
                    mm.then_inc(sem("diag_mm"), 1)
                if step[0] == "level":
                    n = step[2]
                    if n:
                        pe.wait_ge(sem("hq_step"), LEVELS * h + n)
                    take_bl("level_read", LEVELS * h + n + 1)
                    for c in range(NBLK):
                        mm = pe.matmul(BL[c // 4][:, P * (c % 4):P * (c % 4) + P], hk[:, P * c:P * c + P], hq[:, P * c:P * c + P],
                                       start=True, stop=True)
                    mm.then_inc(sem("level_mm"), 1)
                if step[0] in ("kta", "ktb"):
                    a = step[0] == "ktb"
                    pe.wait_ge(sem("hq_step"), LEVELS * (h + 1))
                    take_br("k_rows", 2 * h + a + 1)
                    for b in range(4):
                        c = 4 * a + b
                        mm = pe.transpose(BR[:, P * b:P * b + P], hk[:, P * c:P * c + P], ident[:])
                    mm.then_inc(sem("k_turned"), 1)
                if step[0] == "u":
                    pe.wait_ge(sem("k_rows"), 2 * h + 2)
                    pe.wait_ge(sem("i_rows"), 2 * h + 2)
                    take_bl("chain", NBLK * (h + 1))
                    for c in range(NBLK):
                        mm = pe.matmul(BL[c // 4][:, P * (c % 4):P * (c % 4) + P], krow[:, c, :], irow[:, c, :], start=True, stop=True)
                    mm.then_inc(sem("u_mm"), 1)
                if step[0] == "o":
                    take_bl("o_norm", h + 1)
                    for c in range(NBLK):
                        out = BL[c // 4][:, P * (c % 4):P * (c % 4) + P]
                        mm = pe.matmul(out, ast[:, c, :], irow[:, c, :], start=True, stop=(c == 0))
                        if c:
                            mm = pe.matmul(out, hq[:, P * c:P * c + P], states[:, c, :], start=False, stop=True)
                    mm.then_inc(sem("o_mm"), 1)
                if step[0] in ("ota", "otb"):
                    a = step[0] == "otb"
                    pe.wait_ge(sem("o_norm"), h + 1)
                    take_br("o_cols", 2 * h + a + 1)
                    for b in range(4):
                        c = 4 * a + b
                        mm = pe.transpose(BR[:, P * b:P * b + P], orn[:, P * c:P * c + P], ident[:])
                    mm.then_inc(sem("o_turned"), 1)
            for step in sample_steps(tick):
                if step[0] == "ks_t":
                    pe.wait_ge(sem("win_in"), WIN_LOADS)
                    pe.wait_ge(sem("at_out"), NITEM)
                    for a, b in ((0, BS), (1, BP)):
                        for c in range(4):
                            mm = pe.transpose(b[:, P * c:P * c + P], ks[:, 4 * a + c, :], ident[:])
                        mm.then_inc(sem("ks_turned"), 1)
                if step[0] == "s_score":
                    pe.wait_ge(sem("ks_cols"), 2)
                    pe.wait_ge(sem("qp_done"), 1)
                    for b in range(DECB):
                        mm = pe.matmul(BO[:, NQ * b:NQ * b + NQ], kst[:, b, :], qp[:, b, :], start=True, stop=True)
                    mm.then_inc(sem("s_score"), 1)
                if step[0] == "s_turn":
                    pe.wait_ge(sem("s_scored"), 1)
                    pe.transpose(BP[0:DECB * NQ, 0:P], stx[:], ident[:]).then_inc(sem("s_turn"), 1)
                if step[0] == "s_back":
                    pe.wait_ge(sem("s_prob"), 1)
                    pe.transpose(BP[:, 0:DECB * NQ], px[:], ident[0:DECB * NQ, 0:DECB * NQ]).then_inc(sem("s_back"), 1)
                if step[0] == "s_out":
                    pe.wait_ge(sem("s_pt"), 1)
                    for b in range(DECB):
                        mm = pe.matmul(BO[:, NQ * b:NQ * b + NQ], vs[:, b, :], ptx[:, NQ * b:NQ * b + NQ], start=True, stop=True)
                    mm.then_inc(sem("s_out"), 1)
                if step[0] == "r_turn":
                    h = step[1]
                    pe.wait_ge(sem("ks_saved"), h + 1)
                    if h:
                        pe.wait_ge(sem("s_os"), h)
                    for a, x in ((0, k_s), (1, i_s)):
                        mm = pe.transpose(BP[0:DECB, P * a:P * a + P], x[:, h, :], ident[:])
                    mm.then_inc(sem("s_turned"), 1)
                if step[0] == "r_outer":
                    h = step[1]
                    pe.wait_ge(sem("s_ib"), h + 1)
                    if h == 0:
                        pe.wait_ge(sem("s_mixed"), 1)
                    for a, b in ((0, BS), (1, BO)):
                        mm = pe.matmul(b, ki[:, 0, :], ib[:, 4 * a:4 * a + 4, :], start=True, stop=True)
                    mm.then_inc(sem("s_outer"), 1)
                if step[0] == "r_o":
                    h = step[1]
                    pe.wait_ge(sem("s_state"), 2 * h + 2)
                    for b in range(DECB):
                        mm = pe.matmul(BP[:, b:b + 1], st[:, b, :], q_s[:, h, b:b + 1], start=True, stop=True)
                    mm.then_inc(sem("s_o"), 1)
                if step[0] == "r_rows":
                    pe.wait_ge(sem("s_os"), NREC)
                    pe.transpose(BP[0:NREC * DECB, 0:P], o_s[:].rearrange("p h b -> p (h b)"), ident[:]).then_inc(sem("so_turned"), 1)
                if step[0] == "r_cols":
                    n = NREC * DECB
                    pe.wait_ge(sem("so_norm"), 1)
                    pe.transpose(BP[:, 0:n], px[0:n, :], ident[0:n, 0:n]).then_inc(sem("so_cols"), 1)
        for m in range(NOUT):
            n = NIN + m
            pe.wait_ge(sem("w_split"), n + 1)
            for c in range(CH):
                u = UNITS + CH * m + c
                pe.wait_ge(sem("unit_act"), u - 1)
                if m == 0 and c < 2:
                    pe.wait_ge(sem("th_read"), units_before(SILU, UNITS))
                for k in range(KT):
                    if m == 0 and c == 0:
                        pe.wait_ge(sem("mix_lo"), k + 1)
                    mm = products(J[u % 2][:, 0:CW], n % 4, c, k, k + 1)
                mm.then_inc(sem("unit"), 1)

        def cols_to_rows(i, out_sem):
            r, w = rows_of(i)
            for m in range(KT):
                mm = pe.transpose(pair[i % 2][0:w, m // 4, P * (m % 4):P * (m % 4) + P], mix[:, m, r:r + w], ident[:])
            mm.then_inc(sem(out_sem), 1)

        pe.wait_ge(sem("unit_act"), UNITS + CH * NOUT)
        for i in range(RT + 1):
            if i < RT:
                if i >= 2:
                    pe.wait_ge(sem("p_t"), i - 1)
                cols_to_rows(i, "p_tr")
            if i >= 1:
                pe.wait_ge(sem("h2_rows"), i)
                rows_to_cols(tr, i - 1, 4, "h2_tr", "h2_lo", True)
        pe.wait_ge(sem("h2_lo"), 2 * RT)

        def ffn(g, first, last):
            for j in range(2):
                for c in range(CH):
                    q = 6 * g + 3 * j + c
                    e = (3 * j + c) % 2
                    if c == 0:
                        pe.wait_ge(sem("w_split"), 4 * g + (N12 + 2 * j + 1))
                    if not (first and 3 * j + c < 2):
                        pe.wait_ge(sem("gate_done"), q - 1)
                    products(bank[e][:, 0:CW], (N12 + 2 * j) % 4, c, 0, KT).then_inc(sem("gate_mm"), 1)
                    if c == 0:
                        pe.wait_ge(sem("w_split"), 4 * g + (N12 + 2 * j + 2))
                    if not (first and 3 * j + c < 2):
                        pe.wait_ge(sem("hf_done"), q - 1)
                    products(bank[2 + e][:, 0:CW], (N12 + 2 * j + 1) % 4, c, 0, KT).then_inc(sem("up_mm"), 1)
            pe.wait_ge(sem("d_split"), 2 * g + 2)
            for c in range(CH):
                pe.wait_ge(sem("h_lo_done"), 6 * g + (4 + c))
                for m in range(KT):
                    v = KT * c + m
                    if not (first and v < 4):
                        pe.wait_ge(sem("acc_done"), 24 * g + (v - 3))
                    for j in range(2):
                        for s, (a, b) in enumerate(((d_hi, h_hi), (d_hi, h_lo), (d_lo, h_hi))):
                            mm = pe.matmul(bank[4 + v % 4][:, 0:CW], a[:, j, P * m:P * m + P], b[:, j, cols(c)],
                                           start=(j == 0 and s == 0), stop=(j == 1 and s == 2))
                    mm.then_inc(sem("down_mm"), 1)
                    if last and c > 0 and m == 2:
                        for i in ((0, 1) if c == 1 else (2, 3)):
                            last_rows(i)

        def last_rows(i):
            r, w = rows_of(i)
            pe.wait_ge(sem("acc_done"), 24 * (GROUPS - 1) + KT * ((r + w - 1) // CW + 1))
            if i < 2:
                pe.wait_ge(sem("hf_done"), 6 * GROUPS)
                pe.wait_ge(sem("gate_done"), 6 * GROUPS)
            else:
                pe.wait_ge(sem("y_t"), i - 1)
            cols_to_rows(i, "y_tr")

        ffn(0, True, False)
        with pe.Fori(1, GROUPS - 1) as g:
            ffn(g, False, False)
        ffn(GROUPS - 1, False, True)
        for i in range(4, RT):
            last_rows(i)

    @blk.vector
    def _(dve):
        chain = [0]

        def then(ins):
            chain[0] += 1
            ins.then_inc(sem("dve_chain"), 1)
            dve.wait_ge(sem("dve_chain"), chain[0])

        dve.memset(eps[:], EPS).then_inc(sem("eps_set"), 1)

        def norm_rows(i):
            r, w = rows_of(i)
            dve.wait_ge(sem("n_std"), i + 1)
            then(dve.reciprocal(rstd[0:w, 0, i:i + 1], std[0:w, 0, i:i + 1]))
            if i == 0:
                dve.wait_ge(sem("g_in"), 16)
            dve.scalar_tensor_tensor(out=hr0[0:w, i % 2, :], in0=xr0[0:w, i % 2, :], scalar=rstd[0:w, 0, i:i + 1],
                                     in1=gb0[0:w, :], op0=ALU.mult, op1=ALU.mult).then_inc(sem("h_rows"), 1)

        def low(i, hi_sem, lo_sem, b0):
            r, w = rows_of(i)
            for kk in range(2):
                q = 2 * i + kk
                dve.wait_ge(sem(hi_sem), q + 1)
                dve.tensor_tensor(act_lo[:, 4 * kk:4 * kk + 4, r:r + w],
                                  bank[b0 + q % 4].rearrange("p (k r) -> p k r", k=4)[:, :, 0:w],
                                  act_hi[:, 4 * kk:4 * kk + 4, r:r + w].bitcast(F32), ALU.subtract).then_inc(sem(lo_sem), 1)

        norm_rows(0)
        for i in range(RT):
            if i + 1 < RT:
                norm_rows(i + 1)
            low(i, "n_hi", "n_lo", 0)

        dve.wait_ge(sem("const_in"), NCONST)
        then(dve.tensor_tensor(lbt[:, 4, :], lbl[:, 0, :], lbl[:, 1, :], ALU.max))
        dve.tensor_tensor(lbt[:, 0, :], lbl[:, 0, :], lbt[:, 4, :], ALU.subtract)
        dve.tensor_tensor(lbt[:, 1, :], lbl[:, 1, :], lbt[:, 4, :], ALU.subtract).then_inc(sem("lb_in"), 1)
        then(dve.tensor_scalar(nsink[:], sink[:], -1.0, None, ALU.mult))
        dve.wait_ge(sem("lb_exp"), 1)
        then(dve.tensor_tensor(lbt[:, 5, :], lbt[:, 2, :], lbt[:, 3, :], ALU.add))
        then(dve.reciprocal(lbt[:, 6, :], lbt[:, 5, :]))
        then(dve.tensor_tensor(lbt[:, 4, :], lbt[:, 2, :], lbt[:, 6, :], ALU.mult))
        then(dve.tensor_scalar(lbt[:, 5, :], lbt[:, 4, :], -0.5, 0.5, ALU.mult, ALU.add))
        then(dve.tensor_tensor(lbt[:, 6, :], lbt[:, 4, :], lbt[:, 5, :], ALU.add))
        f_scale, f_shift = lbt[:, 5, :], lbt[:, 6, :]

        def rope(r):
            v = ROPE_UNITS[r]
            kind, m = TILES[v // CH]
            c = v % CH
            dve.wait_ge(sem("rot_mm"), r + 1)
            x = kraw[:, cols(c)] if kind == "k" else mix[:, m, cols(c)]
            tmp = sm_rope[:, 0:CW]
            then(dve.tensor_tensor(x, x, cos[:, cols(c)], ALU.mult))
            ins = dve.tensor_tensor(tmp, BR[:, 0:CW], sin[:, cols(c)], ALU.mult)
            ins.then_inc(sem("rot_read"), 1)
            dve.wait_ge(sem("rot_read"), r + 1)
            if kind == "q":
                dve.tensor_tensor(x, x, tmp, ALU.add).then_inc(sem("rope"), 1)
            else:
                if c == 0:
                    dve.wait_ge(sem("kt2_zero"), 1)
                dve.tensor_tensor(kt2[0:HD, 0, cols(c)], kraw[0:HD, cols(c)], tmp[0:HD, :], ALU.add)
                dve.tensor_tensor(kt2[HD:P, 1, cols(c)], kraw[HD:P, cols(c)], tmp[HD:P, :], ALU.add).then_inc(sem("rope"), 1)

        sm_rope = hk

        def unit_read(u):
            kind, m = TILES[u // CH]
            c = u % CH
            src = J[u % 2][:, 0:CW]
            if kind == "ri":
                if c == CH - 1:
                    dve.wait_ge(sem("unit_act"), u + 1)
                    dve.tensor_copy(i_s[:, m, :], r_i[:, SEQ:ROWS]).then_inc(sem("s_saved"), 1)
            if kind not in SILU:
                return
            s = units_before(SILU, u)
            dve.wait_ge(sem("unit_act"), u + 1)
            if kind == "rf":
                if m and c == 0:
                    dve.wait_ge(sem("g_prod"), LEVELS * (m - 1) + 1)
                dve.tensor_scalar(r_f[:, cols(c)], th[:, s % 2, :], f_scale[:, m:m + 1], f_shift[:, m:m + 1],
                                  ALU.mult, ALU.add).then_inc(sem("th_read"), 1)
                dve.wait_ge(sem("th_read"), s + 1)
                if c == CH - 1:
                    dve.tensor_copy(f_s[:, m, :], r_f[:, SEQ:ROWS]).then_inc(sem("f_done"), 1)
                    dve.tensor_scalar(k_s[:, m, :], r_f[:, SEQ:ROWS], -1.0, 1.0, ALU.mult, ALU.add).then_inc(sem("ks_saved"), 1)
            elif kind == "rq":
                if m and c == 0:
                    dve.wait_ge(sem("diag_mm"), m)
                dve.scalar_tensor_tensor(out=r_q[:, cols(c)], in0=th[:, s % 2, :], scalar=1.0, in1=src,
                                         op0=ALU.add, op1=ALU.mult).then_inc(sem("th_read"), 1)
                if c == CH - 1:
                    dve.wait_ge(sem("th_read"), s + 1)
                    then(dve.tensor_copy(q_s[:, m, :], r_q[:, SEQ:ROWS]))
            else:
                w = CW if c < CH - 1 else CW - DECB
                dve.scalar_tensor_tensor(out=th[:, s % 2, :], in0=th[:, s % 2, :], scalar=1.0, in1=src,
                                         op0=ALU.add, op1=ALU.mult).then_inc(sem("g_gate"), 1)
                dve.wait_ge(sem("g_gate"), units_before(("rg",), u) + 1)
                dve.wait_ge(sem("o_cols"), 2 * (m + 1))
                dst = mix[:, 4 + m, CW * c:CW * c + w]
                if c == CH - 1:
                    then(dve.tensor_copy(g_s[:, m, :], th[:, s % 2, w:CW]))
                dve.tensor_tensor(dst, dst, th[:, s % 2, 0:w], ALU.mult).then_inc(sem("th_read"), 1)

        def decay(h, n):
            hs = 1 << n
            g = r_f[:, 0:SEQ] if n == 0 else g_level(n)
            gv = g.rearrange("p (b e) -> p b e", e=2)
            qv = hq[:].rearrange("p (b e s) -> p b e s", e=2, s=hs)
            kv = hk[:].rearrange("p (b e s) -> p b e s", e=2, s=hs)
            nb = SEQ // (2 * hs)
            if n:
                dve.wait_ge(sem("g_prod"), LEVELS * h + n)
            dve.tensor_tensor(qv[:, :, 1, :], qv[:, :, 1, :], bc(gv[:, :, 0].unsqueeze(2), [P, nb, hs]), ALU.mult)
            dve.tensor_tensor(kv[:, :, 0, :], kv[:, :, 0, :], bc(gv[:, :, 1].unsqueeze(2), [P, nb, hs]), ALU.mult)\
                .then_inc(sem("hq_step"), 1)

        for tick in range(TICKS):
            for step in rot_steps(tick):
                if step[0] == "rot":
                    rope(step[1])
            for step, i in attention_steps(tick):
                t, j, e = i // NBLK, i % NBLK, i % 2
                k0 = WIN if j == 0 else 0
                if step == "S":
                    dve.wait_ge(sem("at_s"), i + 1)
                    if i:
                        dve.wait_ge(sem("at_exp"), i)
                    for g in range(NKV):
                        ins = dve.tensor_tensor_reduce(sm[:, g, k0:], BS[:, 2 * WIN * g + k0:2 * WIN * (g + 1)], amask[:, k0:],
                                                       1.0, -3.0e38, ALU.add, ALU.max, mx[:, e, g:g + 1])
                    then(ins)
                    then(dve.scalar_tensor_tensor(out=negm[:, e, :], in0=mx[:, e, :], scalar=-SCALE, in1=nsink[:, t:t + GRP + 1:GRP],
                                                  op0=ALU.mult, op1=ALU.min))
                    dve.tensor_tensor(tsum[:, e, :], sink[:, t:t + GRP + 1:GRP], negm[:, e, :], ALU.add).then_inc(sem("at_max"), 1)
                elif step == "PT":
                    dve.wait_ge(sem("at_exp"), i + 1)
                    then(dve.tensor_tensor(den[:, e, :], den[:, e, :], esk[:, e, :], ALU.add))
                    then(dve.reciprocal(rden[:, e, :], den[:, e, :]))
                elif step == "PV":
                    dve.wait_ge(sem("at_pv"), i + 1)
                    if i:
                        dve.wait_ge(sem("at_ot"), i)
                    dve.tensor_tensor(orow[:], BO[:, 0:P].rearrange("p (g d) -> p g d", g=2),
                                      bc(rden[:, e, :].unsqueeze(2), [P, 2, HD]), ALU.mult).then_inc(sem("at_or"), 1)
            for step in recurrence_steps(tick):
                h = step[1]
                if step[0] == "prep":
                    dve.wait_ge(sem("f_done"), h + 1)
                    if h:
                        dve.wait_ge(sem("o_turned"), 2 * h)
                    dve.tensor_tensor(hq[:], r_q[:, 0:SEQ], r_f[:, 0:SEQ], ALU.mult)
                    dve.tensor_scalar(hk[:], r_f[:, 0:SEQ], -1.0, 1.0, ALU.mult, ALU.add).then_inc(sem("hq_prep"), 1)
                if step[0] == "diag":
                    dve.wait_ge(sem("diag_mm"), h + 1)
                    if h == 0:
                        dve.wait_ge(sem("stored"), 32)
                    else:
                        dve.wait_ge(sem("o_ss"), h)
                    for a in range(2):
                        ins = dve.tensor_tensor(ast[:, 4 * a:4 * a + 4, :], BL[a].rearrange("p (b t) -> p b t", b=4),
                                                bc(ident[:].unsqueeze(1), [P, 4, P]), ALU.mult)
                    ins.then_inc(sem("diag_read"), 1)
                    dve.wait_ge(sem("diag_read"), h + 1)
                if step[0] == "level":
                    n = step[2]
                    dve.wait_ge(sem("level_mm"), LEVELS * h + n + 1)
                    if n == 0 and h == 0:
                        dve.wait_ge(sem("lmask_done"), 1)
                    decay(h, n)
                    for a in range(2):
                        ins = dve.copy_predicated(ast[:, 4 * a:4 * a + 4, :], bc(lmask[:, n, :].unsqueeze(1), [P, 4, P]),
                                                  BL[a].rearrange("p (b t) -> p b t", b=4))
                    ins.then_inc(sem("level_read"), 1)
                    dve.wait_ge(sem("level_read"), LEVELS * h + n + 1)
                if step[0] == "u":
                    dve.wait_ge(sem("u_mm"), h + 1)
                    dve.wait_ge(sem("g_prod"), LEVELS * (h + 1))
                    if h:
                        dve.wait_ge(sem("stp_out"), 16 * h)
                    gl = g_level(LEVELS)
                    for c in range(NBLK):
                        u_c = BL[c // 4][:, P * (c % 4):P * (c % 4) + P]
                        if c == 0:
                            ins = dve.tensor_copy(states[:, 1, :], u_c)
                        else:
                            ins = dve.scalar_tensor_tensor(out=states[:, c + 1, :], in0=states[:, c, :], scalar=gl[:, c:c + 1],
                                                           in1=u_c, op0=ALU.mult, op1=ALU.add)
                        ins.then_inc(sem("chain"), 1)
                        dve.wait_ge(sem("chain"), NBLK * h + c + 1)
                if step[0] == "o":
                    dve.wait_ge(sem("o_std"), h + 1)
                    then(dve.reciprocal(orstd[:], ostd[:]))
                    then(dve.tensor_scalar(orstd[:], orstd[:], 0.25, None, ALU.mult))
                    for a in range(2):
                        ins = dve.tensor_tensor(orn[:, 4 * P * a:4 * P * a + 4 * P].rearrange("p (b t) -> p b t", b=4),
                                                BL[a].rearrange("p (b t) -> p b t", b=4),
                                                bc(orstd[:, 4 * a:4 * a + 4].unsqueeze(2), [P, 4, P]), ALU.mult)
                    ins.then_inc(sem("o_norm"), 1)
                if step[0] in ("ota", "otb"):
                    a = step[0] == "otb"
                    dve.wait_ge(sem("o_turned"), 2 * h + a + 1)
                    dve.tensor_scalar(mix[:, 4 + h, 4 * P * a:4 * P * a + 4 * P], BR, rnorm[:, h:h + 1], None, ALU.mult)\
                        .then_inc(sem("o_cols"), 1)
            for step in sample_steps(tick):
                n = DECB * NQ
                if step[0] == "ks_t":
                    dve.wait_ge(sem("qp_zero"), 1)
                    dve.wait_ge(sem("at_out"), NITEM)
                    for g in range(NKV):
                        ins = dve.tensor_copy(qp[HD * g:HD * g + HD, :, GRP * g:GRP * g + GRP].rearrange("p b t -> p t b"),
                                              mix[HD * g:HD * g + HD, 0:GRP, SEQ:ROWS])
                    ins.then_inc(sem("qp_done"), 1)
                if step[0] == "s_turn":
                    dve.wait_ge(sem("s_turn"), 1)
                    then(dve.tensor_reduce(sst[0:n, 0:1], BP[0:n, 0:P], AX.X, ALU.max))
                    then(dve.tensor_scalar(sst[0:n, 0:1], sst[0:n, 0:1], SCALE, sinkc[:, 0:1], ALU.mult, ALU.max))
                    then(dve.tensor_scalar(sst[0:n, 1:2], sst[0:n, 0:1], -1.0, None, ALU.mult))
                    dve.tensor_tensor(sst[0:n, 2:3], sinkc[:, 0:1], sst[0:n, 1:2], ALU.add).then_inc(sem("s_max"), 1)
                    dve.wait_ge(sem("s_exp"), 1)
                    then(dve.tensor_tensor(sst[0:n, 3:4], sst[0:n, 3:4], sst[0:n, 4:5], ALU.add))
                    then(dve.reciprocal(sst[0:n, 4:5], sst[0:n, 3:4]))
                    dve.tensor_scalar(px[:], px[:], sst[0:n, 4:5], None, ALU.mult).then_inc(sem("s_prob"), 1)
                if step[0] == "s_out":
                    dve.wait_ge(sem("s_out"), 1)
                    for g in range(NKV):
                        ov = BO[HD * g:HD * g + HD, 0:n].rearrange("p (b t) -> p t b", t=NQ)
                        ins = dve.tensor_copy(mix[HD * g:HD * g + HD, 0:GRP, SEQ:ROWS], ov[:, GRP * g:GRP * g + GRP, :])
                    ins.then_inc(sem("s_mixed"), 1)
                if step[0] == "r_turn":
                    h = step[1]
                    dve.wait_ge(sem("st_in"), 16 * (h + 1))
                    dve.tensor_tensor(st[:], st[:], bc(f_s[:, h, :].unsqueeze(2), [P, DECB, P]), ALU.mult)
                    dve.wait_ge(sem("s_ki"), h + 1)
                    if h == 0:
                        dve.wait_ge(sem("stored"), 64)
                    dve.tensor_tensor(ib[:], bc(ki[:, 1, :].unsqueeze(1), [DECB, DECB, P]),
                                      bc(ident[0:DECB, 0:DECB].unsqueeze(2), [DECB, DECB, P]), ALU.mult).then_inc(sem("s_ib"), 1)
                if step[0] == "r_outer":
                    h = step[1]
                    dve.wait_ge(sem("s_outer"), h + 1)
                    for a, b in ((0, BS), (1, BO)):
                        dve.tensor_tensor(st[:, 4 * a:4 * a + 4, :], st[:, 4 * a:4 * a + 4, :], b.rearrange("p (b d) -> p b d", b=4),
                                          ALU.add).then_inc(sem("s_state"), 1)
                if step[0] == "r_o":
                    h = step[1]
                    dve.wait_ge(sem("s_o"), h + 1)
                    dve.tensor_copy(o_s[:, h, :], BP[:, 0:DECB]).then_inc(sem("s_os"), 1)
                if step[0] == "r_rows":
                    n = NREC * DECB
                    dve.wait_ge(sem("so_std"), 1)
                    then(dve.reciprocal(sst[0:n, 7:8], sst[0:n, 6:7]))
                    dve.tensor_scalar(px[0:n, :], BP[0:n, 0:P], sst[0:n, 7:8], 0.25, ALU.mult, ALU.mult).then_inc(sem("so_norm"), 1)
                if step[0] == "r_cols":
                    n = NREC * DECB
                    dve.wait_ge(sem("so_cols"), 1)
                    then(dve.tensor_tensor(o_s[:], BP[:, 0:n].rearrange("p (h b) -> p h b", h=NREC),
                                           bc(rnorm[:].unsqueeze(2), [P, NREC, DECB]), ALU.mult))
            if tick % 2:
                unit_read(tick // 2)
        dve.tensor_tensor(mix[:, 4:8, SEQ:ROWS], o_s[:], g_s[:], ALU.mult).then_inc(sem("mix_done"), 1)
        dve.wait_ge(sem("mix_done"), 1)
        dve.wait_ge(sem("at_out"), NITEM)
        for k in range(KT):
            dve.wait_ge(sem("mix_hi"), k + 1)
            dve.tensor_tensor(act_lo[:, k, :], mix[:, k, :], act_hi[:, k, :].bitcast(F32), ALU.subtract).then_inc(sem("mix_lo"), 1)

        def post_rows(i):
            r, w = rows_of(i)
            dve.wait_ge(sem("p_std"), i + 1)
            then(dve.reciprocal(rstd[0:w, 0, i:i + 1], std[0:w, 0, i:i + 1]))
            if i == 0:
                dve.wait_ge(sem("g_in"), 48)
            dve.scalar_tensor_tensor(out=tr[0:w, i % 2, :].rearrange("p (a b) -> p a b", a=2), in0=pair[i % 2][0:w, :, :],
                                     scalar=rstd[0:w, 0, i:i + 1], in1=gbl[0:w, :].rearrange("p (a b) -> p a b", a=2),
                                     op0=ALU.mult, op1=ALU.mult).then_inc(sem("p_t"), 1)

        def pre_rows(i):
            r, w = rows_of(i)
            dve.wait_ge(sem("q_std"), i + 1)
            then(dve.reciprocal(rstd[0:w, 1, i:i + 1], std[0:w, 1, i:i + 1]))
            dve.scalar_tensor_tensor(out=tr[0:w, i % 2, :], in0=x2r[0:w, i % 2, :], scalar=rstd[0:w, 1, i:i + 1],
                                     in1=gb2[0:w, :], op0=ALU.mult, op1=ALU.mult).then_inc(sem("h2_rows"), 1)

        post_rows(0)
        for i in range(RT):
            if i + 1 < RT:
                post_rows(i + 1)
            pre_rows(i)
            if i >= 1:
                low(i - 1, "h2_hi", "h2_lo", 4)
        low(RT - 1, "h2_hi", "h2_lo", 4)

        def last_rows(i):
            r, w = rows_of(i)
            dve.wait_ge(sem("y_std"), i + 1)
            then(dve.reciprocal(rstd[0:w, 1, i:i + 1], std[0:w, 1, i:i + 1]))
            if i == 0:
                dve.wait_ge(sem("g_in"), 64)
            dve.scalar_tensor_tensor(out=tr[0:w, i % 2, :].rearrange("p (a b) -> p a b", a=2), in0=pair[i % 2][0:w, :, :],
                                     scalar=rstd[0:w, 1, i:i + 1], in1=gbl[0:w, :].rearrange("p (a b) -> p a b", a=2),
                                     op0=ALU.mult, op1=ALU.mult).then_inc(sem("y_t"), 1)

        def ffn(g, first, last=False):
            for j in range(2):
                for c in range(CH):
                    q = 6 * g + 3 * j + c
                    e = (3 * j + c) % 2
                    dve.wait_ge(sem("up_mm"), q + 1)
                    dve.wait_ge(sem("gate_done"), q + 1)
                    if not (first and 3 * j + c < 2):
                        dve.wait_ge(sem("h_lo_done"), q - 1)
                    dve.tensor_tensor(hf[:, e, :], bank[2 + e][:, 0:CW], sg[:, e, :], ALU.mult).then_inc(sem("hf_done"), 1)
            for c in range(CH):
                for m in range(KT):
                    v = KT * c + m
                    dve.wait_ge(sem("down_mm"), 24 * g + (v + 1))
                    src = bank[4 + v % 4][:, 0:CW]
                    if first:
                        dve.tensor_copy(mix[:, m, cols(c)], src).then_inc(sem("acc_done"), 1)
                    else:
                        if v == 0:
                            dve.wait_ge(sem("acc_done"), 24 * g)
                        dve.tensor_tensor(mix[:, m, cols(c)], mix[:, m, cols(c)], src, ALU.add).then_inc(sem("acc_done"), 1)
                    if last and c > 0 and m == 4:
                        for i in ((0, 1) if c == 1 else (2, 3)):
                            last_rows(i)

        ffn(0, True)
        with dve.Fori(1, GROUPS - 1) as g:
            ffn(g, False)
        ffn(GROUPS - 1, False, True)
        for i in range(4, RT):
            last_rows(i)

    block.__exit__(None, None, None)


_OUTS = [("y_prompt", (1, SEQ, DM)), ("y_sample", (DECB, 1, DM)), ("k_p", (1, 1, WIN, NKV, HD)), ("v_p", (1, 1, WIN, NKV, HD)),
         ("st_p", (1, 1, NREC, RD, RD)), ("k_s", (1, DECB, WIN, NKV, HD)), ("v_s", (1, DECB, WIN, NKV, HD)),
         ("st_s", (1, DECB, NREC, RD, RD))]


def kernel(**inputs):
    import concourse.bacc as bacc
    from concourse.bass_utils import run_bass_kernel_spmd

    nc = bacc.Bacc("TRN2", target_bir_lowering=False, num_devices=1)
    arrays = {name: np.ascontiguousarray(a) for name, a in inputs.items()}
    arrays.update(shape_constants())
    t_in = {name: nc.dram_tensor(f"{name}_dram", a.shape, mybir.dt.from_np(a.dtype), kind="ExternalInput").ap()
            for name, a in arrays.items()}
    t_out = {name: nc.dram_tensor(f"{name}_out", shape, F32, kind="ExternalOutput").ap() for name, shape in _OUTS}
    build(nc, t_in, t_out)
    r = run_bass_kernel_spmd(nc, [{f"{name}_dram": a for name, a in arrays.items()}], core_ids=[0])
    return tuple(r.results[0][f"{name}_out"] for name, _ in _OUTS)
```

```python
import math

import numpy as np

import concourse.bass as bass
from concourse import mybir

F32 = mybir.dt.float32
F32R = mybir.dt.float32r
U8 = mybir.dt.uint8
ALU = mybir.AluOpType
ACT = mybir.ActivationFunctionType
AX = mybir.AxisListType

P = 128
DM = 1024
SEQ, DECB = 1024, 8
ROWS = SEQ + DECB
KT = DM // P
HD, NQ, NKV = 64, 8, 2
GRP = NQ // NKV
WIN = 128
NREC, RD = 4, 128
DFF = 2816
FT = DFF // P
CH = 3
CW = ROWS // CH
NBLK = SEQ // P
RT = NBLK + 1
LEVELS = 7
PAST = 2048
ROT = HD // 4
THETA = 500000.0
EPS = 1e-6
SCALE = HD ** -0.5
NEG = -1.0e30

CQ, CK, CV = 0, NQ * HD, NQ * HD + NKV * HD
CRQ = CV + NKV * HD
CRF, CRI, CRG = CRQ + NREC * RD, CRQ + 2 * NREC * RD, CRQ + 3 * NREC * RD

TILES = [("k", 0), ("v", 0)] + [("q", t) for t in range(4)]
for _h in range(NREC):
    TILES += [("rq", _h), ("ri", _h), ("rf", _h)]
TILES += [("rg", h) for h in range(NREC)]
NIN = len(TILES)
NOUT = DM // P
N12 = NIN + NOUT
LEAD = 4
ORDER = [(n, c) for c in range(CH) for n in range(LEAD)] + [(n, c) for n in range(LEAD, NIN) for c in range(CH)]
UNITS = NIN * CH
LAST_UNIT = [max(u for u, (m, _) in enumerate(ORDER) if m == n) for n in range(NIN)]
NORM_ROWS = {0: (0, 1, 2), 1: (3,), 2: (4,), 3: (5,), 4: (6,), 5: (7,), 6: (8,)}
TICKS = 2 * UNITS
AT0 = 16
NITEM = 4 * NBLK
HG0, HGS = 55, 18
SA0 = 88
SR0, SRS = 98, 6
SLOTS = 24 + 12
ROW_OUT = (9, 11, 17, 19, 21, 24, 25, 27, 29)
ROW_IN = (12, 14, 20, 22, 24, 27, 28, 30, 32)
DOWN_SLOTS = (33, 34)
LAST_ROWS = [(1, 1), (1, 3), (2, 1), (2, 3), (2, 5)]
Y_VECTOR = (6, 8)
GROUPS = FT // 2


def rows_of(i):
    return (P * i, P if i < NBLK else DECB)


def shape_constants():
    ident = np.eye(P, dtype=np.float32)
    perm = np.zeros((P, P), np.float32)
    half = ROT // 2
    for b in range(0, P, HD):
        for d in range(half):
            perm[b + d + half, b + d] = -1.0
            perm[b + d, b + d + half] = 1.0
    q = WIN + np.arange(WIN)[:, None]
    k = np.arange(2 * WIN)[None, :]
    band = (k <= q) & (q - k < WIN)
    amask = np.where(band, 0.0, NEG).astype(np.float32)
    s, t = np.arange(P)[:, None], np.arange(P)[None, :]
    lmask = np.stack([(s // (2 * h) == t // (2 * h)) & (s // h % 2 == 0) & (t // h % 2 == 1)
                      for h in (2 ** n for n in range(LEVELS))], axis=1).astype(np.float32)
    pos = np.concatenate([np.arange(SEQ), np.full(DECB, PAST)]).astype(np.float32)
    inv = np.exp(-np.log(np.float32(THETA)) * np.arange(half, dtype=np.float32) * np.float32(2.0 / ROT))
    ang = (pos[None, :] * inv.astype(np.float32)[:, None]).astype(np.float32)
    cos, sin = np.ones((P, ROWS), np.float32), np.zeros((P, ROWS), np.float32)
    for b in range(0, P, HD):
        for d in range(ROT):
            cos[b + d], sin[b + d] = np.cos(ang[d % half]), np.sin(ang[d % half])
    return {"c_ident": ident, "c_perm": perm, "c_amask": amask, "c_lmask": lmask, "c_cos": cos, "c_sin": sin}


def build(nc, t_in, t_out):
    base = (nc.sbuf_base + 31) // 32 * 32
    end = nc.sbuf_top // 32 * 32

    def at(name, shape, dt, offset):
        size = math.prod(shape[1:]) * (1 if dt == U8 else 4)
        assert offset + size <= end, (name, offset + size - end)
        return nc.alloc_sbuf_tensor_at(name, shape, dt, offset=offset), (offset + size + 31) // 32 * 32

    o = base
    act_hi, o = at("act_hi", [P, KT, ROWS], F32R, o)
    act_lo, o = at("act_lo", [P, KT, ROWS], F32R, o)
    at_mix = o
    mix, o = at("mix", [P, KT, ROWS], F32, o)
    w_hi, o = at("w_hi", [P, 4, KT, P], F32R, o)
    w_lo, o = at("w_lo", [P, 4, KT, P], F32R, o)
    raw, o = at("raw", [P, 2, KT, P], F32, o)
    ident, o = at("ident", [P, P], F32, o)
    small_from = o

    def small(name, shape):
        nonlocal o
        x, o = at(name, shape, F32, o)
        return x

    eps = small("eps", [P, 1])
    ss = small("ss", [P, 2, RT])
    std = small("std", [P, 2, RT])
    rstd = small("rstd", [P, 2, RT])
    lbl = small("lbl", [P, 2, NREC])
    lbt = small("lbt", [P, 8, NREC])
    rnorm = small("rnorm", [P, NREC])
    sink = small("sink", [P, NQ])
    nsink = small("nsink", [P, NQ])
    mx = small("mx", [P, 2, 2])
    negm = small("negm", [P, 2, 2])
    tsum = small("tsum", [P, 2, 2])
    esk = small("esk", [P, 2, 2])
    den = small("den", [P, 2, 2])
    rden = small("rden", [P, 2, 2])
    oss = small("oss", [P, NBLK])
    ostd = small("ostd", [P, NBLK])
    orstd = small("orstd", [P, NBLK])
    q_s = small("q_s", [P, NREC, DECB])
    f_s = small("f_s", [P, NREC, DECB])
    i_s = small("i_s", [P, NREC, DECB])
    k_s = small("k_s", [P, NREC, DECB])
    g_s = small("g_s", [P, NREC, DECB])
    o_s = small("o_s", [P, NREC, DECB])
    kn_s = small("kn_s", [DECB, P])
    qp = small("qp", [P, DECB, NQ])
    stx = small("stx", [P, DECB * NQ])
    ptx = small("ptx", [P, DECB * NQ])
    sinkc = small("sinkc", [DECB * NQ, 1])
    sst = small("sst", [P, 8])
    assert o - small_from <= 4096, o - small_from
    region = small_from + 4096

    o = region
    kt2, o = at("kt2", [P, NKV, ROWS], F32, o)
    vrow, o = at("vrow", [P, RT, P], F32, o)
    at_in = o
    r_i, o = at("r_i", [P, ROWS], F32, o)
    r_q, o = at("r_q", [P, ROWS], F32, o)
    r_f, o = at("r_f", [P, ROWS], F32, o)
    th, o = at("th", [P, 2, CW], F32, o)
    at_att = o
    sm, o = at("sm", [P, 2, 2 * WIN], F32, o)
    at_prob = o
    prob, o = at("prob", [P, 2, 2, 2 * WIN], F32, o)
    pt, o = at("pt", [P, 4, P], F32, o)
    orow, o = at("orow", [P, 2, HD], F32, o)
    amask, o = at("amask", [P, 2 * WIN], F32, o)
    lmask, o = at("lmask", [P, LEVELS, P], U8, o)
    at_hq = o
    hq, o = at("hq", [P, SEQ], F32, o)
    hk, o = at("hk", [P, SEQ], F32, o)
    hg, o = at("hg", [P, 1016], F32, o)
    ast, o = at("ast", [P, NBLK, P], F32, o)
    irow, o = at("irow", [P, NBLK, P], F32, o)
    at_krow = o
    krow, o = at("krow", [P, NBLK, P], F32, o)
    states, o = at("states", [P, NBLK + 1, P], F32, o)
    cos, oo = at("cos", [P, ROWS], F32, at_krow)
    sin, oo = at("sin", [P, ROWS], F32, oo)
    perm, _ = at("perm", [P, P], F32, at_krow - 2 * 4096 - 4064)
    kwin, _ = at("kwin", [P, P], F32, at_krow - 2 * 4096)
    lmask32, _ = at("lmask32", [P, LEVELS, P], F32, at_krow - 4096)
    kraw = r_f
    vt = r_i
    xr0, oo = at("xr0", [P, 2, DM], F32, at_mix + 4 * 4 * ROWS)
    hr0, oo = at("hr0", [P, 2, DM], F32, oo)
    assert oo <= at_mix + KT * 4 * ROWS
    xr0b, _ = at("xr0b", [P, DM], F32, at_prob)
    hr0b, _ = at("hr0b", [P, DM], F32, at_krow - 2 * 4096)

    def xr_first(i):
        w = rows_of(i)[1]
        return xr0b[0:w, :] if i % 3 == 2 else xr0[0:w, i % 3, :]

    def hr_first(i):
        w = rows_of(i)[1]
        return hr0b[0:w, :] if i % 3 == 2 else hr0[0:w, i % 3, :]

    gb0, _ = at("gb0", [P, DM], F32, at_hq)
    ks, oo = at("ks", [P, DECB, P], F32, at_att)
    vs, oo = at("vs", [P, DECB, P], F32, oo)
    px, oo = at("px", [DECB * NQ, P], F32, oo)
    ki, oo = at("ki", [DECB, 2, P], F32, oo)
    kst, oo = at("kst", [P, DECB, P], F32, region)
    st, oo = at("st", [P, DECB, P], F32, oo)
    ib, _ = at("ib", [DECB, DECB, P], F32, region + 8256)
    orn = hk
    o = region
    h_hi, o = at("h_hi", [P, 2, ROWS], F32R, o)
    h_lo, o = at("h_lo", [P, 2, ROWS], F32R, o)
    sg, o = at("sg", [P, 2, CW], F32, o)
    hf, o = at("hf", [P, 2, CW], F32, o)
    free = o
    o = end - 6 * 4096
    d_hi, o = at("d_hi", [P, 2, DM], F32R, o)
    d_lo, o = at("d_lo", [P, 2, DM], F32R, o)
    draw, o = at("draw", [P, 2, DM], F32, o)
    o = free
    xr, o = at("xr", [P, 2, DM], F32, o)
    tr, o = at("tr", [P, 2, DM], F32, o)
    gbl, o = at("gbl", [P, DM], F32, o)
    assert o <= end - 6 * 4096
    gb2, o = at("gb2", [P, DM], F32, end - 6 * 4096)
    x2r, o = at("x2r", [P, 2, DM], F32, o)
    assert o <= end - 2 * 4096

    x2b, _ = at("x2b", [P, RT, DM], F32, base)
    ty, oo = at("ty", [P, 4, DM], F32, free)
    assert oo <= end - 6 * 4096

    wx_hi = [at(f"wx_hi{i}", [P, KT, P], F32R, region + 4096 * i)[0] for i in range(4)]
    wx_lo = [at(f"wx_lo{i}", [P, KT, P], F32R, region + 4 * 4096 if i == 0 else end - 4096 * (4 - i))[0] for i in range(4)]

    def w_tiles(n):
        if NIN + 2 <= n < NIN + 6:
            return wx_hi[n - NIN - 2][:], wx_lo[n - NIN - 2][:]
        return w_hi[:, n % 4], w_lo[:, n % 4]

    x2d = nc.dram_tensor("x2_scratch", (ROWS, DM), F32).ap()

    pair = [nc.alloc_psum_tensor(f"pair{i}", [P, 2, 512], F32) for i in range(4)]
    bank = [pair[i // 2][:, i % 2, :] for i in range(8)]
    J = [bank[0], bank[1]]
    BS, BP, BO, BR = bank[2], bank[3], bank[4], bank[5]
    BL = [bank[6], bank[7]]
    NB = [bank[2], bank[3], bank[6], bank[7]]

    sems = {}

    def sem(name):
        if name not in sems:
            sems[name] = nc.alloc_semaphore(name)
        return sems[name]

    xp = t_in["x_prompt"].rearrange("b s d -> (b s) d")
    xs = t_in["x_sample"].rearrange("b s d -> (b s) d")
    w_in = t_in["w_in"][0]
    w_out = t_in["w_out"][0]
    yp = t_out["y_prompt"].rearrange("b s d -> (b s) d")
    ys = t_out["y_sample"].rearrange("b s d -> (b s) d")

    def x_rows(i):
        return xp[P * i:P * i + P, :] if i < NBLK else xs

    def y_rows(i):
        return yp[P * i:P * i + P, :] if i < NBLK else ys

    def gain(name):
        return t_in[name].partition_broadcast(P).rearrange("p o d -> p (o d)")

    def cols(c):
        return slice(CW * c, CW * c + CW)

    def bc(ap, shape):
        return ap.broadcast_to(shape)

    def g_level(n):
        off = sum(SEQ >> m for m in range(1, n))
        return hg[:, off:off + (SEQ >> n)]

    def weight_parts(n):
        dst = raw[:, n % 2]
        if n < NIN:
            kind, m = TILES[n]
            if kind == "q":
                return [(dst[:, :, HD * g:HD * g + HD],
                         w_in[:, CQ + HD * (m + GRP * g):CQ + HD * (m + GRP * g) + HD].rearrange("(k p) n -> p k n", p=P))
                        for g in range(NKV)]
            c = {"k": CK, "v": CV, "rq": CRQ, "rf": CRF, "ri": CRI, "rg": CRG}[kind] + P * m
            return [(dst, w_in[:, c:c + P].rearrange("(k p) n -> p k n", p=P))]
        c = P * (n - NIN)
        part = [(dst[HD * g:HD * g + HD, 0:4, :],
                 w_out[HD * GRP * g:HD * GRP * (g + 1), c:c + P].rearrange("(t p) n -> p t n", p=HD)) for g in range(NKV)]
        return part + [(dst[:, 4:8, :], w_out[4 * P:8 * P, c:c + P].rearrange("(k p) n -> p k n", p=P))]

    raw_count = []
    slot_total = [0, 0]
    for n in range(N12):
        slot_total[n % 2] += 16 * len(weight_parts(n))
        raw_count.append(slot_total[n % 2])
    for n in range(N12, N12 + 4):
        raw_count.append(slot_total[n % 2] + 16 * ((n - N12) // 2 + 1))

    def unit_of(u):
        n, c = ORDER[u]
        return TILES[n] + (c,)

    def units_before(kinds, u):
        return sum(unit_of(v)[0] in kinds for v in range(min(u, UNITS)))

    def unit_index(kind, m, c):
        return ORDER.index((TILES.index((kind, m)), c))

    def split_at(tick):
        out = [n for n, t in ((4, 19), (5, 21), (NIN, 118), (NIN + 1, 121), (NIN + 2, 124), (NIN + 3, 126), (NIN + 4, 128),
                              (NIN + 5, 130)) if t == tick]
        if tick % 6 == 1 and 6 <= tick // 6 + 2 < NIN:
            out.append(tick // 6 + 2)
        return sorted(out)

    def row_steps(slot):
        return ([("in", i) for i in range(RT) if ROW_IN[i] == slot] + [("mid", i) for i in range(RT) if ROW_OUT[i] + 1 == slot]
                + [("out", i) for i in range(RT) if ROW_OUT[i] == slot])

    def first_tiles(slot):
        return [N12 + k for k, v in enumerate((19, 20, 23, 24)) if v == slot]

    def chunk_of_rows(c):
        return -(-CW * (c + 1) // P)

    SILU = ("rq", "rg", "rf")
    ROPE = ("k", "q")
    WIN_LOADS = 2 * (1 + DECB) * 16
    NCONST = 8 * 16 + DECB * 16 + 16

    def attention_steps(tick):
        d = tick - AT0
        out = []
        if d % 2 == 0:
            for step, i in (("PT", d // 2 - 1), ("OT", d // 2 - 2), ("S", d // 2)):
                if 0 <= i < NITEM:
                    out.append((step, i))
        elif 0 <= (d - 3) // 2 < NITEM:
            out.append(("PV", (d - 3) // 2))
        return out

    def recurrence_steps(tick):
        out = []
        for h in range(NREC):
            d = tick - (HG0 + HGS * h)
            if d in (-4, -1):
                out.append(("it" + "ab"[d == -1], h))
            if d == -1:
                out.append(("prep", h))
            if d == 0:
                out.append(("diag", h))
            if 1 <= d <= LEVELS:
                out.append(("level", h, d - 1))
            out += [(s, h) for s, v in (("kta", 9), ("ktb", 10), ("u", 11), ("o", 13), ("ota", 15), ("otb", 16)) if d == v]
        return out

    def br_uses():
        out = []
        for tick in range(TICKS):
            out += rot_steps(tick)
            out += [("br", s) for s in recurrence_steps(tick) if s[0] in ("ita", "itb", "kta", "ktb", "ota", "otb")]
        return out

    ROPE_UNITS = [u for u in range(UNITS) if unit_of(u)[0] in ROPE]

    def rot_steps(tick):
        out = []
        if tick % 2 == 1 and (tick - 3) // 2 in ROPE_UNITS and tick >= 3:
            out.append(("rot", ROPE_UNITS.index((tick - 3) // 2)))
        out += [("vt", n) for n, t in enumerate((12, 22, 24)) if t == tick]
        if tick == 26:
            out.append(("kw", 0))
        return out

    def sample_steps(tick):
        out = []
        d = tick - SA0
        out += [(s,) for s, v in (("ks_t", 0), ("s_score", 2), ("s_turn", 4), ("s_back", 6), ("s_out", 7)) if d == v]
        for h in range(NREC):
            d = tick - (SR0 + SRS * h)
            out += [(s, h) for s, v in (("r_turn", 0), ("r_outer", 2), ("r_o", 4)) if d == v]
        d = tick - (SR0 + SRS * NREC)
        out += [(s,) for s, v in (("r_rows", 0), ("r_cols", 2)) if d == v]
        return out

    def y_added(i):
        by_vector = i in Y_VECTOR
        return sem("y_vector" if by_vector else "y_pool"), sum((k in Y_VECTOR) == by_vector for k in range(i + 1))

    def x2_back(i):
        return (sem("x2_back0"), 16) if i < 4 else (sem("x2_back1"), 32)

    V_GROUPS = [(0, 4), (4, 4), (8, 1)]

    block = nc.Block()
    blk = block.__enter__()

    @blk.sync
    def _(sp):
        def load_x(i):
            if i >= 3:
                sp.wait_ge(sem("h_rows"), i - 2)
            sp.dma_start(xr_first(i), x_rows(i)).then_inc(sem(f"x0_in{i % 3}"), 16)

        def load_weight(n):
            if n >= 2:
                sp.wait_ge(sem("w_split"), n - 1)
            for dst, src in weight_parts(n):
                sp.dma_start(dst, src).then_inc(sem(f"raw_in{n % 2}"), 16)

        load_x(0)
        sp.dma_start(gb0[:], gain("norm_pre_mix")).then_inc(sem("g_in"), 16)
        sp.dma_start(ident[:], t_in["c_ident"]).then_inc(sem("id_in"), 16)
        load_x(1)
        load_x(2)
        load_weight(0)
        for i in range(3, 6):
            load_x(i)
            load_weight(i - 2)
        for dst, src in ((perm[:], t_in["c_perm"]), (amask[:], t_in["c_amask"]), (lmask32[:], t_in["c_lmask"]),
                         (cos[:], t_in["c_cos"]), (sin[:], t_in["c_sin"]),
                         (sink[:], t_in["attn_sinks"].partition_broadcast(P).rearrange("p o h -> p (o h)"))):
            sp.dma_start(dst, src).then_inc(sem("const_in"), 16)
        for l in range(2):
            sp.dma_start(lbl[:, l, :], t_in["rec_lb"][l].rearrange("(h p) -> p h", p=P), allow_slow_non_contiguous=True).then_inc(sem("const_in"), 16)
        sp.dma_start(rnorm[:], t_in["rec_out_norm"][0].rearrange("h v -> v h"), allow_slow_non_contiguous=True).then_inc(sem("const_in"), 16)
        for b in range(DECB):
            sp.dma_start(sinkc[NQ * b:NQ * b + NQ, :], t_in["attn_sinks"].rearrange("o h -> h o"), allow_slow_non_contiguous=True).then_inc(sem("const_in"), 16)
        for i in range(6, RT):
            load_x(i)
        stores = 0
        for tick in range(TICKS):
            for n in split_at(tick):
                load_weight(n)
            if tick == 28:
                sp.wait_ge(sem("kw_out"), 1)
                sp.dma_start(t_out["k_p"].rearrange("o b w n d -> (o b w) (n d)"), kwin[:]).then_inc(sem("stored"), 16)
            if tick == 30:
                sp.wait_ge(sem("v_rows"), 3)
                sp.dma_start(t_out["v_p"].rearrange("o b w n d -> (o b w) (n d)"), vrow[:, NBLK - 1, :]).then_inc(sem("stored"), 16)
            if tick == AT0 + 2 * NITEM + 5:
                sp.wait_ge(sem("at_out"), NITEM)
                sp.wait_ge(sem("kw_out"), 1)
                for dst, cache, new in ((ks, "cache_k_win", kn_s), (vs, "cache_v_win", vrow[:, NBLK, :])):
                    sp.dma_start(dst[0:P - 1, :, :], t_in[cache][0, :, 1:WIN].rearrange("b w n d -> w b (n d)"))\
                      .then_inc(sem("win_in"), 16)
                    for b in range(DECB):
                        sp.dma_start(dst[P - 1:P, b, :], new[b:b + 1, :]).then_inc(sem("win_in"), 16)
            if tick == SA0:
                sp.wait_ge(sem("win_in"), WIN_LOADS)
                for src, dst in ((ks, "k_s"), (vs, "v_s")):
                    sp.dma_start(t_out[dst][0].rearrange("b w n d -> w b (n d)"), src[:]).then_inc(sem("stored"), 16)
            for step in sample_steps(tick + 1):
                if step[0] == "r_turn":
                    h = step[1]
                    if h:
                        sp.wait_ge(sem("s_o"), h)
                        sp.wait_ge(sem("st_out"), 16 * h)
                    else:
                        sp.wait_ge(sem("at_out"), NITEM)
                    sp.dma_start(st[:], t_in["state_hgrn"][0, :, h].rearrange("b k v -> k b v")).then_inc(sem("st_in"), 16)
            for step in sample_steps(tick):
                if step[0] == "r_o":
                    h = step[1]
                    sp.wait_ge(sem("s_state"), 2 * h + 2)
                    sp.dma_start(t_out["st_s"][0, :, h].rearrange("b k v -> k b v"), st[:]).then_inc(sem("st_out"), 16)
            for step in recurrence_steps(tick):
                if step[0] == "o":
                    sp.wait_ge(sem("chain"), NBLK * (step[1] + 1))
                    sp.dma_start(t_out["st_p"][0, 0, step[1]], states[:, NBLK, :]).then_inc(sem("stp_out"), 16)
        for n in range(NIN + 6, N12):
            load_weight(n)
        sp.wait_ge(sem("stored"), 64)
        sp.wait_ge(sem("st_out"), 16 * NREC)
        sp.wait_ge(sem("stp_out"), 16 * NREC)
        sp.wait_ge(sem("mix_done"), 1)
        sp.dma_start(gbl[:], gain("norm_post_mix")).then_inc(sem("g_in"), 16)
        sp.dma_start(gb2[:], gain("norm_pre_ffn")).then_inc(sem("g_in"), 16)

        def ffn_raw(g, j, k):
            w = t_in["w_gate" if k == 0 else "w_up"][0]
            n = N12 + 4 * g + 2 * j + k
            sp.wait_ge(sem("w_split"), n - 1)
            sp.dma_start(raw[:, k], w[:, bass.ds(2 * P * g + P * j, P)].rearrange("(k p) n -> p k n", p=P))\
              .then_inc(sem(f"raw_in{k}"), 16)

        def load_row(i, buf, src, free_sem, free_val):
            if free_val > 0:
                sp.wait_ge(sem(free_sem), free_val)
            r, w = rows_of(i)
            sp.dma_start(buf[0:w, i % 2, :], src).then_inc(sem(f"x_in{i % 2}"), 16)

        def ffn_down(g):
            for j in range(2):
                if not isinstance(g, int) or g > 0:
                    sp.wait_ge(sem("d_split"), 2 * g + j - 1)
                sp.dma_start(draw[:, j, :], t_in["w_down"][0, bass.ds(2 * P * g + P * j, P), :]).then_inc(sem(f"draw_in{j}"), 16)

        load_row(0, xr, x_rows(0), "", 0)
        load_row(1, xr, x_rows(1), "", 0)
        for k in range(2):
            ffn_raw(0, 0, k)
        for i in range(RT):
            if i == 4:
                for k in range(2):
                    ffn_raw(0, 1, k)
            if i == 6:
                sp.wait_ge(sem("unit"), UNITS + CH * NOUT)
                ffn_down(0)
            if i + 2 < RT:
                load_row(i + 2, xr, x_rows(i + 2), "x2", i + 1)
            sp.wait_ge(sem("x2"), i + 1)
            r, w = rows_of(i)
            sp.dma_start(x2d[r:r + w, :], x2r[0:w, i % 2, :]).then_inc(sem(f"x2_out{i % 2}"), 16)
        sp.wait_ge(sem("x2_out0"), 16 * 5)
        sp.wait_ge(sem("x2_out1"), 16 * 4)

        def next_raw(g):
            for j in range(2):
                for k in range(2):
                    ffn_raw(g + 1, j, k)

        next_raw(0)
        with sp.Fori(1, GROUPS - 1) as g:
            ffn_down(g)
            next_raw(g)
        ffn_down(GROUPS - 1)
        sp.dma_start(gbl[:], gain("norm_post_ffn")).then_inc(sem("g_in"), 16)
        sp.wait_ge(sem("up_mm"), 6 * GROUPS)
        for a in range(2):
            sp.dma_start(x2b[:, 4 * a:4 * a + 4, :], x2d[4 * P * a:4 * P * a + 4 * P, :].rearrange("(i p) d -> p i d", p=P))\
              .then_inc(sem(f"x2_back{a}"), 16)
        sp.dma_start(x2b[0:DECB, NBLK, :], x2d[SEQ:ROWS, :]).then_inc(sem("x2_back1"), 16)
        for i in range(RT):
            sp.wait_ge(*y_added(i))
            sp.dma_start(y_rows(i), x2b[0:rows_of(i)[1], i, :]).then_inc(sem("y_out"), 16)
        sp.wait_ge(sem("y_out"), 16 * RT)

    @blk.gpsimd
    def _(pool):
        def weight_lo(n, slot=None):
            hi, lo = w_tiles(n) if slot is None else (w_hi[:, slot], w_lo[:, slot])
            pool.wait_ge(sem("w_hi_done"), n + 1)
            pool.tensor_tensor(lo, raw[:, (n if slot is None else slot) % 2], hi.bitcast(F32), ALU.subtract)\
                .then_inc(sem("w_split"), 1)

        pool.memset(kt2[:], 0.0).then_inc(sem("kt2_zero"), 1)
        pool.memset(qp[:], 0.0).then_inc(sem("qp_zero"), 1)
        for n in range(LEAD):
            weight_lo(n)
        pool.wait_ge(sem("const_in"), NCONST)
        pool.tensor_copy(lmask[:], lmask32[:]).then_inc(sem("lmask_done"), 1)
        for tick in range(TICKS):
            for step in recurrence_steps(tick):
                if step[0] == "prep":
                    h = step[1]
                    pool.wait_ge(sem("f_done"), h + 1)
                    if h:
                        pool.wait_ge(sem("chain"), NBLK * h)
                    for n in range(1, LEVELS + 1):
                        src = r_f[:, 0:SEQ] if n == 1 else g_level(n - 1)
                        if n > 1:
                            pool.wait_ge(sem("g_prod"), LEVELS * h + n - 1)
                        v = src.rearrange("p (b e) -> p b e", e=2)
                        pool.tensor_tensor(g_level(n), v[:, :, 0], v[:, :, 1], ALU.mult).then_inc(sem("g_prod"), 1)
            for n in split_at(tick):
                weight_lo(n)
        for n in range(NIN + 6, N12):
            weight_lo(n)

        def hidden_lo(q, j, c, e):
            pool.wait_ge(sem("h_hi_done"), q + 1)
            pool.tensor_tensor(h_lo[:, j, cols(c)], hf[:, e, :], h_hi[:, j, cols(c)].bitcast(F32), ALU.subtract)\
                .then_inc(sem("h_lo_done"), 1)

        def down_lo_tile(g, j):
            pool.wait_ge(sem("d_hi_done"), 2 * g + j + 1)
            pool.tensor_tensor(d_lo[:, j, :], draw[:, j, :], d_hi[:, j, :].bitcast(F32), ALU.subtract)\
                .then_inc(sem("d_split"), 1)

        for slot in range(SLOTS):
            for step, i in row_steps(slot):
                if step == "out":
                    r, w = rows_of(i)
                    pool.wait_ge(sem("p_t"), i + 1)
                    pool.wait_ge(sem(f"x_in{i % 2}"), 16 * (i // 2 + 1))
                    if i >= 2:
                        pool.wait_ge(sem(f"x2_out{i % 2}"), 16 * (i // 2))
                        pool.wait_ge(sem("h2_rows"), i - 1)
                    pool.tensor_tensor(x2r[0:w, i % 2, :], tr[0:w, i % 2, :], xr[0:w, i % 2, :], ALU.add).then_inc(sem("x2"), 1)
            for n in first_tiles(slot):
                weight_lo(n, n % 4)
            if slot >= 24 and slot % 2:
                q = (slot - 24) // 2
                hidden_lo(q, q % 2, q // 2, q % 2)
            if slot in DOWN_SLOTS:
                down_lo_tile(0, DOWN_SLOTS.index(slot))

        def down_lo(g):
            for j in range(2):
                down_lo_tile(g, j)

        def next_lo(g, j):
            for k in range(2):
                weight_lo(4 * g + (N12 + 4 + 2 * j + k), (N12 + 2 * j + k) % 4)

        def ffn(g, more):
            down_lo(g)
            for j in range(2):
                for c in range(CH):
                    hidden_lo(6 * g + (3 * j + c), j, c, (3 * j + c) % 2)
                if more:
                    next_lo(g, j)

        next_lo(0, 0)
        next_lo(0, 1)
        with pool.Fori(1, GROUPS - 1) as g:
            ffn(g, True)
        ffn(GROUPS - 1, False)
        for i in range(RT):
            if i not in Y_VECTOR:
                r, w = rows_of(i)
                pool.wait_ge(sem("y_t"), i + 1)
                pool.wait_ge(*x2_back(i))
                pool.tensor_tensor(x2b[0:w, i, :], ty[0:w, i % 4, :], x2b[0:w, i, :], ALU.add).then_inc(sem("y_pool"), 1)

    @blk.scalar
    def _(act):
        def copy(out, in_):
            return act.activation(out, in_, ACT.Copy)

        def weight_hi(n, slot=None, count=None, used=None):
            hi = w_tiles(n)[0] if slot is None else w_hi[:, slot]
            part = (n if slot is None else slot) % 2
            act.wait_ge(sem(f"raw_in{part}"), raw_count[n] if count is None else count)
            if used is not None:
                act.wait_ge(sem(used[0]), used[1])
            elif NIN + 2 <= n < NIN + 6:
                act.wait_ge(sem("o_mm"), NREC)
                act.wait_ge(sem("s_os"), NREC)
                act.wait_ge(sem("st_out"), 16 * NREC)
                act.wait_ge(sem("stp_out"), 16 * NREC)
            elif n >= N12:
                act.wait_ge(sem("unit"), UNITS + 2 * NOUT + (0, 1, 6, 7)[n - N12] + 1)
            elif n >= NIN + 6:
                act.wait_ge(sem("unit"), LAST_UNIT[n - 8] + 1)
            elif n >= 4:
                act.wait_ge(sem("unit"), LAST_UNIT[n - 4] + 1)
            copy(hi, raw[:, part]).then_inc(sem("w_hi_done"), 1)

        def root(out, in_, scale, done, value):
            act.wait_ge(sem(done), value)
            return act.activation(out, in_, ACT.Sqrt, bias=eps[0:out.shape[0], :], scale=scale)

        def squares(i):
            r, w = rows_of(i)
            act.wait_ge(sem(f"x0_in{i % 3}"), 16 * (i // 3 + 1))
            if i >= 3:
                act.wait_ge(sem("n_tr"), 2 * (i - 2))
            act.activation(hr_first(i), xr_first(i), ACT.Square, accum_out=ss[0:w, 0, i:i + 1]).then_inc(sem("n_ss"), 1)
            root(std[0:w, 0, i:i + 1], ss[0:w, 0, i:i + 1], 1.0 / DM, "n_ss", i + 1).then_inc(sem("n_std"), 1)

        def high(i, tr_sem, hi_sem, banks):
            r, w = rows_of(i)
            for kk in range(2):
                q = 2 * i + kk
                act.wait_ge(sem(tr_sem), q + 1)
                copy(act_hi[:, 4 * kk:4 * kk + 4, r:r + w],
                     banks[q % len(banks)].rearrange("p (k r) -> p k r", k=4)[:, :, 0:w]).then_inc(sem(hi_sem), 1)

        act.wait_ge(sem("eps_set"), 1)
        act.activation(ostd[:, 0:1], eps[:], ACT.Sqrt)
        squares(0)
        squares(1)

        def unit_read(u):
            kind, m, c = unit_of(u)
            act.wait_ge(sem("unit"), u + 1)
            src = J[u % 2][:, 0:CW]
            if kind == "k":
                copy(kraw[:, cols(c)], src).then_inc(sem("unit_act"), 1)
            elif kind == "v":
                copy(vt[:, cols(c)], src).then_inc(sem("unit_act"), 1)
            elif kind == "q":
                copy(mix[:, m, cols(c)], src).then_inc(sem("unit_act"), 1)
            elif kind == "ri":
                if m:
                    act.wait_ge(sem("i_turned"), 2 * m)
                    act.wait_ge(sem("s_saved"), m)
                else:
                    act.wait_ge(sem("v_turned"), 3)
                copy(r_i[:, cols(c)], src).then_inc(sem("unit_act"), 1)
            else:
                s = units_before(SILU, u)
                if s >= 2:
                    act.wait_ge(sem("th_read"), s - 1)
                act.activation(th[:, s % 2, :], src, ACT.Tanh, scale=0.5).then_inc(sem("unit_act"), 1)

        def mix_high(c):
            act.wait_ge(sem("at_out"), NITEM)
            act.wait_ge(sem("s_mixed"), 1)
            copy(act_hi[:, 0:4, cols(c)], mix[:, 0:4, cols(c)]).then_inc(sem("mix_hi"), 1)
            act.wait_ge(sem("th_read"), units_before(SILU, UNITS - CH + c + 1))
            if c == CH - 1:
                act.wait_ge(sem("mix_done"), 1)
            copy(act_hi[:, 4:8, cols(c)], mix[:, 4:8, cols(c)]).then_inc(sem("mix_hi"), 1)

        for tick in range(TICKS):
            for i in NORM_ROWS.get(tick // 2, ()) if tick % 2 == 0 else ():
                if 2 <= i + 1 < RT:
                    squares(i + 1)
                high(i, "n_tr", "n_hi", NB)
                if 1 <= i <= LEAD:
                    weight_hi(i - 1)
            if tick == AT0:
                act.wait_ge(sem("lb_in"), 1)
                act.activation(lbt[:, 2:4, :], lbt[:, 0:2, :], ACT.Exp).then_inc(sem("lb_exp"), 1)
            for n in split_at(tick):
                weight_hi(n)
            for step in rot_steps(tick):
                if step[0] == "vt":
                    act.wait_ge(sem("v_turned"), step[1] + 1)
                    b0, n = V_GROUPS[step[1]]
                    if n == 4:
                        copy(vrow[:, b0:b0 + 4, :], BR.rearrange("p (b d) -> p b d", b=4)).then_inc(sem("v_rows"), 1)
                    else:
                        copy(vrow[0:DECB, b0, :], BR[0:DECB, 0:P]).then_inc(sem("v_rows"), 1)
                if step[0] == "kw":
                    act.wait_ge(sem("kw_mm"), 1)
                    copy(kn_s[:, :], BR[0:DECB, P:2 * P])
                    copy(kwin[:], BR[:, 0:P]).then_inc(sem("kw_out"), 1)
            for step, i in attention_steps(tick):
                t, j, e = i // NBLK, i % NBLK, i % 2
                k0 = WIN if j == 0 else 0
                if step == "S":
                    act.wait_ge(sem("at_max"), i + 1)
                    if i >= 2:
                        act.wait_ge(sem("at_pt"), i - 1)
                    for g in range(NKV):
                        act.activation(prob[:, e, g, k0:], sm[:, g, k0:], ACT.Exp, bias=negm[:, e, g:g + 1], scale=SCALE,
                                       accum_out=den[:, e, g:g + 1])
                    act.activation(esk[:, e, :], tsum[:, e, :], ACT.Exp).then_inc(sem("at_exp"), 1)
                elif step == "PT":
                    act.wait_ge(sem("at_pt"), i + 1)
                    if i >= 1:
                        act.wait_ge(sem("at_pv"), i)
                    kb = 1 if j == 0 else 0
                    pv = pt[:].rearrange("p (g b) q -> p g b q", g=2)
                    bv = BP.rearrange("p (g b q) -> p g b q", g=2, b=2)
                    copy(pv[:, :, kb:, :], bv[:, :, kb:, :]).then_inc(sem("at_ptc"), 1)
                elif step == "OT":
                    act.wait_ge(sem("at_ot"), i + 1)
                    copy(mix[:, t, P * j:P * j + P], BO[:, P:2 * P]).then_inc(sem("at_out"), 1)
            for step in recurrence_steps(tick):
                h = step[1]
                if step[0] in ("ita", "itb"):
                    a = step[0] == "itb"
                    act.wait_ge(sem("i_turned"), 2 * h + a + 1)
                    if h and not a:
                        act.wait_ge(sem("o_mm"), h)
                    copy(irow[:, 4 * a:4 * a + 4, :], BR.rearrange("p (b d) -> p b d", b=4)).then_inc(sem("i_rows"), 1)
                if step[0] in ("kta", "ktb"):
                    a = step[0] == "ktb"
                    act.wait_ge(sem("k_turned"), 2 * h + a + 1)
                    copy(krow[:, 4 * a:4 * a + 4, :], BR.rearrange("p (b d) -> p b d", b=4)).then_inc(sem("k_rows"), 1)
                if step[0] == "o":
                    act.wait_ge(sem("o_mm"), h + 1)
                    for c in range(NBLK):
                        ins = act.activation(ast[:, c, :], BL[c // 4][:, P * (c % 4):P * (c % 4) + P], ACT.Square,
                                             accum_out=oss[:, c:c + 1])
                    ins.then_inc(sem("o_ss"), 1)
                    root(ostd[:], oss[:], 1.0 / (4 * RD), "o_ss", h + 1).then_inc(sem("o_std"), 1)
            for step in sample_steps(tick):
                if step[0] == "ks_t":
                    for a, b in ((0, BS), (1, BP)):
                        act.wait_ge(sem("ks_turned"), a + 1)
                        copy(kst[:, 4 * a:4 * a + 4, :], b.rearrange("p (b d) -> p b d", b=4)).then_inc(sem("ks_cols"), 1)
                if step[0] == "s_score":
                    act.wait_ge(sem("s_score"), 1)
                    copy(stx[:], BO[:, 0:DECB * NQ]).then_inc(sem("s_scored"), 1)
                if step[0] == "s_turn":
                    act.wait_ge(sem("s_max"), 1)
                    n = DECB * NQ
                    act.activation(px[:], BP[0:n, 0:P], ACT.Exp, bias=sst[0:n, 1:2], scale=SCALE, accum_out=sst[0:n, 3:4])
                    act.activation(sst[0:n, 4:5], sst[0:n, 2:3], ACT.Exp).then_inc(sem("s_exp"), 1)
                if step[0] == "s_back":
                    act.wait_ge(sem("s_back"), 1)
                    copy(ptx[:], BP[:, 0:DECB * NQ]).then_inc(sem("s_pt"), 1)
                if step[0] == "r_turn":
                    act.wait_ge(sem("s_turned"), step[1] + 1)
                    if step[1]:
                        act.wait_ge(sem("s_outer"), step[1])
                    copy(ki[:], BP[0:DECB, 0:2 * P].rearrange("p (a d) -> p a d", a=2)).then_inc(sem("s_ki"), 1)
                if step[0] == "r_rows":
                    n = NREC * DECB
                    act.wait_ge(sem("so_turned"), 1)
                    act.activation(px[0:n, :], BP[0:n, 0:P], ACT.Square, accum_out=sst[0:n, 5:6]).then_inc(sem("so_ss"), 1)
                    root(sst[0:n, 6:7], sst[0:n, 5:6], 1.0 / (4 * RD), "so_ss", 1).then_inc(sem("so_std"), 1)
            if tick % 2:
                unit_read(tick // 2)
                if tick // 2 >= UNITS - CH:
                    mix_high(tick // 2 - (UNITS - CH))
        for n in range(NIN + 6, N12):
            weight_hi(n)

        def gate(q, e, first=False):
            act.wait_ge(sem("gate_mm"), q + 1)
            if not first:
                act.wait_ge(sem("hf_done"), q - 1)
            act.activation(sg[:, e, :], bank[e][:, 0:CW], ACT.Silu).then_inc(sem("gate_done"), 1)

        def hidden_hi(q, j, c, e):
            act.wait_ge(sem("hf_done"), q + 1)
            copy(h_hi[:, j, cols(c)], hf[:, e, :]).then_inc(sem("h_hi_done"), 1)

        for slot in range(SLOTS):
            for step, i in row_steps(slot):
                r, w = rows_of(i)
                if step == "out":
                    act.wait_ge(sem("p_tr"), i + 1)
                    if i >= 2:
                        act.wait_ge(sem("h2_tr"), 2 * (i - 1))
                    act.activation(tr[0:w, i % 2, :].rearrange("p (a b) -> p a b", a=2), pair[2][0:w, :, :], ACT.Square,
                                   accum_out=ss[0:w, 0, i:i + 1]).then_inc(sem("p_ss"), 1)
                    root(std[0:w, 0, i:i + 1], ss[0:w, 0, i:i + 1], 1.0 / DM, "p_ss", i + 1).then_inc(sem("p_std"), 1)
                if step == "mid":
                    act.wait_ge(sem("x2"), i + 1)
                    act.activation(tr[0:w, i % 2, :], x2r[0:w, i % 2, :], ACT.Square, accum_out=ss[0:w, 1, i:i + 1])\
                        .then_inc(sem("q_ss"), 1)
                    root(std[0:w, 1, i:i + 1], ss[0:w, 1, i:i + 1], 1.0 / DM, "q_ss", i + 1).then_inc(sem("q_std"), 1)
                if step == "in":
                    high(i, "h2_tr", "h2_hi", bank[6:8])
            if slot < 24:
                m, c = slot % NOUT, slot // NOUT
                u = UNITS + slot
                act.wait_ge(sem("unit"), u + 1)
                act.wait_ge(sem("mix_lo"), 2 * c + 2)
                copy(mix[:, m, cols(c)], J[u % 2][:, 0:CW]).then_inc(sem("unit_act"), 1)
            for n in first_tiles(slot):
                weight_hi(n)
            if slot >= 24:
                q = (slot - 24) // 2
                if slot % 2 == 0:
                    gate(q, q % 2, q < 2)
                else:
                    hidden_hi(q, q % 2, q // 2, q % 2)
            if slot in DOWN_SLOTS:
                j = DOWN_SLOTS.index(slot)
                act.wait_ge(sem("h2_rows"), RT)
                act.wait_ge(sem("x2_out0"), 16 * 5)
                act.wait_ge(sem("x2_out1"), 16 * 4)
                act.wait_ge(sem(f"draw_in{j}"), 16)
                copy(d_hi[:, j, :], draw[:, j, :]).then_inc(sem("d_hi_done"), 1)

        def down_hi(g):
            for j in range(2):
                act.wait_ge(sem(f"draw_in{j}"), 16 * g + 16)
                act.wait_ge(sem("down_mm"), 24 * g)
                copy(d_hi[:, j, :], draw[:, j, :]).then_inc(sem("d_hi_done"), 1)

        def next_hi(g, j, done):
            for k in range(2):
                n = 4 * g + (N12 + 4 + 2 * j + k)
                weight_hi(n, (N12 + 2 * j + k) % 4, slot_total[k] + 16 * (2 + j + 1) + 32 * g, (("gate_mm", "up_mm")[k], done))

        def ffn(g, more):
            down_hi(g)
            for j in range(2):
                for c in range(CH):
                    q, e = 6 * g + (3 * j + c), (3 * j + c) % 2
                    gate(q, e)
                    hidden_hi(q, j, c, e)
                if more:
                    next_hi(g, j, 6 * g + (3 * j + 3))

        next_hi(0, 0, 5)
        next_hi(0, 1, 6)
        with act.Fori(1, GROUPS - 1) as g:
            ffn(g, True)
        ffn(GROUPS - 1, False)

        for i in range(RT):
            r, w = rows_of(i)
            act.wait_ge(sem("y_tr"), i + 1)
            if i >= 4:
                act.wait_ge(*y_added(i - 4))
            act.activation(ty[0:w, i % 4, :].rearrange("p (a b) -> p a b", a=2), pair[i % 2][0:w, :, :], ACT.Square,
                           accum_out=ss[0:w, 1, i:i + 1]).then_inc(sem("y_ss"), 1)
            root(std[0:w, 1, i:i + 1], ss[0:w, 1, i:i + 1], 1.0 / DM, "y_ss", i + 1).then_inc(sem("y_std"), 1)

    @blk.tensor
    def _(pe):
        def rows_to_cols(rows, i, banks, q_sem, free_sem):
            r, w = rows_of(i)
            for kk in range(2):
                q = 2 * i + kk
                if q >= len(banks):
                    pe.wait_ge(sem(free_sem), q - len(banks) + 1)
                for k in range(4):
                    mm = pe.transpose(banks[q % len(banks)][:, P * k:P * k + w],
                                      rows[:, P * (4 * kk + k):P * (4 * kk + k) + P], ident[0:w, 0:w])
                mm.then_inc(sem(q_sem), 1)

        pe.wait_ge(sem("id_in"), 16)

        def products(out, weights, c, lo, hi):
            for k in range(lo, hi):
                for s, (a, b) in enumerate(((weights[0], act_hi), (weights[0], act_lo), (weights[1], act_hi))):
                    mm = pe.matmul(out, a[:, k, :], b[:, k, cols(c)], start=(k == 0 and s == 0), stop=(k == KT - 1 and s == 2))
            return mm

        br_free = None

        def take_br(sem_name, value):
            nonlocal br_free
            if br_free is not None:
                pe.wait_ge(sem(br_free[0]), br_free[1])
            br_free = (sem_name, value)

        bl_free = None

        def take_bl(sem_name, value):
            nonlocal bl_free
            if bl_free is not None:
                pe.wait_ge(sem(bl_free[0]), bl_free[1])
            bl_free = (sem_name, value)

        for tick in range(TICKS):
            u, half = tick // 2, tick % 2
            n, c = ORDER[u]
            if half == 0:
                for i in NORM_ROWS.get(u, ()):
                    pe.wait_ge(sem("h_rows"), i + 1)
                    rows_to_cols(hr_first(i), i, NB, "n_tr", "n_lo")
                if u < LEAD * CH:
                    pe.wait_ge(sem("n_lo"), 2 * min(RT, chunk_of_rows(c)))
                pe.wait_ge(sem("w_split"), n + 1)
                if u >= 2:
                    pe.wait_ge(sem("unit_act"), u - 1)
                    if unit_of(u - 2)[0] in ("rq", "rg"):
                        pe.wait_ge(sem("th_read"), units_before(SILU, u - 1))
            mm = products(J[u % 2][:, 0:CW], w_tiles(n), c, 4 * half, 4 * half + 4)
            if half:
                mm.then_inc(sem("unit"), 1)
            for step in rot_steps(tick):
                if step[0] == "rot":
                    r = step[1]
                    if r == 0:
                        pe.wait_ge(sem("const_in"), NCONST - 0)
                    v = ROPE_UNITS[r]
                    kind, m, c = unit_of(v)
                    pe.wait_ge(sem("unit_act"), v + 1)
                    src = kraw[:, cols(c)] if kind == "k" else mix[:, m, cols(c)]
                    take_br("rot_read", r + 1)
                    pe.matmul(BR[:, 0:CW], perm[:], src, start=True, stop=True).then_inc(sem("rot_mm"), 1)
                if step[0] == "vt":
                    b0, nb = V_GROUPS[step[1]]
                    pe.wait_ge(sem("unit_act"), unit_index("v", 0, 1 if step[1] == 0 else 2) + 1)
                    take_br("v_rows", step[1] + 1)
                    for b in range(nb):
                        r, w = rows_of(b0 + b)
                        mm = pe.transpose(BR[0:w, P * b:P * b + P], vt[:, r:r + w], ident[:])
                    mm.then_inc(sem("v_turned"), 1)
                if step[0] == "kw":
                    pe.wait_ge(sem("rope"), ROPE_UNITS.index(unit_index("k", 0, 2)) + 1)
                    take_br("kw_out", 1)
                    for (r, w), c in ((rows_of(NBLK - 1), 0), (rows_of(NBLK), P)):
                        for g in range(NKV):
                            mm = pe.matmul(BR[0:w, c:c + P], kt2[:, g, r:r + w], ident[:], start=(g == 0), stop=(g == NKV - 1))
                    mm.then_inc(sem("kw_mm"), 1)
            for step, i in attention_steps(tick):
                t, j, e = i // NBLK, i % NBLK, i % 2
                kbs = (1,) if j == 0 else (0, 1)
                if step == "S":
                    c = (P * (j + 1) - 1) // CW
                    pe.wait_ge(sem("rope"), 1 + max(ROPE_UNITS.index(unit_index(*x, c)) for x in (("k", 0), ("q", t))))
                    if i == 0:
                        pe.wait_ge(sem("n_lo"), 2 * RT)
                    if i:
                        pe.wait_ge(sem("at_max"), i)
                    out = BS.rearrange("p (g k) -> p g k", g=2)
                    if j == 0:
                        pe.matmul(out[:, :, WIN:], mix[:, t, 0:P], kt2[:, :, 0:P], start=True, stop=True).then_inc(sem("at_s"), 1)
                    else:
                        pe.matmul(out, mix[:, t, P * j:P * j + P], kt2[:, :, P * (j - 1):P * (j + 1)],
                                  start=True, stop=True).then_inc(sem("at_s"), 1)
                elif step == "PT":
                    pe.wait_ge(sem("at_exp"), i + 1)
                    if i:
                        pe.wait_ge(sem("at_ptc"), i)
                    for g in range(NKV):
                        for kb in kbs:
                            mm = pe.transpose(BP[:, P * (2 * g + kb):P * (2 * g + kb) + P], prob[:, e, g, P * kb:P * kb + P], ident[:])
                    mm.then_inc(sem("at_pt"), 1)
                elif step == "PV":
                    pe.wait_ge(sem("at_ptc"), i + 1)
                    pe.wait_ge(sem("v_rows"), j // 4 + 1)
                    if i:
                        pe.wait_ge(sem("at_out"), i)
                    for g in range(NKV):
                        for kb in kbs:
                            mm = pe.matmul(BO[:, HD * g:HD * g + HD], pt[:, 2 * g + kb, :], vrow[:, j - 1 + kb, HD * g:HD * g + HD],
                                           start=(kb == kbs[0]), stop=(kb == 1))
                    mm.then_inc(sem("at_pv"), 1)
                elif step == "OT":
                    pe.wait_ge(sem("at_or"), i + 1)
                    pe.transpose(BO[:, P:2 * P], orow[:].rearrange("p g d -> p (g d)"), ident[:]).then_inc(sem("at_ot"), 1)
            for step in recurrence_steps(tick):
                h = step[1]
                if step[0] in ("ita", "itb"):
                    a = step[0] == "itb"
                    if not a:
                        pe.wait_ge(sem("unit_act"), unit_index("ri", h, 2) + 1)
                    take_br("i_rows", 2 * h + a + 1)
                    for b in range(4):
                        c = 4 * a + b
                        mm = pe.transpose(BR[:, P * b:P * b + P], r_i[:, P * c:P * c + P], ident[:])
                    mm.then_inc(sem("i_turned"), 1)
                if step[0] == "diag":
                    pe.wait_ge(sem("hq_prep"), h + 1)
                    take_bl("diag_read", h + 1)
                    for c in range(NBLK):
                        mm = pe.matmul(BL[c // 4][:, P * (c % 4):P * (c % 4) + P], hk[:, P * c:P * c + P], r_q[:, P * c:P * c + P],
                                       start=True, stop=True)
                    mm.then_inc(sem("diag_mm"), 1)
                if step[0] == "level":
                    n = step[2]
                    if n:
                        pe.wait_ge(sem("hq_step"), LEVELS * h + n)
                    if n == 0:
                        take_bl("level_read", LEVELS * (h + 1))
                    elif n >= 2:
                        pe.wait_ge(sem("level_read"), LEVELS * h + n - 1)
                    hs = 1 << n
                    qv = hq[:].rearrange("p (c b e s) -> p c b e s", c=NBLK, e=2, s=hs)
                    for c in range(NBLK):
                        mm = pe.matmul(BL[n % 2][:, P // 2 * c:P // 2 * (c + 1)], hk[:, P * c:P * c + P], qv[:, c, :, 1, :],
                                       start=True, stop=True)
                    mm.then_inc(sem("level_mm"), 1)
                if step[0] in ("kta", "ktb"):
                    a = step[0] == "ktb"
                    pe.wait_ge(sem("hq_step"), LEVELS * (h + 1))
                    take_br("k_rows", 2 * h + a + 1)
                    for b in range(4):
                        c = 4 * a + b
                        mm = pe.transpose(BR[:, P * b:P * b + P], hk[:, P * c:P * c + P], ident[:])
                    mm.then_inc(sem("k_turned"), 1)
                if step[0] == "u":
                    pe.wait_ge(sem("k_rows"), 2 * h + 2)
                    pe.wait_ge(sem("i_rows"), 2 * h + 2)
                    take_bl("chain", NBLK * (h + 1))
                    for c in range(NBLK):
                        mm = pe.matmul(BL[c // 4][:, P * (c % 4):P * (c % 4) + P], krow[:, c, :], irow[:, c, :], start=True, stop=True)
                    mm.then_inc(sem("u_mm"), 1)
                if step[0] == "o":
                    take_bl("o_norm", h + 1)
                    for c in range(NBLK):
                        out = BL[c // 4][:, P * (c % 4):P * (c % 4) + P]
                        mm = pe.matmul(out, ast[:, c, :], irow[:, c, :], start=True, stop=(c == 0))
                        if c:
                            mm = pe.matmul(out, hq[:, P * c:P * c + P], states[:, c, :], start=False, stop=True)
                    mm.then_inc(sem("o_mm"), 1)
                if step[0] in ("ota", "otb"):
                    a = step[0] == "otb"
                    pe.wait_ge(sem("o_norm"), h + 1)
                    take_br("o_cols", 2 * h + a + 1)
                    for b in range(4):
                        c = 4 * a + b
                        mm = pe.transpose(BR[:, P * b:P * b + P], orn[:, P * c:P * c + P], ident[:])
                    mm.then_inc(sem("o_turned"), 1)
            for step in sample_steps(tick):
                if step[0] == "ks_t":
                    pe.wait_ge(sem("win_in"), WIN_LOADS)
                    pe.wait_ge(sem("at_out"), NITEM)
                    for a, b in ((0, BS), (1, BP)):
                        for c in range(4):
                            mm = pe.transpose(b[:, P * c:P * c + P], ks[:, 4 * a + c, :], ident[:])
                        mm.then_inc(sem("ks_turned"), 1)
                if step[0] == "s_score":
                    pe.wait_ge(sem("ks_cols"), 2)
                    pe.wait_ge(sem("qp_done"), 1)
                    for b in range(DECB):
                        mm = pe.matmul(BO[:, NQ * b:NQ * b + NQ], kst[:, b, :], qp[:, b, :], start=True, stop=True)
                    mm.then_inc(sem("s_score"), 1)
                if step[0] == "s_turn":
                    pe.wait_ge(sem("s_scored"), 1)
                    pe.transpose(BP[0:DECB * NQ, 0:P], stx[:], ident[:]).then_inc(sem("s_turn"), 1)
                if step[0] == "s_back":
                    pe.wait_ge(sem("s_prob"), 1)
                    pe.transpose(BP[:, 0:DECB * NQ], px[:], ident[0:DECB * NQ, 0:DECB * NQ]).then_inc(sem("s_back"), 1)
                if step[0] == "s_out":
                    pe.wait_ge(sem("s_pt"), 1)
                    for b in range(DECB):
                        mm = pe.matmul(BO[:, NQ * b:NQ * b + NQ], vs[:, b, :], ptx[:, NQ * b:NQ * b + NQ], start=True, stop=True)
                    mm.then_inc(sem("s_out"), 1)
                if step[0] == "r_turn":
                    h = step[1]
                    pe.wait_ge(sem("ks_saved"), h + 1)
                    if h:
                        pe.wait_ge(sem("s_os"), h)
                    for a, x in ((0, k_s), (1, i_s)):
                        mm = pe.transpose(BP[0:DECB, P * a:P * a + P], x[:, h, :], ident[:])
                    mm.then_inc(sem("s_turned"), 1)
                if step[0] == "r_outer":
                    h = step[1]
                    pe.wait_ge(sem("s_ib"), h + 1)
                    if h == 0:
                        pe.wait_ge(sem("s_mixed"), 1)
                    for a, b in ((0, BS), (1, BO)):
                        mm = pe.matmul(b, ki[:, 0, :], ib[:, 4 * a:4 * a + 4, :], start=True, stop=True)
                    mm.then_inc(sem("s_outer"), 1)
                if step[0] == "r_o":
                    h = step[1]
                    pe.wait_ge(sem("s_state"), 2 * h + 2)
                    for b in range(DECB):
                        mm = pe.matmul(BP[:, b:b + 1], st[:, b, :], q_s[:, h, b:b + 1], start=True, stop=True)
                    mm.then_inc(sem("s_o"), 1)
                if step[0] == "r_rows":
                    pe.wait_ge(sem("s_os"), NREC)
                    pe.transpose(BP[0:NREC * DECB, 0:P], o_s[:].rearrange("p h b -> p (h b)"), ident[:]).then_inc(sem("so_turned"), 1)
                if step[0] == "r_cols":
                    n = NREC * DECB
                    pe.wait_ge(sem("so_norm"), 1)
                    pe.transpose(BP[:, 0:n], px[0:n, :], ident[0:n, 0:n]).then_inc(sem("so_cols"), 1)
        def cols_to_rows(i, out, out_sem):
            r, w = rows_of(i)
            for m in range(KT):
                mm = pe.transpose(out[0:w, m // 4, P * (m % 4):P * (m % 4) + P], mix[:, m, r:r + w], ident[:])
            mm.then_inc(sem(out_sem), 1)

        for slot in range(SLOTS):
            for step, i in row_steps(slot):
                if step == "out":
                    pe.wait_ge(sem("unit_act"), UNITS + NOUT * min(CH, (P * i + rows_of(i)[1] - 1) // CW + 1))
                    if i:
                        pe.wait_ge(sem("p_t"), i)
                    cols_to_rows(i, pair[2], "p_tr")
                if step == "in":
                    pe.wait_ge(sem("h2_rows"), i + 1)
                    rows_to_cols(tr[0:rows_of(i)[1], i % 2, :], i, bank[6:8], "h2_tr", "h2_lo")
            if slot < 24:
                m, c = slot % NOUT, slot // NOUT
                n, u = NIN + m, UNITS + slot
                if c == 0:
                    pe.wait_ge(sem("w_split"), n + 1)
                pe.wait_ge(sem("unit_act"), u - 1)
                if slot < 2:
                    pe.wait_ge(sem("th_read"), units_before(SILU, UNITS - 1 + slot))
                if m == 0:
                    pe.wait_ge(sem("mix_lo"), 2 * c + 2)
                products(J[u % 2][:, 0:CW], w_tiles(n), c, 0, KT).then_inc(sem("unit"), 1)
            else:
                q, k = (slot - 24) // 2, slot % 2
                c, j = q // 2, q % 2
                if j == 0 and k == 0:
                    pe.wait_ge(sem("h2_lo"), 2 * min(RT, chunk_of_rows(c)))
                if c == 0:
                    pe.wait_ge(sem("w_split"), N12 + 2 * j + k + 1)
                if q < 2 and k == 0:
                    pe.wait_ge(sem("unit_act"), UNITS + 24)
                if q >= 2:
                    pe.wait_ge(sem(("gate_done", "hf_done")[k]), q - 1)
                s4 = (N12 + 2 * j + k) % 4
                products(bank[2 * k + q % 2][:, 0:CW], (w_hi[:, s4], w_lo[:, s4]), c, 0, KT).then_inc(sem(("gate_mm", "up_mm")[k]), 1)

        def up(g):
            for j in range(2):
                for c in range(CH):
                    q = 6 * g + 3 * j + c
                    e = (3 * j + c) % 2
                    for k in range(2):
                        if c == 0:
                            pe.wait_ge(sem("w_split"), 4 * g + (N12 + 2 * j + k + 1))
                        pe.wait_ge(sem(("gate_done", "hf_done")[k]), q - 1)
                        s4 = (N12 + 2 * j + k) % 4
                        products(bank[2 * k + e][:, 0:CW], (w_hi[:, s4], w_lo[:, s4]), c, 0, KT)\
                            .then_inc(sem(("gate_mm", "up_mm")[k]), 1)

        def down(g, first, last):
            pe.wait_ge(sem("d_split"), 2 * g + 2)
            for c in range(CH):
                pe.wait_ge(sem("h_lo_done"), 2 * c + 2 if first else 6 * g + (4 + c))
                for m in range(KT):
                    v = KT * c + m
                    if not (first and v < 4):
                        pe.wait_ge(sem("acc_done"), 24 * g + (v - 3))
                    for j in range(2):
                        for s, (a, b) in enumerate(((d_hi, h_hi), (d_hi, h_lo), (d_lo, h_hi))):
                            mm = pe.matmul(bank[4 + v % 4][:, 0:CW], a[:, j, P * m:P * m + P], b[:, j, cols(c)],
                                           start=(j == 0 and s == 0), stop=(j == 1 and s == 2))
                    mm.then_inc(sem("down_mm"), 1)
                    if last and (c, m) in LAST_ROWS:
                        last_rows(LAST_ROWS.index((c, m)))

        def last_rows(i):
            r, w = rows_of(i)
            pe.wait_ge(sem("acc_done"), 24 * (GROUPS - 1) + KT * ((r + w - 1) // CW + 1))
            if i >= 2:
                pe.wait_ge(sem("y_t"), i - 1)
            cols_to_rows(i, pair[i % 2], "y_tr")

        down(0, True, False)
        with pe.Fori(1, GROUPS - 1) as g:
            up(g)
            down(g, False, False)
        up(GROUPS - 1)
        down(GROUPS - 1, False, True)
        for i in range(len(LAST_ROWS), RT):
            last_rows(i)

    @blk.vector
    def _(dve):
        chain = [0]

        def then(ins):
            chain[0] += 1
            ins.then_inc(sem("dve_chain"), 1)
            dve.wait_ge(sem("dve_chain"), chain[0])

        dve.memset(eps[:], EPS).then_inc(sem("eps_set"), 1)

        def norm_rows(i):
            r, w = rows_of(i)
            dve.wait_ge(sem("n_std"), i + 1)
            then(dve.reciprocal(rstd[0:w, 0, i:i + 1], std[0:w, 0, i:i + 1]))
            if i == 0:
                dve.wait_ge(sem("g_in"), 16)
            dve.scalar_tensor_tensor(out=hr_first(i), in0=xr_first(i), scalar=rstd[0:w, 0, i:i + 1],
                                     in1=gb0[0:w, :], op0=ALU.mult, op1=ALU.mult).then_inc(sem("h_rows"), 1)

        def low(i, hi_sem, lo_sem, banks):
            r, w = rows_of(i)
            for kk in range(2):
                q = 2 * i + kk
                dve.wait_ge(sem(hi_sem), q + 1)
                dve.tensor_tensor(act_lo[:, 4 * kk:4 * kk + 4, r:r + w],
                                  banks[q % len(banks)].rearrange("p (k r) -> p k r", k=4)[:, :, 0:w],
                                  act_hi[:, 4 * kk:4 * kk + 4, r:r + w].bitcast(F32), ALU.subtract).then_inc(sem(lo_sem), 1)

        norm_rows(0)
        norm_rows(1)

        def lower_bound():
            then(dve.tensor_tensor(lbt[:, 4, :], lbl[:, 0, :], lbl[:, 1, :], ALU.max))
            dve.tensor_tensor(lbt[:, 0, :], lbl[:, 0, :], lbt[:, 4, :], ALU.subtract)
            dve.tensor_tensor(lbt[:, 1, :], lbl[:, 1, :], lbt[:, 4, :], ALU.subtract).then_inc(sem("lb_in"), 1)
            then(dve.tensor_scalar(nsink[:], sink[:], -1.0, None, ALU.mult))
            dve.wait_ge(sem("lb_exp"), 1)
            then(dve.tensor_tensor(lbt[:, 5, :], lbt[:, 2, :], lbt[:, 3, :], ALU.add))
            then(dve.reciprocal(lbt[:, 6, :], lbt[:, 5, :]))
            then(dve.tensor_tensor(lbt[:, 4, :], lbt[:, 2, :], lbt[:, 6, :], ALU.mult))
            then(dve.tensor_scalar(lbt[:, 5, :], lbt[:, 4, :], -0.5, 0.5, ALU.mult, ALU.add))
            then(dve.tensor_tensor(lbt[:, 6, :], lbt[:, 4, :], lbt[:, 5, :], ALU.add))

        f_scale, f_shift = lbt[:, 5, :], lbt[:, 6, :]

        def rope(r):
            kind, m, c = unit_of(ROPE_UNITS[r])
            if r == 0:
                dve.wait_ge(sem("const_in"), NCONST)
            dve.wait_ge(sem("rot_mm"), r + 1)
            x = kraw[:, cols(c)] if kind == "k" else mix[:, m, cols(c)]
            tmp = sm_rope[:, 0:CW]
            then(dve.tensor_tensor(x, x, cos[:, cols(c)], ALU.mult))
            ins = dve.tensor_tensor(tmp, BR[:, 0:CW], sin[:, cols(c)], ALU.mult)
            ins.then_inc(sem("rot_read"), 1)
            dve.wait_ge(sem("rot_read"), r + 1)
            if kind == "q":
                dve.tensor_tensor(x, x, tmp, ALU.add).then_inc(sem("rope"), 1)
            else:
                if c == 0:
                    dve.wait_ge(sem("kt2_zero"), 1)
                dve.tensor_tensor(kt2[0:HD, 0, cols(c)], kraw[0:HD, cols(c)], tmp[0:HD, :], ALU.add)
                dve.tensor_tensor(kt2[HD:P, 1, cols(c)], kraw[HD:P, cols(c)], tmp[HD:P, :], ALU.add).then_inc(sem("rope"), 1)

        sm_rope = hk

        def unit_read(u):
            kind, m, c = unit_of(u)
            src = J[u % 2][:, 0:CW]
            if kind == "ri":
                if c == CH - 1:
                    dve.wait_ge(sem("unit_act"), u + 1)
                    dve.tensor_copy(i_s[:, m, :], r_i[:, SEQ:ROWS]).then_inc(sem("s_saved"), 1)
            if kind not in SILU:
                return
            s = units_before(SILU, u)
            dve.wait_ge(sem("unit_act"), u + 1)
            if kind == "rf":
                if m and c == 0:
                    dve.wait_ge(sem("g_prod"), LEVELS * (m - 1) + 1)
                dve.tensor_scalar(r_f[:, cols(c)], th[:, s % 2, :], f_scale[:, m:m + 1], f_shift[:, m:m + 1],
                                  ALU.mult, ALU.add).then_inc(sem("th_read"), 1)
                dve.wait_ge(sem("th_read"), s + 1)
                if c == CH - 1:
                    dve.tensor_copy(f_s[:, m, :], r_f[:, SEQ:ROWS]).then_inc(sem("f_done"), 1)
                    dve.tensor_scalar(k_s[:, m, :], r_f[:, SEQ:ROWS], -1.0, 1.0, ALU.mult, ALU.add).then_inc(sem("ks_saved"), 1)
            elif kind == "rq":
                if m and c == 0:
                    dve.wait_ge(sem("diag_mm"), m)
                dve.scalar_tensor_tensor(out=r_q[:, cols(c)], in0=th[:, s % 2, :], scalar=1.0, in1=src,
                                         op0=ALU.add, op1=ALU.mult).then_inc(sem("th_read"), 1)
                if c == CH - 1:
                    dve.wait_ge(sem("th_read"), s + 1)
                    then(dve.tensor_copy(q_s[:, m, :], r_q[:, SEQ:ROWS]))
            else:
                w = CW if c < CH - 1 else CW - DECB
                dve.scalar_tensor_tensor(out=th[:, s % 2, :], in0=th[:, s % 2, :], scalar=1.0, in1=src,
                                         op0=ALU.add, op1=ALU.mult).then_inc(sem("g_gate"), 1)
                dve.wait_ge(sem("g_gate"), units_before(("rg",), u) + 1)
                dve.wait_ge(sem("o_cols"), 2 * (m + 1))
                dst = mix[:, 4 + m, CW * c:CW * c + w]
                if c == CH - 1:
                    then(dve.tensor_copy(g_s[:, m, :], th[:, s % 2, w:CW]))
                dve.tensor_tensor(dst, dst, th[:, s % 2, 0:w], ALU.mult).then_inc(sem("th_read"), 1)

        def decay(h, n):
            hs = 1 << n
            g = r_f[:, 0:SEQ] if n == 0 else g_level(n)
            gv = g.rearrange("p (b e) -> p b e", e=2)
            qv = hq[:].rearrange("p (b e s) -> p b e s", e=2, s=hs)
            kv = hk[:].rearrange("p (b e s) -> p b e s", e=2, s=hs)
            nb = SEQ // (2 * hs)
            if n:
                dve.wait_ge(sem("g_prod"), LEVELS * h + n)
            dve.tensor_tensor(qv[:, :, 1, :], qv[:, :, 1, :], bc(gv[:, :, 0].unsqueeze(2), [P, nb, hs]), ALU.mult)
            dve.tensor_tensor(kv[:, :, 0, :], kv[:, :, 0, :], bc(gv[:, :, 1].unsqueeze(2), [P, nb, hs]), ALU.mult)\
                .then_inc(sem("hq_step"), 1)

        def mix_low(c):
            for kk in range(2):
                dve.wait_ge(sem("mix_hi"), 2 * c + kk + 1)
                dve.tensor_tensor(act_lo[:, 4 * kk:4 * kk + 4, cols(c)], mix[:, 4 * kk:4 * kk + 4, cols(c)],
                                  act_hi[:, 4 * kk:4 * kk + 4, cols(c)].bitcast(F32), ALU.subtract).then_inc(sem("mix_lo"), 1)

        for tick in range(TICKS):
            for i in NORM_ROWS.get(tick // 2, ()) if tick % 2 == 0 else ():
                if 2 <= i + 1 < RT:
                    norm_rows(i + 1)
                low(i, "n_hi", "n_lo", NB)
            if tick == AT0:
                lower_bound()
            for step in rot_steps(tick):
                if step[0] == "rot":
                    rope(step[1])
            for step, i in attention_steps(tick):
                t, j, e = i // NBLK, i % NBLK, i % 2
                k0 = WIN if j == 0 else 0
                if step == "S":
                    dve.wait_ge(sem("at_s"), i + 1)
                    if i:
                        dve.wait_ge(sem("at_exp"), i)
                    for g in range(NKV):
                        ins = dve.tensor_tensor_reduce(sm[:, g, k0:], BS[:, 2 * WIN * g + k0:2 * WIN * (g + 1)], amask[:, k0:],
                                                       1.0, -3.0e38, ALU.add, ALU.max, mx[:, e, g:g + 1])
                    then(ins)
                    then(dve.scalar_tensor_tensor(out=negm[:, e, :], in0=mx[:, e, :], scalar=-SCALE, in1=nsink[:, t:t + GRP + 1:GRP],
                                                  op0=ALU.mult, op1=ALU.min))
                    dve.tensor_tensor(tsum[:, e, :], sink[:, t:t + GRP + 1:GRP], negm[:, e, :], ALU.add).then_inc(sem("at_max"), 1)
                elif step == "PT":
                    dve.wait_ge(sem("at_exp"), i + 1)
                    then(dve.tensor_tensor(den[:, e, :], den[:, e, :], esk[:, e, :], ALU.add))
                    then(dve.reciprocal(rden[:, e, :], den[:, e, :]))
                elif step == "PV":
                    dve.wait_ge(sem("at_pv"), i + 1)
                    if i:
                        dve.wait_ge(sem("at_ot"), i)
                    dve.tensor_tensor(orow[:], BO[:, 0:P].rearrange("p (g d) -> p g d", g=2),
                                      bc(rden[:, e, :].unsqueeze(2), [P, 2, HD]), ALU.mult).then_inc(sem("at_or"), 1)
            for step in recurrence_steps(tick):
                h = step[1]
                if step[0] == "prep":
                    dve.wait_ge(sem("f_done"), h + 1)
                    if h:
                        dve.wait_ge(sem("o_turned"), 2 * h)
                    dve.tensor_tensor(hq[:], r_q[:, 0:SEQ], r_f[:, 0:SEQ], ALU.mult)
                    dve.tensor_scalar(hk[:], r_f[:, 0:SEQ], -1.0, 1.0, ALU.mult, ALU.add).then_inc(sem("hq_prep"), 1)
                if step[0] == "diag":
                    dve.wait_ge(sem("diag_mm"), h + 1)
                    if h == 0:
                        dve.wait_ge(sem("stored"), 32)
                    else:
                        dve.wait_ge(sem("o_ss"), h)
                    for a in range(2):
                        ins = dve.tensor_tensor(ast[:, 4 * a:4 * a + 4, :], BL[a].rearrange("p (b t) -> p b t", b=4),
                                                bc(ident[:].unsqueeze(1), [P, 4, P]), ALU.mult)
                    ins.then_inc(sem("diag_read"), 1)
                    dve.wait_ge(sem("diag_read"), h + 1)
                if step[0] == "level":
                    n = step[2]
                    dve.wait_ge(sem("level_mm"), LEVELS * h + n + 1)
                    if n == 0 and h == 0:
                        dve.wait_ge(sem("lmask_done"), 1)
                    decay(h, n)
                    nb, hs = P // (2 << n), 1 << n
                    av = ast[:].rearrange("p c (b e s) -> p c b e s", e=2, s=hs)
                    mv = lmask[:, n, :].rearrange("p (b e s) -> p b e s", e=2, s=hs)[:, :, 1, :]
                    dve.copy_predicated(av[:, :, :, 1, :], bc(mv.unsqueeze(1), [P, NBLK, nb, hs]),
                                        BL[n % 2].rearrange("p (c b s) -> p c b s", c=NBLK, s=hs)).then_inc(sem("level_read"), 1)
                    dve.wait_ge(sem("level_read"), LEVELS * h + n + 1)
                if step[0] == "u":
                    dve.wait_ge(sem("u_mm"), h + 1)
                    dve.wait_ge(sem("g_prod"), LEVELS * (h + 1))
                    if h:
                        dve.wait_ge(sem("stp_out"), 16 * h)
                    gl = g_level(LEVELS)
                    for c in range(NBLK):
                        u_c = BL[c // 4][:, P * (c % 4):P * (c % 4) + P]
                        if c == 0:
                            ins = dve.tensor_copy(states[:, 1, :], u_c)
                        else:
                            ins = dve.scalar_tensor_tensor(out=states[:, c + 1, :], in0=states[:, c, :], scalar=gl[:, c:c + 1],
                                                           in1=u_c, op0=ALU.mult, op1=ALU.add)
                        ins.then_inc(sem("chain"), 1)
                        dve.wait_ge(sem("chain"), NBLK * h + c + 1)
                if step[0] == "o":
                    dve.wait_ge(sem("o_std"), h + 1)
                    then(dve.reciprocal(orstd[:], ostd[:]))
                    then(dve.tensor_scalar(orstd[:], orstd[:], 0.25, None, ALU.mult))
                    for a in range(2):
                        ins = dve.tensor_tensor(orn[:, 4 * P * a:4 * P * a + 4 * P].rearrange("p (b t) -> p b t", b=4),
                                                BL[a].rearrange("p (b t) -> p b t", b=4),
                                                bc(orstd[:, 4 * a:4 * a + 4].unsqueeze(2), [P, 4, P]), ALU.mult)
                    ins.then_inc(sem("o_norm"), 1)
                if step[0] in ("ota", "otb"):
                    a = step[0] == "otb"
                    dve.wait_ge(sem("o_turned"), 2 * h + a + 1)
                    dve.tensor_scalar(mix[:, 4 + h, 4 * P * a:4 * P * a + 4 * P], BR, rnorm[:, h:h + 1], None, ALU.mult)\
                        .then_inc(sem("o_cols"), 1)
            for step in sample_steps(tick):
                n = DECB * NQ
                if step[0] == "ks_t":
                    dve.wait_ge(sem("qp_zero"), 1)
                    dve.wait_ge(sem("at_out"), NITEM)
                    for g in range(NKV):
                        ins = dve.tensor_copy(qp[HD * g:HD * g + HD, :, GRP * g:GRP * g + GRP].rearrange("p b t -> p t b"),
                                              mix[HD * g:HD * g + HD, 0:GRP, SEQ:ROWS])
                    ins.then_inc(sem("qp_done"), 1)
                if step[0] == "s_turn":
                    dve.wait_ge(sem("s_turn"), 1)
                    then(dve.tensor_reduce(sst[0:n, 0:1], BP[0:n, 0:P], AX.X, ALU.max))
                    then(dve.tensor_scalar(sst[0:n, 0:1], sst[0:n, 0:1], SCALE, sinkc[:, 0:1], ALU.mult, ALU.max))
                    then(dve.tensor_scalar(sst[0:n, 1:2], sst[0:n, 0:1], -1.0, None, ALU.mult))
                    dve.tensor_tensor(sst[0:n, 2:3], sinkc[:, 0:1], sst[0:n, 1:2], ALU.add).then_inc(sem("s_max"), 1)
                    dve.wait_ge(sem("s_exp"), 1)
                    then(dve.tensor_tensor(sst[0:n, 3:4], sst[0:n, 3:4], sst[0:n, 4:5], ALU.add))
                    then(dve.reciprocal(sst[0:n, 4:5], sst[0:n, 3:4]))
                    dve.tensor_scalar(px[:], px[:], sst[0:n, 4:5], None, ALU.mult).then_inc(sem("s_prob"), 1)
                if step[0] == "s_out":
                    dve.wait_ge(sem("s_out"), 1)
                    for g in range(NKV):
                        ov = BO[HD * g:HD * g + HD, 0:n].rearrange("p (b t) -> p t b", t=NQ)
                        ins = dve.tensor_copy(mix[HD * g:HD * g + HD, 0:GRP, SEQ:ROWS], ov[:, GRP * g:GRP * g + GRP, :])
                    ins.then_inc(sem("s_mixed"), 1)
                if step[0] == "r_turn":
                    h = step[1]
                    dve.wait_ge(sem("st_in"), 16 * (h + 1))
                    dve.tensor_tensor(st[:], st[:], bc(f_s[:, h, :].unsqueeze(2), [P, DECB, P]), ALU.mult)
                    dve.wait_ge(sem("s_ki"), h + 1)
                    if h == 0:
                        dve.wait_ge(sem("stored"), 64)
                    dve.tensor_tensor(ib[:], bc(ki[:, 1, :].unsqueeze(1), [DECB, DECB, P]),
                                      bc(ident[0:DECB, 0:DECB].unsqueeze(2), [DECB, DECB, P]), ALU.mult).then_inc(sem("s_ib"), 1)
                if step[0] == "r_outer":
                    h = step[1]
                    dve.wait_ge(sem("s_outer"), h + 1)
                    for a, b in ((0, BS), (1, BO)):
                        dve.tensor_tensor(st[:, 4 * a:4 * a + 4, :], st[:, 4 * a:4 * a + 4, :], b.rearrange("p (b d) -> p b d", b=4),
                                          ALU.add).then_inc(sem("s_state"), 1)
                if step[0] == "r_o":
                    h = step[1]
                    dve.wait_ge(sem("s_o"), h + 1)
                    dve.tensor_copy(o_s[:, h, :], BP[:, 0:DECB]).then_inc(sem("s_os"), 1)
                if step[0] == "r_rows":
                    n = NREC * DECB
                    dve.wait_ge(sem("so_std"), 1)
                    then(dve.reciprocal(sst[0:n, 7:8], sst[0:n, 6:7]))
                    dve.tensor_scalar(px[0:n, :], BP[0:n, 0:P], sst[0:n, 7:8], 0.25, ALU.mult, ALU.mult).then_inc(sem("so_norm"), 1)
                if step[0] == "r_cols":
                    n = NREC * DECB
                    dve.wait_ge(sem("so_cols"), 1)
                    then(dve.tensor_tensor(o_s[:], BP[:, 0:n].rearrange("p (h b) -> p h b", h=NREC),
                                           bc(rnorm[:].unsqueeze(2), [P, NREC, DECB]), ALU.mult))
            if tick % 2:
                unit_read(tick // 2)
                c = tick // 2 - (UNITS - CH)
                if c == CH - 1:
                    dve.tensor_tensor(mix[:, 4:8, SEQ:ROWS], o_s[:], g_s[:], ALU.mult).then_inc(sem("mix_done"), 1)
                if c >= 0:
                    mix_low(c)

        def hidden(q, e, first=False):
            dve.wait_ge(sem("up_mm"), q + 1)
            dve.wait_ge(sem("gate_done"), q + 1)
            if not first:
                dve.wait_ge(sem("h_lo_done"), q - 1)
            dve.tensor_tensor(hf[:, e, :], bank[2 + e][:, 0:CW], sg[:, e, :], ALU.mult).then_inc(sem("hf_done"), 1)

        for slot in range(SLOTS):
            for step, i in row_steps(slot):
                r, w = rows_of(i)
                if step == "out":
                    dve.wait_ge(sem("p_std"), i + 1)
                    then(dve.reciprocal(rstd[0:w, 0, i:i + 1], std[0:w, 0, i:i + 1]))
                    if i == 0:
                        dve.wait_ge(sem("g_in"), 48)
                    dve.scalar_tensor_tensor(out=tr[0:w, i % 2, :].rearrange("p (a b) -> p a b", a=2), in0=pair[2][0:w, :, :],
                                             scalar=rstd[0:w, 0, i:i + 1], in1=gbl[0:w, :].rearrange("p (a b) -> p a b", a=2),
                                             op0=ALU.mult, op1=ALU.mult).then_inc(sem("p_t"), 1)
                if step == "mid":
                    dve.wait_ge(sem("q_std"), i + 1)
                    then(dve.reciprocal(rstd[0:w, 1, i:i + 1], std[0:w, 1, i:i + 1]))
                    dve.scalar_tensor_tensor(out=tr[0:w, i % 2, :], in0=x2r[0:w, i % 2, :], scalar=rstd[0:w, 1, i:i + 1],
                                             in1=gb2[0:w, :], op0=ALU.mult, op1=ALU.mult).then_inc(sem("h2_rows"), 1)
                if step == "in":
                    low(i, "h2_hi", "h2_lo", bank[6:8])
            if slot >= 24 and slot % 2:
                q = (slot - 24) // 2
                hidden(q, q % 2, q < 2)

        def last_rows(i):
            r, w = rows_of(i)
            dve.wait_ge(sem("y_std"), i + 1)
            then(dve.reciprocal(rstd[0:w, 1, i:i + 1], std[0:w, 1, i:i + 1]))
            if i == 0:
                dve.wait_ge(sem("g_in"), 64)
            dve.scalar_tensor_tensor(out=ty[0:w, i % 4, :].rearrange("p (a b) -> p a b", a=2), in0=pair[i % 2][0:w, :, :],
                                     scalar=rstd[0:w, 1, i:i + 1], in1=gbl[0:w, :].rearrange("p (a b) -> p a b", a=2),
                                     op0=ALU.mult, op1=ALU.mult).then_inc(sem("y_t"), 1)
            if i in Y_VECTOR:
                dve.wait_ge(sem("y_t"), i + 1)
                dve.wait_ge(*x2_back(i))
                dve.tensor_tensor(x2b[0:w, i, :], ty[0:w, i % 4, :], x2b[0:w, i, :], ALU.add).then_inc(sem("y_vector"), 1)

        def up(g):
            for j in range(2):
                for c in range(CH):
                    hidden(6 * g + (3 * j + c), (3 * j + c) % 2)

        def down(g, first=False, last=False):
            if not first:
                dve.wait_ge(sem("acc_done"), 24 * g)
            for c in range(CH):
                for m in range(KT):
                    v = KT * c + m
                    dve.wait_ge(sem("down_mm"), 24 * g + (v + 1))
                    src = bank[4 + v % 4][:, 0:CW]
                    if first:
                        dve.tensor_copy(mix[:, m, cols(c)], src).then_inc(sem("acc_done"), 1)
                    else:
                        dve.tensor_tensor(mix[:, m, cols(c)], mix[:, m, cols(c)], src, ALU.add).then_inc(sem("acc_done"), 1)
                    if last and (c, m - 2) in LAST_ROWS:
                        last_rows(LAST_ROWS.index((c, m - 2)))

        down(0, True)
        with dve.Fori(1, GROUPS - 1) as g:
            up(g)
            down(g)
        up(GROUPS - 1)
        down(GROUPS - 1, False, True)
        for i in range(len(LAST_ROWS), RT):
            last_rows(i)

    block.__exit__(None, None, None)


_OUTS = [("y_prompt", (1, SEQ, DM)), ("y_sample", (DECB, 1, DM)), ("k_p", (1, 1, WIN, NKV, HD)), ("v_p", (1, 1, WIN, NKV, HD)),
         ("st_p", (1, 1, NREC, RD, RD)), ("k_s", (1, DECB, WIN, NKV, HD)), ("v_s", (1, DECB, WIN, NKV, HD)),
         ("st_s", (1, DECB, NREC, RD, RD))]


def kernel(**inputs):
    import concourse.bacc as bacc
    from concourse.bass_utils import run_bass_kernel_spmd

    nc = bacc.Bacc("TRN2", target_bir_lowering=False, num_devices=1)
    arrays = {name: np.ascontiguousarray(a) for name, a in inputs.items()}
    arrays.update(shape_constants())
    t_in = {name: nc.dram_tensor(f"{name}_dram", a.shape, mybir.dt.from_np(a.dtype), kind="ExternalInput").ap()
            for name, a in arrays.items()}
    t_out = {name: nc.dram_tensor(f"{name}_out", shape, F32, kind="ExternalOutput").ap() for name, shape in _OUTS}
    build(nc, t_in, t_out)
    r = run_bass_kernel_spmd(nc, [{f"{name}_dram": a for name, a in arrays.items()}], core_ids=[0])
    return tuple(r.results[0][f"{name}_out"] for name, _ in _OUTS)
```

```python
import math

import numpy as np

import concourse.bass as bass
from concourse import mybir

F32 = mybir.dt.float32
F32R = mybir.dt.float32r
U8 = mybir.dt.uint8
ALU = mybir.AluOpType
ACT = mybir.ActivationFunctionType
AX = mybir.AxisListType

P = 128
DM = 1024
SEQ, DECB = 1024, 8
ROWS = SEQ + DECB
KT = DM // P
HD, NQ, NKV = 64, 8, 2
GRP = NQ // NKV
WIN = 128
NREC, RD = 4, 128
DFF = 2816
FT = DFF // P
CH = 3
CW = ROWS // CH
NBLK = SEQ // P
RT = NBLK + 1
LEVELS = 7
PAST = 2048
ROT = HD // 4
ROT_MASK = list(range(ROT // 2, ROT)) + list(range(ROT // 2)) + list(range(ROT, 32))
THETA = 500000.0
EPS = 1e-6
SCALE = HD ** -0.5
NEG = -1.0e30

CQ, CK, CV = 0, NQ * HD, NQ * HD + NKV * HD
CRQ = CV + NKV * HD
CRF, CRI, CRG = CRQ + NREC * RD, CRQ + 2 * NREC * RD, CRQ + 3 * NREC * RD

TILES = [("k", 0), ("v", 0)] + [("q", t) for t in range(4)]
for _h in range(NREC):
    TILES += [("rq", _h), ("ri", _h), ("rf", _h)]
TILES += [("rg", h) for h in range(NREC)]
NIN = len(TILES)
NOUT = DM // P
N12 = NIN + NOUT
LEAD = 4
BACK = tuple(reversed(range(CH)))
ORDER = ([(n, c) for c in range(CH) for n in range(LEAD)]
         + [(n, c) for n in range(LEAD, NIN) for c in (BACK if n == NIN - 1 else range(CH))])
UNITS = NIN * CH
LAST_UNIT = [max(u for u, (m, _) in enumerate(ORDER) if m == n) for n in range(NIN)]
NORM_ROWS = {0: (0, 1, 2), 1: (3,), 2: (4,), 3: (5,), 4: (6,), 5: (7,), 6: (8,)}
TICKS = 2 * UNITS
AT0 = 16
NITEM = 4 * NBLK
HG0, HGS = 55, 18
SA0 = 88
SR0, SRS = 99, 6
SLOTS = 24 + 12
ROW_OUT = (9, 11, 13, 17, 19, 21, 24, 26, 28)
ROW_IN = (12, 14, 16, 20, 22, 24, 27, 29, 31)
DOWN_SLOTS = (33, 34)
CHUNKS = tuple((CW * c, CW) for c in range(CH))
LAST_CHUNKS = ((0, CW), (CW, CW), (2 * CW, 7 * P - 2 * CW), (7 * P, ROWS - 7 * P))
LAST_ROWS = [9, 11, 17, 19, 22, 25, 29]
X2_VECTOR = (6, 8)
Y_VECTOR = (8,)
GROUPS = FT // 2


def rows_of(i):
    return (P * i, P if i < NBLK else DECB)


def back_row(i):
    return RT - 1 - i


def shape_constants():
    ident = np.eye(P, dtype=np.float32)
    half = ROT // 2
    q = WIN + np.arange(WIN)[:, None]
    k = np.arange(2 * WIN)[None, :]
    band = (k <= q) & (q - k < WIN)
    amask = np.where(band, 0.0, NEG).astype(np.float32)
    s, t = np.arange(P)[:, None], np.arange(P)[None, :]
    lmask = np.stack([(s // (2 * h) == t // (2 * h)) & (s // h % 2 == 0) & (t // h % 2 == 1)
                      for h in (2 ** n for n in range(LEVELS))], axis=1).astype(np.float32)
    pos = np.concatenate([np.arange(SEQ), np.full(DECB, PAST)]).astype(np.float32)
    inv = np.exp(-np.log(np.float32(THETA)) * np.arange(half, dtype=np.float32) * np.float32(2.0 / ROT))
    ang = (pos[None, :] * inv.astype(np.float32)[:, None]).astype(np.float32)
    cos, sin = np.ones((P, ROWS), np.float32), np.zeros((P, ROWS), np.float32)
    for b in range(0, P, HD):
        for d in range(ROT):
            cos[b + d], sin[b + d] = np.cos(ang[d % half]), np.sin(ang[d % half]) * (-1 if d < half else 1)
    return {"c_ident": ident, "c_amask": amask, "c_lmask": lmask, "c_cos": cos, "c_sin": sin}


def build(nc, t_in, t_out):
    base = (nc.sbuf_base + 31) // 32 * 32
    end = nc.sbuf_top // 32 * 32

    def at(name, shape, dt, offset):
        size = math.prod(shape[1:]) * (1 if dt == U8 else 4)
        assert offset + size <= end, (name, offset + size - end)
        return nc.alloc_sbuf_tensor_at(name, shape, dt, offset=offset), (offset + size + 31) // 32 * 32

    o = base
    act_hi, o = at("act_hi", [P, KT, ROWS], F32R, o)
    act_lo, o = at("act_lo", [P, KT, ROWS], F32R, o)
    at_mix = o
    mix, o = at("mix", [P, KT, ROWS], F32, o)
    w_hi, o = at("w_hi", [P, 4, KT, P], F32R, o)
    w_lo, o = at("w_lo", [P, 4, KT, P], F32R, o)
    raw, o = at("raw", [P, 2, KT, P], F32, o)
    ident, o = at("ident", [P, P], F32, o)
    small_from = o

    def small(name, shape):
        nonlocal o
        x, o = at(name, shape, F32, o)
        return x

    eps = small("eps", [P, 1])
    ss = small("ss", [P, 2, RT])
    std = small("std", [P, 2, RT])
    rstd = small("rstd", [P, 2, RT])
    lbl = small("lbl", [P, 2, NREC])
    lbt = small("lbt", [P, 8, NREC])
    rnorm = small("rnorm", [P, NREC])
    sink = small("sink", [P, NQ])
    nsink = small("nsink", [P, NQ])
    mx = small("mx", [P, 2, 2])
    negm = small("negm", [P, 2, 2])
    tsum = small("tsum", [P, 2, 2])
    esk = small("esk", [P, 2, 2])
    den = small("den", [P, 2, 2])
    rden = small("rden", [P, 2, 2])
    oss = small("oss", [P, NBLK])
    ostd = small("ostd", [P, NBLK])
    orstd = small("orstd", [P, NBLK])
    q_s = small("q_s", [P, NREC, DECB])
    f_s = small("f_s", [P, NREC, DECB])
    i_s = small("i_s", [P, NREC, DECB])
    k_s = small("k_s", [P, NREC, DECB])
    g_s = small("g_s", [P, NREC, DECB])
    o_s = small("o_s", [P, NREC, DECB])
    kn_s = small("kn_s", [DECB, P])
    qp = small("qp", [P, DECB, NQ])
    stx = small("stx", [P, DECB * NQ])
    ptx = small("ptx", [P, DECB * NQ])
    sinkc = small("sinkc", [DECB * NQ, 1])
    sst = small("sst", [P, 8])
    assert o - small_from <= 4096, o - small_from
    region = small_from + 4096

    o = region
    k_hi, o = at("k_hi", [P, NKV, ROWS], F32R, o)
    vrow, o = at("vrow", [P, RT, P], F32, o)
    r_i, o = at("r_i", [P, ROWS], F32, o)
    at_rq = o
    r_q, o = at("r_q", [P, ROWS], F32, o)
    r_f, o = at("r_f", [P, ROWS], F32, o)
    th, o = at("th", [P, 2, CW], F32, o)
    at_att = o
    at_sm = o
    sm, o = at("sm", [P, 2, 2 * WIN], F32, o)
    prob, o = at("prob", [P, 2, 2, 2 * WIN], F32, o)
    pt, o = at("pt", [P, 4, P], F32, o)
    orow, o = at("orow", [P, 2, HD], F32, o)
    at_amask = o
    amask, o = at("amask", [P, 2 * WIN], F32, o)
    lmask, o = at("lmask", [P, LEVELS, P], U8, o)
    at_hq = o
    hq, o = at("hq", [P, SEQ], F32, o)
    hk, o = at("hk", [P, SEQ], F32, o)
    hg, o = at("hg", [P, 1016], F32, o)
    ast, o = at("ast", [P, NBLK, P], F32, o)
    irow, o = at("irow", [P, NBLK, P], F32, o)
    at_krow = o
    krow, o = at("krow", [P, NBLK, P], F32, o)
    states, o = at("states", [P, NBLK + 1, P], F32, o)
    cos, oo = at("cos", [P, ROWS], F32, at_krow)
    sin, oo = at("sin", [P, ROWS], F32, oo)
    kwin, _ = at("kwin", [P, P], F32, at_krow - 2 * 4096)
    lmask32, _ = at("lmask32", [P, LEVELS, P], F32, at_krow - 4096)
    kraw = r_f
    vt = r_i
    k_lo, _ = at("k_lo", [P, NKV, ROWS], F32R, at_mix + 6 * 4 * ROWS)
    q_hi, oo = at("q_hi", [P, 2, P], F32R, at_mix + 5 * 4 * ROWS)
    q_lo, _ = at("q_lo", [P, 2, P], F32R, oo)
    xr0, oo = at("xr0", [P, 2, DM], F32, at_mix + 4 * 4 * ROWS)
    assert oo <= at_mix + 6 * 4 * ROWS
    hr0, oo = at("hr0", [P, 2, DM], F32, at_sm)
    assert oo <= at_amask
    xr0b, _ = at("xr0b", [P, DM], F32, at_rq)
    hr0b, _ = at("hr0b", [P, DM], F32, at_krow - 2 * 4096)

    def xr_first(i):
        w = rows_of(i)[1]
        return xr0b[0:w, :] if i % 3 == 2 else xr0[0:w, i % 3, :]

    def hr_first(i):
        w = rows_of(i)[1]
        return hr0b[0:w, :] if i % 3 == 2 else hr0[0:w, i % 3, :]

    gb0, _ = at("gb0", [P, DM], F32, at_hq)
    ks, oo = at("ks", [P, DECB, P], F32, at_att)
    vs, oo = at("vs", [P, DECB, P], F32, oo)
    px, oo = at("px", [DECB * NQ, P], F32, oo)
    ki, oo = at("ki", [DECB, 2, P], F32, oo)
    kst, oo = at("kst", [P, DECB, P], F32, region)
    st, oo = at("st", [P, DECB, P], F32, oo)
    ib, _ = at("ib", [DECB, DECB, P], F32, region + 8256)
    orn = hk
    o = region
    h_hi, o = at("h_hi", [P, 2, ROWS], F32R, o)
    h_lo, o = at("h_lo", [P, 2, ROWS], F32R, o)
    sg, o = at("sg", [P, 2, CW], F32, o)
    hf, o = at("hf", [P, 2, CW], F32, o)
    free = o
    o = end - 6 * 4096
    d_hi, o = at("d_hi", [P, 2, DM], F32R, o)
    d_lo, o = at("d_lo", [P, 2, DM], F32R, o)
    draw, o = at("draw", [P, 2, DM], F32, o)
    o = free
    xr, o = at("xr", [P, 2, DM], F32, o)
    tr, o = at("tr", [P, 2, DM], F32, o)
    gbl, o = at("gbl", [P, DM], F32, o)
    assert o <= end - 6 * 4096
    gb2, o = at("gb2", [P, DM], F32, end - 6 * 4096)
    x2r, o = at("x2r", [P, 2, DM], F32, o)
    assert o <= end - 2 * 4096

    x2b, _ = at("x2b", [P, RT, DM], F32, base)
    ty, oo = at("ty", [P, 4, DM], F32, free)
    assert oo <= end - 6 * 4096

    wx_hi = [at(f"wx_hi{i}", [P, KT, P], F32R, region + 4096 * i)[0] for i in range(4)]
    wx_lo = [at(f"wx_lo{i}", [P, KT, P], F32R, region + 4 * 4096 if i == 0 else end - 4096 * (4 - i))[0] for i in range(4)]

    def w_tiles(n):
        if NIN + 2 <= n < NIN + 6:
            return wx_hi[n - NIN - 2][:], wx_lo[n - NIN - 2][:]
        return w_hi[:, n % 4], w_lo[:, n % 4]

    x2d = nc.dram_tensor("x2_scratch", (ROWS, DM), F32).ap()

    pair = [nc.alloc_psum_tensor(f"pair{i}", [P, 2, 512], F32) for i in range(4)]
    bank = [pair[i // 2][:, i % 2, :] for i in range(8)]
    J = [bank[0], bank[1]]
    BS, BP, BO, BR = bank[2], bank[3], bank[4], bank[5]
    BL = [bank[6], bank[7]]
    NB = [bank[2], bank[3], bank[6], bank[7]]

    sems = {}

    def sem(name):
        if name not in sems:
            sems[name] = nc.alloc_semaphore(name)
        return sems[name]

    xp = t_in["x_prompt"].rearrange("b s d -> (b s) d")
    xs = t_in["x_sample"].rearrange("b s d -> (b s) d")
    w_in = t_in["w_in"][0]
    w_out = t_in["w_out"][0]
    yp = t_out["y_prompt"].rearrange("b s d -> (b s) d")
    ys = t_out["y_sample"].rearrange("b s d -> (b s) d")

    def x_rows(i):
        return xp[P * i:P * i + P, :] if i < NBLK else xs

    def y_rows(i):
        return yp[P * i:P * i + P, :] if i < NBLK else ys

    def gain(name):
        return t_in[name].partition_broadcast(P).rearrange("p o d -> p (o d)")

    def cols(c):
        return slice(CW * c, CW * c + CW)

    def bc(ap, shape):
        return ap.broadcast_to(shape)

    def g_level(n):
        off = sum(SEQ >> m for m in range(1, n))
        return hg[:, off:off + (SEQ >> n)]

    def weight_parts(n):
        dst = raw[:, n % 2]
        if n < NIN:
            kind, m = TILES[n]
            if kind == "q":
                return [(dst[:, :, HD * g:HD * g + HD],
                         w_in[:, CQ + HD * (m + GRP * g):CQ + HD * (m + GRP * g) + HD].rearrange("(k p) n -> p k n", p=P))
                        for g in range(NKV)]
            c = {"k": CK, "v": CV, "rq": CRQ, "rf": CRF, "ri": CRI, "rg": CRG}[kind] + P * m
            return [(dst, w_in[:, c:c + P].rearrange("(k p) n -> p k n", p=P))]
        c = P * (n - NIN)
        part = [(dst[HD * g:HD * g + HD, 0:4, :],
                 w_out[HD * GRP * g:HD * GRP * (g + 1), c:c + P].rearrange("(t p) n -> p t n", p=HD)) for g in range(NKV)]
        return part + [(dst[:, 4:8, :], w_out[4 * P:8 * P, c:c + P].rearrange("(k p) n -> p k n", p=P))]

    raw_count = []
    slot_total = [0, 0]
    for n in range(N12):
        slot_total[n % 2] += 16 * len(weight_parts(n))
        raw_count.append(slot_total[n % 2])
    for n in range(N12, N12 + 4):
        raw_count.append(slot_total[n % 2] + 16 * ((n - N12) // 2 + 1))

    def unit_of(u):
        n, c = ORDER[u]
        return TILES[n] + (c,)

    def units_before(kinds, u):
        return sum(unit_of(v)[0] in kinds for v in range(min(u, UNITS)))

    def unit_index(kind, m, c):
        return ORDER.index((TILES.index((kind, m)), c))

    def split_at(tick):
        out = [n for n, t in ((4, 19), (5, 21), (NIN, 118), (NIN + 1, 121), (NIN + 2, 124), (NIN + 3, 126), (NIN + 4, 128),
                              (NIN + 5, 130)) if t == tick]
        if tick % 6 == 1 and 6 <= tick // 6 + 2 < NIN:
            out.append(tick // 6 + 2)
        return sorted(out)

    def row_steps(slot):
        return ([("in", i) for i in range(RT) if ROW_IN[i] == slot] + [("mid", i) for i in range(RT) if ROW_OUT[i] + 1 == slot]
                + [("out", i) for i in range(RT) if ROW_OUT[i] == slot])

    def slot_tiles(slot):
        return [NIN + 6 + k for k, v in enumerate((1, 3, 19, 20, 23, 24)) if v == slot]

    def chunk_of_rows(c):
        return -(-CW * (c + 1) // P)

    SILU = ("rq", "rg", "rf")
    ROPE = ("k", "q")
    WIN_LOADS = 2 * (1 + DECB) * 16
    NCONST = 5 * 16 + DECB * 16 + 16

    def attention_steps(tick):
        d = tick - AT0
        out = []
        if d % 2 == 0:
            for step, i in (("PT", d // 2 - 1), ("OT", d // 2 - 2), ("S", d // 2)):
                if 0 <= i < NITEM:
                    out.append((step, i))
        else:
            for step, i in (("PV", (d - 3) // 2), ("Q", (d + 1) // 2)):
                if 0 <= i < NITEM:
                    out.append((step, i))
        return out

    def recurrence_steps(tick):
        out = []
        for h in range(NREC):
            d = tick - (HG0 + HGS * h)
            if d in (-4, -1):
                out.append(("it" + "ab"[d == -1], h))
            if d == -1:
                out.append(("prep", h))
            if d == 0:
                out.append(("diag", h))
            if 1 <= d <= LEVELS:
                out.append(("level", h, d - 1))
            out += [(s, h) for s, v in (("kta", 9), ("ktb", 10), ("u", 11), ("o", 13), ("ot", 16)) if d == v]
        return out

    ROPE_UNITS = [u for u in range(UNITS) if unit_of(u)[0] in ROPE]

    def rot_steps(tick):
        out = []
        if tick % 2 == 1 and (tick - 3) // 2 in ROPE_UNITS and tick >= 3:
            out.append(("rot", ROPE_UNITS.index((tick - 3) // 2)))
        out += [("vt", n) for n, t in enumerate((12, 22, 24)) if t == tick]
        for c in range(CH):
            done = 2 * unit_index("k", 0, c) + 3
            out += [("k_high", c)] * (tick == done + 1) + [("k_low", c)] * (tick == done + 2)
        if tick == 26:
            out.append(("kw", 0))
        return out

    def sample_steps(tick):
        out = []
        d = tick - SA0
        out += [(s,) for s, v in (("ks_t", 0), ("s_score", 2), ("s_turn", 4), ("s_back", 6), ("s_out", 7)) if d == v]
        for h in range(NREC):
            d = tick - (SR0 + SRS * h)
            out += [(s, h) for s, v in (("r_turn", 0), ("r_outer", 2), ("r_o", 4)) if d == v]
        d = tick - (SR0 + SRS * NREC)
        out += [(s,) for s, v in (("r_rows", 0), ("r_cols", 2)) if d == v]
        return out

    def y_added(i):
        by_vector = i in Y_VECTOR
        return sem("y_vector" if by_vector else "y_pool"), sum((k in Y_VECTOR) == by_vector for k in range(i + 1))

    def x2_back(i):
        return (sem("x2_back0"), 16) if i < 4 else (sem("x2_back1"), 32)

    def add_x(eng, i):
        w = rows_of(back_row(i))[1]
        eng.wait_ge(sem("p_t"), i + 1)
        eng.wait_ge(sem(f"x_in{i % 2}"), 16 * (i // 2 + 1))
        if i >= 2:
            eng.wait_ge(sem(f"x2_out{i % 2}"), 16 * (i // 2))
            eng.wait_ge(sem("h2_rows"), i - 1)
        eng.tensor_tensor(x2r[0:w, i % 2, :], tr[0:w, i % 2, :], xr[0:w, i % 2, :], ALU.add).then_inc(sem("x2"), 1)

    V_GROUPS = [(0, 4), (4, 4), (8, 1)]

    block = nc.Block()
    blk = block.__enter__()

    @blk.sync
    def _(sp):
        def load_x(i):
            if i >= 3:
                sp.wait_ge(sem("h_rows"), i - 2)
            sp.dma_start(xr_first(i), x_rows(i)).then_inc(sem(f"x0_in{i % 3}"), 16)

        def load_weight(n):
            if n >= 2:
                sp.wait_ge(sem("w_split"), n - 1)
            for dst, src in weight_parts(n):
                sp.dma_start(dst, src).then_inc(sem(f"raw_in{n % 2}"), 16)

        load_x(0)
        sp.dma_start(gb0[:], gain("norm_pre_mix")).then_inc(sem("g_in"), 16)
        sp.dma_start(ident[:], t_in["c_ident"]).then_inc(sem("id_in"), 16)
        load_x(1)
        load_x(2)
        load_weight(0)
        load_x(3)
        load_weight(1)
        load_x(4)
        for dst, src in ((cos[:], t_in["c_cos"]), (sin[:], t_in["c_sin"])):
            sp.dma_start(dst, src).then_inc(sem("rot_in"), 16)
        load_weight(2)
        load_x(5)
        load_weight(3)
        for dst, src in ((amask[:], t_in["c_amask"]), (lmask32[:], t_in["c_lmask"]),
                         (sink[:], t_in["attn_sinks"].partition_broadcast(P).rearrange("p o h -> p (o h)"))):
            sp.dma_start(dst, src).then_inc(sem("const_in"), 16)
        for l in range(2):
            sp.dma_start(lbl[:, l, :], t_in["rec_lb"][l].rearrange("(h p) -> p h", p=P), allow_slow_non_contiguous=True).then_inc(sem("const_in"), 16)
        sp.dma_start(rnorm[:], t_in["rec_out_norm"][0].rearrange("h v -> v h"), allow_slow_non_contiguous=True).then_inc(sem("const_in"), 16)
        for b in range(DECB):
            sp.dma_start(sinkc[NQ * b:NQ * b + NQ, :], t_in["attn_sinks"].rearrange("o h -> h o"), allow_slow_non_contiguous=True).then_inc(sem("const_in"), 16)
        for i in range(6, RT):
            load_x(i)
        stores = 0
        for tick in range(TICKS):
            for n in split_at(tick):
                load_weight(n)
            if tick == 28:
                sp.wait_ge(sem("kw_out"), 1)
                sp.dma_start(t_out["k_p"].rearrange("o b w n d -> (o b w) (n d)"), kwin[:]).then_inc(sem("stored"), 16)
            if tick == 30:
                sp.wait_ge(sem("v_rows"), 3)
                sp.dma_start(t_out["v_p"].rearrange("o b w n d -> (o b w) (n d)"), vrow[:, NBLK - 1, :]).then_inc(sem("stored"), 16)
            if tick == AT0 + 2 * NITEM + 5:
                sp.wait_ge(sem("at_out"), NITEM)
                sp.wait_ge(sem("kw_out"), 1)
                for dst, cache, new in ((ks, "cache_k_win", kn_s), (vs, "cache_v_win", vrow[:, NBLK, :])):
                    sp.dma_start(dst[0:P - 1, :, :], t_in[cache][0, :, 1:WIN].rearrange("b w n d -> w b (n d)"))\
                      .then_inc(sem("win_in"), 16)
                    for b in range(DECB):
                        sp.dma_start(dst[P - 1:P, b, :], new[b:b + 1, :]).then_inc(sem("win_in"), 16)
            if tick == SA0:
                sp.wait_ge(sem("win_in"), WIN_LOADS)
                for src, dst in ((ks, "k_s"), (vs, "v_s")):
                    sp.dma_start(t_out[dst][0].rearrange("b w n d -> w b (n d)"), src[:]).then_inc(sem("stored"), 16)
            for step in sample_steps(tick + 1):
                if step[0] == "r_turn":
                    h = step[1]
                    if h:
                        sp.wait_ge(sem("s_o"), h)
                        sp.wait_ge(sem("st_out"), 16 * h)
                    else:
                        sp.wait_ge(sem("at_out"), NITEM)
                    sp.dma_start(st[:], t_in["state_hgrn"][0, :, h].rearrange("b k v -> k b v")).then_inc(sem("st_in"), 16)
            for step in sample_steps(tick):
                if step[0] == "r_o":
                    h = step[1]
                    sp.wait_ge(sem("s_state"), 2 * h + 2)
                    sp.dma_start(t_out["st_s"][0, :, h].rearrange("b k v -> k b v"), st[:]).then_inc(sem("st_out"), 16)
            for step in recurrence_steps(tick):
                if step[0] == "o":
                    sp.wait_ge(sem("chain"), NBLK * (step[1] + 1))
                    sp.dma_start(t_out["st_p"][0, 0, step[1]], states[:, NBLK, :]).then_inc(sem("stp_out"), 16)
        for n in range(NIN + 6, N12):
            load_weight(n)
        sp.wait_ge(sem("stored"), 64)
        sp.wait_ge(sem("st_out"), 16 * NREC)
        sp.wait_ge(sem("stp_out"), 16 * NREC)
        sp.wait_ge(sem("mix_done"), 1)
        sp.wait_ge(sem("th_read"), units_before(SILU, UNITS))
        sp.dma_start(gbl[:], gain("norm_post_mix")).then_inc(sem("g_in"), 16)
        sp.dma_start(gb2[:], gain("norm_pre_ffn")).then_inc(sem("g_in"), 16)

        def ffn_raw(g, j, k):
            w = t_in["w_gate" if k == 0 else "w_up"][0]
            n = N12 + 4 * g + 2 * j + k
            sp.wait_ge(sem("w_split"), n - 1)
            sp.dma_start(raw[:, k], w[:, bass.ds(2 * P * g + P * j, P)].rearrange("(k p) n -> p k n", p=P))\
              .then_inc(sem(f"raw_in{k}"), 16)

        def load_row(i, buf, src, free_sem, free_val):
            if free_val > 0:
                sp.wait_ge(sem(free_sem), free_val)
            w = rows_of(back_row(i))[1]
            sp.dma_start(buf[0:w, i % 2, :], src).then_inc(sem(f"x_in{i % 2}"), 16)

        def ffn_down(g):
            for j in range(2):
                if not isinstance(g, int) or g > 0:
                    sp.wait_ge(sem("d_split"), 2 * g + j - 1)
                sp.dma_start(draw[:, j, :], t_in["w_down"][0, bass.ds(2 * P * g + P * j, P), :]).then_inc(sem(f"draw_in{j}"), 16)

        load_row(0, xr, x_rows(back_row(0)), "", 0)
        load_row(1, xr, x_rows(back_row(1)), "", 0)
        for k in range(2):
            ffn_raw(0, 0, k)
        for i in range(RT):
            if i == 4:
                for k in range(2):
                    ffn_raw(0, 1, k)
            if i == 6:
                sp.wait_ge(sem("unit"), UNITS + CH * NOUT)
                ffn_down(0)
            if i + 2 < RT:
                load_row(i + 2, xr, x_rows(back_row(i + 2)), "x2", i + 1)
            sp.wait_ge(sem("x2"), i + 1)
            r, w = rows_of(back_row(i))
            sp.dma_start(x2d[r:r + w, :], x2r[0:w, i % 2, :]).then_inc(sem(f"x2_out{i % 2}"), 16)
        sp.wait_ge(sem("x2_out0"), 16 * 5)
        sp.wait_ge(sem("x2_out1"), 16 * 4)

        def next_raw(g):
            for j in range(2):
                for k in range(2):
                    ffn_raw(g + 1, j, k)

        next_raw(0)
        with sp.Fori(1, GROUPS - 1) as g:
            ffn_down(g)
            next_raw(g)
        ffn_down(GROUPS - 1)
        sp.dma_start(gbl[:], gain("norm_post_ffn")).then_inc(sem("g_in"), 16)
        sp.wait_ge(sem("up_mm"), 6 * GROUPS)
        for a in range(2):
            sp.dma_start(x2b[:, 4 * a:4 * a + 4, :], x2d[4 * P * a:4 * P * a + 4 * P, :].rearrange("(i p) d -> p i d", p=P))\
              .then_inc(sem(f"x2_back{a}"), 16)
        sp.dma_start(x2b[0:DECB, NBLK, :], x2d[SEQ:ROWS, :]).then_inc(sem("x2_back1"), 16)
        for i in range(RT):
            sp.wait_ge(*y_added(i))
            sp.dma_start(y_rows(i), x2b[0:rows_of(i)[1], i, :]).then_inc(sem("y_out"), 16)
        sp.wait_ge(sem("y_out"), 16 * RT)

    @blk.gpsimd
    def _(pool):
        def weight_lo(n, slot=None):
            hi, lo = w_tiles(n) if slot is None else (w_hi[:, slot], w_lo[:, slot])
            pool.wait_ge(sem("w_hi_done"), n + 1)
            pool.tensor_tensor(lo, raw[:, (n if slot is None else slot) % 2], hi.bitcast(F32), ALU.subtract)\
                .then_inc(sem("w_split"), 1)

        pool.memset(k_hi[:].bitcast(F32), 0.0)
        pool.memset(k_lo[:].bitcast(F32), 0.0).then_inc(sem("k_zero"), 1)
        pool.memset(qp[:], 0.0).then_inc(sem("qp_zero"), 1)
        for n in range(LEAD):
            weight_lo(n)
        pool.wait_ge(sem("const_in"), NCONST)
        pool.tensor_copy(lmask[:], lmask32[:]).then_inc(sem("lmask_done"), 1)
        for tick in range(TICKS):
            for step in recurrence_steps(tick):
                if step[0] == "prep":
                    h = step[1]
                    pool.wait_ge(sem("f_done"), h + 1)
                    if h:
                        pool.wait_ge(sem("chain"), NBLK * h)
                    for n in range(1, LEVELS + 1):
                        src = r_f[:, 0:SEQ] if n == 1 else g_level(n - 1)
                        if n > 1:
                            pool.wait_ge(sem("g_prod"), LEVELS * h + n - 1)
                        v = src.rearrange("p (b e) -> p b e", e=2)
                        pool.tensor_tensor(g_level(n), v[:, :, 0], v[:, :, 1], ALU.mult).then_inc(sem("g_prod"), 1)
            for step in sample_steps(tick):
                if step[0] == "r_turn":
                    h = step[1]
                    pool.wait_ge(sem("st_in"), 16 * (h + 1))
                    pool.wait_ge(sem("f_done"), h + 1)
                    pool.tensor_tensor(st[:], st[:], bc(f_s[:, h, :].unsqueeze(2), [P, DECB, P]), ALU.mult).then_inc(sem("st_scaled"), 1)
            for n in split_at(tick):
                weight_lo(n)

        def hidden_lo(q, j, c, e):
            pool.wait_ge(sem("h_hi_done"), q + 1)
            pool.tensor_tensor(h_lo[:, j, cols(c)], hf[:, e, :], h_hi[:, j, cols(c)].bitcast(F32), ALU.subtract)\
                .then_inc(sem("h_lo_done"), 1)

        def down_lo_tile(g, j):
            pool.wait_ge(sem("d_hi_done"), 2 * g + j + 1)
            pool.tensor_tensor(d_lo[:, j, :], draw[:, j, :], d_hi[:, j, :].bitcast(F32), ALU.subtract)\
                .then_inc(sem("d_split"), 1)

        for slot in range(SLOTS):
            for step, i in row_steps(slot):
                if step == "out" and i not in X2_VECTOR:
                    add_x(pool, i)
            for n in slot_tiles(slot):
                weight_lo(n)
            if slot >= 24 and slot % 2:
                q = (slot - 24) // 2
                hidden_lo(q, q % 2, BACK[q // 2], q % 2)
            if slot in DOWN_SLOTS:
                down_lo_tile(0, DOWN_SLOTS.index(slot))

        def down_lo(g):
            for j in range(2):
                down_lo_tile(g, j)

        def next_lo(g, j):
            for k in range(2):
                weight_lo(4 * g + (N12 + 4 + 2 * j + k), (N12 + 2 * j + k) % 4)

        def ffn(g, more):
            down_lo(g)
            for j in range(2):
                for c in range(CH):
                    hidden_lo(6 * g + (3 * j + c), j, c, (3 * j + c) % 2)
                if more:
                    next_lo(g, j)

        next_lo(0, 0)
        next_lo(0, 1)
        with pool.Fori(1, GROUPS - 1) as g:
            ffn(g, True)
        ffn(GROUPS - 1, False)
        for i in range(RT):
            if i not in Y_VECTOR:
                r, w = rows_of(i)
                pool.wait_ge(sem("y_t"), i + 1)
                pool.wait_ge(*x2_back(i))
                pool.tensor_tensor(x2b[0:w, i, :], ty[0:w, i % 4, :], x2b[0:w, i, :], ALU.add).then_inc(sem("y_pool"), 1)

    @blk.scalar
    def _(act):
        def copy(out, in_):
            return act.activation(out, in_, ACT.Copy)

        def weight_hi(n, slot=None, count=None, used=None):
            hi = w_tiles(n)[0] if slot is None else w_hi[:, slot]
            part = (n if slot is None else slot) % 2
            act.wait_ge(sem(f"raw_in{part}"), raw_count[n] if count is None else count)
            if used is not None:
                act.wait_ge(sem(used[0]), used[1])
            elif NIN + 2 <= n < NIN + 6:
                act.wait_ge(sem("o_mm"), NREC)
                act.wait_ge(sem("s_os"), NREC)
                act.wait_ge(sem("st_out"), 16 * NREC)
                act.wait_ge(sem("stp_out"), 16 * NREC)
            elif n >= N12:
                act.wait_ge(sem("unit"), UNITS + 2 * NOUT + (0, 1, 6, 7)[n - N12] + 1)
            elif n >= NIN + 6:
                act.wait_ge(sem("unit"), LAST_UNIT[n - 8] + 1)
            elif n >= 4:
                act.wait_ge(sem("unit"), LAST_UNIT[n - 4] + 1)
            copy(hi, raw[:, part]).then_inc(sem("w_hi_done"), 1)

        def root(out, in_, scale, done, value):
            act.wait_ge(sem(done), value)
            return act.activation(out, in_, ACT.Sqrt, bias=eps[0:out.shape[0], :], scale=scale)

        def squares(i):
            r, w = rows_of(i)
            act.wait_ge(sem(f"x0_in{i % 3}"), 16 * (i // 3 + 1))
            if i >= 3:
                act.wait_ge(sem("n_tr"), 2 * (i - 2))
            act.activation(hr_first(i), xr_first(i), ACT.Square, accum_out=ss[0:w, 0, i:i + 1]).then_inc(sem("n_ss"), 1)
            root(std[0:w, 0, i:i + 1], ss[0:w, 0, i:i + 1], 1.0 / DM, "n_ss", i + 1).then_inc(sem("n_std"), 1)

        def high(i, tr_sem, hi_sem, banks, tile=None):
            r, w = rows_of(i if tile is None else tile)
            for kk in range(2):
                q = 2 * i + kk
                act.wait_ge(sem(tr_sem), q + 1)
                copy(act_hi[:, 4 * kk:4 * kk + 4, r:r + w],
                     banks[q % len(banks)].rearrange("p (k r) -> p k r", k=4)[:, :, 0:w]).then_inc(sem(hi_sem), 1)

        act.wait_ge(sem("eps_set"), 1)
        act.activation(ostd[:, 0:1], eps[:], ACT.Sqrt)
        squares(0)
        squares(1)

        def unit_read(u):
            kind, m, c = unit_of(u)
            act.wait_ge(sem("unit"), u + 1)
            src = J[u % 2][:, 0:CW]
            if kind == "k":
                copy(kraw[:, cols(c)], src).then_inc(sem("unit_act"), 1)
            elif kind == "v":
                copy(vt[:, cols(c)], src).then_inc(sem("unit_act"), 1)
            elif kind == "q":
                copy(mix[:, m, cols(c)], src).then_inc(sem("unit_act"), 1)
            elif kind == "ri":
                if m:
                    act.wait_ge(sem("i_turned"), 2 * m)
                    act.wait_ge(sem("s_saved"), m)
                else:
                    act.wait_ge(sem("v_turned"), 3)
                copy(r_i[:, cols(c)], src).then_inc(sem("unit_act"), 1)
            else:
                s = units_before(SILU, u)
                if s >= 2:
                    act.wait_ge(sem("th_read"), s - 1)
                act.activation(th[:, s % 2, :], src, ACT.Tanh, scale=0.5).then_inc(sem("unit_act"), 1)

        def mix_high(i):
            c = BACK[i]
            act.wait_ge(sem("at_out"), NITEM)
            act.wait_ge(sem("s_mixed"), 1)
            copy(act_hi[:, 0:4, cols(c)], mix[:, 0:4, cols(c)]).then_inc(sem("mix_hi"), 1)
            act.wait_ge(sem("th_read"), units_before(SILU, UNITS - CH + i + 1))
            if c == CH - 1:
                act.wait_ge(sem("mix_done"), 1)
            copy(act_hi[:, 4:8, cols(c)], mix[:, 4:8, cols(c)]).then_inc(sem("mix_hi"), 1)

        for tick in range(TICKS):
            for i in NORM_ROWS.get(tick // 2, ()) if tick % 2 == 0 else ():
                if 3 <= i <= LEAD:
                    weight_hi(i - 1)
                if i == 2:
                    high(i, "n_tr", "n_hi", NB)
                if 2 <= i + 1 < RT:
                    squares(i + 1)
                if i != 2:
                    high(i, "n_tr", "n_hi", NB)
                if 1 <= i <= 2:
                    weight_hi(i - 1)
            if tick == AT0:
                act.wait_ge(sem("lb_in"), 1)
                act.activation(lbt[:, 2:4, :], lbt[:, 0:2, :], ACT.Exp).then_inc(sem("lb_exp"), 1)
            for n in split_at(tick):
                weight_hi(n)
            for step in rot_steps(tick):
                if step[0] == "k_high":
                    c = step[1]
                    act.wait_ge(sem("rope"), ROPE_UNITS.index(unit_index("k", 0, c)) + 1)
                    if c == 0:
                        act.wait_ge(sem("k_zero"), 1)
                    for g in range(NKV):
                        h = slice(HD * g, HD * g + HD)
                        ins = copy(k_hi[h, g, cols(c)], kraw[h, cols(c)])
                    ins.then_inc(sem("k_high"), 1)
                if step[0] == "vt":
                    act.wait_ge(sem("v_turned"), step[1] + 1)
                    b0, n = V_GROUPS[step[1]]
                    if n == 4:
                        copy(vrow[:, b0:b0 + 4, :], BR.rearrange("p (b d) -> p b d", b=4)).then_inc(sem("v_rows"), 1)
                    else:
                        copy(vrow[0:DECB, b0, :], BR[0:DECB, 0:P]).then_inc(sem("v_rows"), 1)
                if step[0] == "kw":
                    act.wait_ge(sem("kw_mm"), 1)
                    copy(kn_s[:, :], BR[0:DECB, P:2 * P])
                    copy(kwin[:], BR[:, 0:P]).then_inc(sem("kw_out"), 1)
            for step, i in attention_steps(tick):
                t, j, e = i // NBLK, i % NBLK, i % 2
                k0 = WIN if j == 0 else 0
                if step == "Q":
                    act.wait_ge(sem("rope"), 1 + ROPE_UNITS.index(unit_index("q", t, (P * (j + 1) - 1) // CW)))
                    if i >= 2:
                        act.wait_ge(sem("at_s"), i - 1)
                    copy(q_hi[:, e, :], mix[:, t, P * j:P * j + P]).then_inc(sem("q_high"), 1)
                elif step == "S":
                    act.wait_ge(sem("at_max"), i + 1)
                    if i >= 2:
                        act.wait_ge(sem("at_pt"), i - 1)
                    for g in range(NKV):
                        act.activation(prob[:, e, g, k0:], sm[:, g, k0:], ACT.Exp, bias=negm[:, e, g:g + 1], scale=SCALE,
                                       accum_out=den[:, e, g:g + 1])
                    act.activation(esk[:, e, :], tsum[:, e, :], ACT.Exp).then_inc(sem("at_exp"), 1)
                elif step == "PT":
                    act.wait_ge(sem("at_pt"), i + 1)
                    if i >= 1:
                        act.wait_ge(sem("at_pv"), i)
                    kb = 1 if j == 0 else 0
                    pv = pt[:].rearrange("p (g b) q -> p g b q", g=2)
                    bv = BP.rearrange("p (g b q) -> p g b q", g=2, b=2)
                    copy(pv[:, :, kb:, :], bv[:, :, kb:, :]).then_inc(sem("at_ptc"), 1)
                elif step == "OT":
                    act.wait_ge(sem("at_ot"), i + 1)
                    copy(mix[:, t, P * j:P * j + P], BO[:, P:2 * P]).then_inc(sem("at_out"), 1)
            for step in recurrence_steps(tick):
                h = step[1]
                if step[0] in ("ita", "itb"):
                    a = step[0] == "itb"
                    act.wait_ge(sem("i_turned"), 2 * h + a + 1)
                    if h and not a:
                        act.wait_ge(sem("o_mm"), h)
                    copy(irow[:, 4 * a:4 * a + 4, :], BR.rearrange("p (b d) -> p b d", b=4)).then_inc(sem("i_rows"), 1)
                if step[0] in ("kta", "ktb"):
                    a = step[0] == "ktb"
                    act.wait_ge(sem("k_turned"), 2 * h + a + 1)
                    copy(krow[:, 4 * a:4 * a + 4, :], BR.rearrange("p (b d) -> p b d", b=4)).then_inc(sem("k_rows"), 1)
                if step[0] == "o":
                    act.wait_ge(sem("o_mm"), h + 1)
                    for c in range(NBLK):
                        ins = act.activation(ast[:, c, :], BL[c // 4][:, P * (c % 4):P * (c % 4) + P], ACT.Square,
                                             accum_out=oss[:, c:c + 1])
                    ins.then_inc(sem("o_ss"), 1)
                    root(ostd[:], oss[:], 1.0 / (4 * RD), "o_ss", h + 1).then_inc(sem("o_std"), 1)
            for step in sample_steps(tick):
                if step[0] == "ks_t":
                    for a, b in ((0, BS), (1, BP)):
                        act.wait_ge(sem("ks_turned"), a + 1)
                        copy(kst[:, 4 * a:4 * a + 4, :], b.rearrange("p (b d) -> p b d", b=4)).then_inc(sem("ks_cols"), 1)
                if step[0] == "s_score":
                    act.wait_ge(sem("s_score"), 1)
                    copy(stx[:], BO[:, 0:DECB * NQ]).then_inc(sem("s_scored"), 1)
                if step[0] == "s_turn":
                    act.wait_ge(sem("s_max"), 1)
                    n = DECB * NQ
                    act.activation(px[:], BP[0:n, 0:P], ACT.Exp, bias=sst[0:n, 1:2], scale=SCALE, accum_out=sst[0:n, 3:4])
                    act.activation(sst[0:n, 4:5], sst[0:n, 2:3], ACT.Exp).then_inc(sem("s_exp"), 1)
                if step[0] == "s_back":
                    act.wait_ge(sem("s_back"), 1)
                    copy(ptx[:], BP[:, 0:DECB * NQ]).then_inc(sem("s_pt"), 1)
                if step[0] == "r_turn":
                    act.wait_ge(sem("s_turned"), step[1] + 1)
                    if step[1]:
                        act.wait_ge(sem("s_outer"), step[1])
                    copy(ki[:], BP[0:DECB, 0:2 * P].rearrange("p (a d) -> p a d", a=2)).then_inc(sem("s_ki"), 1)
                if step[0] == "r_rows":
                    n = NREC * DECB
                    act.wait_ge(sem("so_turned"), 1)
                    act.activation(px[0:n, :], BP[0:n, 0:P], ACT.Square, accum_out=sst[0:n, 5:6]).then_inc(sem("so_ss"), 1)
                    root(sst[0:n, 6:7], sst[0:n, 5:6], 1.0 / (4 * RD), "so_ss", 1).then_inc(sem("so_std"), 1)
            if tick % 2:
                unit_read(tick // 2)
                if tick // 2 >= UNITS - CH:
                    mix_high(tick // 2 - (UNITS - CH))
        def gate(q, e, first=False):
            act.wait_ge(sem("gate_mm"), q + 1)
            if not first:
                act.wait_ge(sem("hf_done"), q - 1)
            act.activation(sg[:, e, :], bank[e][:, 0:CW], ACT.Silu).then_inc(sem("gate_done"), 1)

        def hidden_hi(q, j, c, e):
            act.wait_ge(sem("hf_done"), q + 1)
            copy(h_hi[:, j, cols(c)], hf[:, e, :]).then_inc(sem("h_hi_done"), 1)

        for slot in range(SLOTS):
            for step, i in row_steps(slot):
                w = rows_of(back_row(i))[1]
                if step == "out":
                    act.wait_ge(sem("p_tr"), i + 1)
                    if i >= 2:
                        act.wait_ge(sem("h2_tr"), 2 * (i - 1))
                    act.activation(tr[0:w, i % 2, :].rearrange("p (a b) -> p a b", a=2), pair[2][0:w, :, :], ACT.Square,
                                   accum_out=ss[0:w, 0, i:i + 1]).then_inc(sem("p_ss"), 1)
                    root(std[0:w, 0, i:i + 1], ss[0:w, 0, i:i + 1], 1.0 / DM, "p_ss", i + 1).then_inc(sem("p_std"), 1)
                if step == "mid":
                    act.wait_ge(sem("x2"), i + 1)
                    act.activation(tr[0:w, i % 2, :], x2r[0:w, i % 2, :], ACT.Square, accum_out=ss[0:w, 1, i:i + 1])\
                        .then_inc(sem("q_ss"), 1)
                    root(std[0:w, 1, i:i + 1], ss[0:w, 1, i:i + 1], 1.0 / DM, "q_ss", i + 1).then_inc(sem("q_std"), 1)
                if step == "in":
                    high(i, "h2_tr", "h2_hi", bank[6:8], back_row(i))
            if slot < 24:
                m, c = slot % NOUT, BACK[slot // NOUT]
                u = UNITS + slot
                act.wait_ge(sem("unit"), u + 1)
                act.wait_ge(sem("mix_lo"), 2 * (slot // NOUT) + 2)
                copy(mix[:, m, cols(c)], J[u % 2][:, 0:CW]).then_inc(sem("unit_act"), 1)
            for n in slot_tiles(slot):
                weight_hi(n)
            if slot >= 24:
                q = (slot - 24) // 2
                if slot % 2 == 0:
                    gate(q, q % 2, q < 2)
                else:
                    hidden_hi(q, q % 2, BACK[q // 2], q % 2)
            if slot in DOWN_SLOTS:
                j = DOWN_SLOTS.index(slot)
                act.wait_ge(sem("h2_rows"), RT)
                act.wait_ge(sem("x2_out0"), 16 * 5)
                act.wait_ge(sem("x2_out1"), 16 * 4)
                act.wait_ge(sem(f"draw_in{j}"), 16)
                copy(d_hi[:, j, :], draw[:, j, :]).then_inc(sem("d_hi_done"), 1)

        def down_hi(g):
            for j in range(2):
                act.wait_ge(sem(f"draw_in{j}"), 16 * g + 16)
                act.wait_ge(sem("down_mm"), 24 * g)
                copy(d_hi[:, j, :], draw[:, j, :]).then_inc(sem("d_hi_done"), 1)

        def next_hi(g, j, done):
            for k in range(2):
                n = 4 * g + (N12 + 4 + 2 * j + k)
                weight_hi(n, (N12 + 2 * j + k) % 4, slot_total[k] + 16 * (2 + j + 1) + 32 * g, (("gate_mm", "up_mm")[k], done))

        def ffn(g, more):
            down_hi(g)
            for j in range(2):
                for c in range(CH):
                    q, e = 6 * g + (3 * j + c), (3 * j + c) % 2
                    gate(q, e)
                    hidden_hi(q, j, c, e)
                if more:
                    next_hi(g, j, 6 * g + (3 * j + 3))

        next_hi(0, 0, 5)
        next_hi(0, 1, 6)
        with act.Fori(1, GROUPS - 1) as g:
            ffn(g, True)
        ffn(GROUPS - 1, False)

        for i in range(RT):
            r, w = rows_of(i)
            act.wait_ge(sem("y_tr"), i + 1)
            if i >= 4:
                act.wait_ge(*y_added(i - 4))
            act.activation(ty[0:w, i % 4, :].rearrange("p (a b) -> p a b", a=2), pair[i % 2][0:w, :, :], ACT.Square,
                           accum_out=ss[0:w, 1, i:i + 1]).then_inc(sem("y_ss"), 1)
            root(std[0:w, 1, i:i + 1], ss[0:w, 1, i:i + 1], 1.0 / DM, "y_ss", i + 1).then_inc(sem("y_std"), 1)

    @blk.tensor
    def _(pe):
        def rows_to_cols(rows, i, banks, q_sem, free_sem, tile=None):
            w = rows_of(i if tile is None else tile)[1]
            for kk in range(2):
                q = 2 * i + kk
                if q >= len(banks):
                    pe.wait_ge(sem(free_sem), q - len(banks) + 1)
                for k in range(4):
                    mm = pe.transpose(banks[q % len(banks)][:, P * k:P * k + w],
                                      rows[:, P * (4 * kk + k):P * (4 * kk + k) + P], ident[0:w, 0:w])
                mm.then_inc(sem(q_sem), 1)

        pe.wait_ge(sem("id_in"), 16)

        def products(out, weights, c, lo, hi):
            for k in range(lo, hi):
                for s, (a, b) in enumerate(((weights[0], act_hi), (weights[0], act_lo), (weights[1], act_hi))):
                    mm = pe.matmul(out, a[:, k, :], b[:, k, cols(c)], start=(k == 0 and s == 0), stop=(k == KT - 1 and s == 2))
            return mm

        def keep_warm(n):
            for _ in range(n):
                pe.transpose(BR[:, 0:P], ident[:], ident[:])

        br_free = None

        def take_br(sem_name, value):
            nonlocal br_free
            if br_free is not None:
                pe.wait_ge(sem(br_free[0]), br_free[1])
            br_free = (sem_name, value)

        bl_free = None

        def take_bl(sem_name, value):
            nonlocal bl_free
            if bl_free is not None:
                pe.wait_ge(sem(bl_free[0]), bl_free[1])
            bl_free = (sem_name, value)

        for tick in range(TICKS):
            u, half = tick // 2, tick % 2
            n, c = ORDER[u]
            if half == 0:
                for i in NORM_ROWS.get(u, ()):
                    if u == 0:
                        keep_warm((7, 6, 4)[i])
                    pe.wait_ge(sem("h_rows"), i + 1)
                    rows_to_cols(hr_first(i), i, NB, "n_tr", "n_lo")
                if u == 0:
                    keep_warm(12)
                if u < LEAD * CH:
                    pe.wait_ge(sem("n_lo"), 2 * min(RT, chunk_of_rows(c)))
                pe.wait_ge(sem("w_split"), n + 1)
                if u >= 2:
                    pe.wait_ge(sem("unit_act"), u - 1)
                    if unit_of(u - 2)[0] in ("rq", "rg"):
                        pe.wait_ge(sem("th_read"), units_before(SILU, u - 1))
            mm = products(J[u % 2][:, 0:CW], w_tiles(n), c, 4 * half, 4 * half + 4)
            if half:
                mm.then_inc(sem("unit"), 1)
            for step in rot_steps(tick):
                if step[0] == "vt":
                    b0, nb = V_GROUPS[step[1]]
                    pe.wait_ge(sem("unit_act"), unit_index("v", 0, 1 if step[1] == 0 else 2) + 1)
                    take_br("v_rows", step[1] + 1)
                    for b in range(nb):
                        r, w = rows_of(b0 + b)
                        mm = pe.transpose(BR[0:w, P * b:P * b + P], vt[:, r:r + w], ident[:])
                    mm.then_inc(sem("v_turned"), 1)
                if step[0] == "kw":
                    pe.wait_ge(sem("rope"), ROPE_UNITS.index(unit_index("k", 0, 2)) + 1)
                    take_br("kw_out", 1)
                    for (r, w), c in ((rows_of(NBLK - 1), 0), (rows_of(NBLK), P)):
                        mm = pe.transpose(BR[0:w, c:c + P], kraw[:, r:r + w], ident[:])
                    mm.then_inc(sem("kw_mm"), 1)
            for step, i in attention_steps(tick):
                t, j, e = i // NBLK, i % NBLK, i % 2
                kbs = (1,) if j == 0 else (0, 1)
                if step == "S":
                    pe.wait_ge(sem("k_low"), (P * (j + 1) - 1) // CW + 1)
                    pe.wait_ge(sem("q_low"), i + 1)
                    if i == 0:
                        pe.wait_ge(sem("n_lo"), 2 * RT)
                    if i:
                        pe.wait_ge(sem("at_max"), i)
                    out = BS.rearrange("p (g k) -> p g k", g=2)
                    k0 = WIN if j == 0 else 0
                    for n, (a, b) in enumerate(((q_hi, k_hi), (q_hi, k_lo), (q_lo, k_hi))):
                        mm = pe.matmul(out[:, :, k0:], a[:, e, :], b[:, :, P * (j - 1) + k0:P * (j + 1)], start=(n == 0), stop=(n == 2))
                    mm.then_inc(sem("at_s"), 1)
                elif step == "PT":
                    pe.wait_ge(sem("at_exp"), i + 1)
                    if i:
                        pe.wait_ge(sem("at_ptc"), i)
                    for g in range(NKV):
                        for kb in kbs:
                            mm = pe.transpose(BP[:, P * (2 * g + kb):P * (2 * g + kb) + P], prob[:, e, g, P * kb:P * kb + P], ident[:])
                    mm.then_inc(sem("at_pt"), 1)
                elif step == "PV":
                    pe.wait_ge(sem("at_ptc"), i + 1)
                    pe.wait_ge(sem("v_rows"), j // 4 + 1)
                    if i:
                        pe.wait_ge(sem("at_out"), i)
                    for g in range(NKV):
                        for kb in kbs:
                            mm = pe.matmul(BO[:, HD * g:HD * g + HD], pt[:, 2 * g + kb, :], vrow[:, j - 1 + kb, HD * g:HD * g + HD],
                                           start=(kb == kbs[0]), stop=(kb == 1))
                    mm.then_inc(sem("at_pv"), 1)
                elif step == "OT":
                    pe.wait_ge(sem("at_or"), i + 1)
                    pe.transpose(BO[:, P:2 * P], orow[:].rearrange("p g d -> p (g d)"), ident[:]).then_inc(sem("at_ot"), 1)
            for step in recurrence_steps(tick):
                h = step[1]
                if step[0] in ("ita", "itb"):
                    a = step[0] == "itb"
                    if not a:
                        pe.wait_ge(sem("unit_act"), unit_index("ri", h, 2) + 1)
                    take_br("i_rows", 2 * h + a + 1)
                    for b in range(4):
                        c = 4 * a + b
                        mm = pe.transpose(BR[:, P * b:P * b + P], r_i[:, P * c:P * c + P], ident[:])
                    mm.then_inc(sem("i_turned"), 1)
                if step[0] == "diag":
                    pe.wait_ge(sem("hq_prep"), h + 1)
                    take_bl("diag_read", h + 1)
                    for c in range(NBLK):
                        mm = pe.matmul(BL[c // 4][:, P * (c % 4):P * (c % 4) + P], hk[:, P * c:P * c + P], r_q[:, P * c:P * c + P],
                                       start=True, stop=True)
                    mm.then_inc(sem("diag_mm"), 1)
                if step[0] == "level":
                    n = step[2]
                    if n:
                        pe.wait_ge(sem("hq_step"), LEVELS * h + n)
                    if n == 0:
                        take_bl("level_read", LEVELS * (h + 1))
                    elif n >= 2:
                        pe.wait_ge(sem("level_read"), LEVELS * h + n - 1)
                    hs = 1 << n
                    qv = hq[:].rearrange("p (c b e s) -> p c b e s", c=NBLK, e=2, s=hs)
                    for c in range(NBLK):
                        mm = pe.matmul(BL[n % 2][0:P - hs, P // 2 * c:P // 2 * (c + 1)], hk[:, P * c:P * c + P - hs], qv[:, c, :, 1, :],
                                       start=True, stop=True)
                    mm.then_inc(sem("level_mm"), 1)
                if step[0] in ("kta", "ktb"):
                    a = step[0] == "ktb"
                    pe.wait_ge(sem("hq_step"), LEVELS * (h + 1))
                    take_br("k_rows", 2 * h + a + 1)
                    for b in range(4):
                        c = 4 * a + b
                        mm = pe.transpose(BR[:, P * b:P * b + P], hk[:, P * c:P * c + P], ident[:])
                    mm.then_inc(sem("k_turned"), 1)
                if step[0] == "u":
                    pe.wait_ge(sem("k_rows"), 2 * h + 2)
                    pe.wait_ge(sem("i_rows"), 2 * h + 2)
                    take_bl("chain", NBLK * (h + 1))
                    for c in range(NBLK):
                        mm = pe.matmul(BL[c // 4][:, P * (c % 4):P * (c % 4) + P], krow[:, c, :], irow[:, c, :], start=True, stop=True)
                    mm.then_inc(sem("u_mm"), 1)
                if step[0] == "o":
                    take_bl("o_norm", h + 1)
                    for c in range(NBLK):
                        out = BL[c // 4][:, P * (c % 4):P * (c % 4) + P]
                        mm = pe.matmul(out, ast[:, c, :], irow[:, c, :], start=True, stop=(c == 0))
                        if c:
                            mm = pe.matmul(out, hq[:, P * c:P * c + P], states[:, c, :], start=False, stop=True)
                    mm.then_inc(sem("o_mm"), 1)
                if step[0] == "ot":
                    take_bl("o_cols", 2 * h + 2)
                    for a in range(2):
                        for b in range(4):
                            c = 4 * a + b
                            mm = pe.transpose(BL[a][:, P * b:P * b + P], orn[:, P * c:P * c + P], ident[:])
                        mm.then_inc(sem("o_turned"), 1)
            for step in sample_steps(tick):
                if step[0] == "ks_t":
                    pe.wait_ge(sem("win_in"), WIN_LOADS)
                    pe.wait_ge(sem("at_out"), NITEM)
                    for a, b in ((0, BS), (1, BP)):
                        for c in range(4):
                            mm = pe.transpose(b[:, P * c:P * c + P], ks[:, 4 * a + c, :], ident[:])
                        mm.then_inc(sem("ks_turned"), 1)
                if step[0] == "s_score":
                    pe.wait_ge(sem("ks_cols"), 2)
                    pe.wait_ge(sem("qp_done"), 1)
                    for b in range(DECB):
                        mm = pe.matmul(BO[:, NQ * b:NQ * b + NQ], kst[:, b, :], qp[:, b, :], start=True, stop=True)
                    mm.then_inc(sem("s_score"), 1)
                if step[0] == "s_turn":
                    pe.wait_ge(sem("s_scored"), 1)
                    pe.transpose(BP[0:DECB * NQ, 0:P], stx[:], ident[:]).then_inc(sem("s_turn"), 1)
                if step[0] == "s_back":
                    pe.wait_ge(sem("s_prob"), 1)
                    pe.transpose(BP[:, 0:DECB * NQ], px[:], ident[0:DECB * NQ, 0:DECB * NQ]).then_inc(sem("s_back"), 1)
                if step[0] == "s_out":
                    pe.wait_ge(sem("s_pt"), 1)
                    for b in range(DECB):
                        mm = pe.matmul(BO[:, NQ * b:NQ * b + NQ], vs[:, b, :], ptx[:, NQ * b:NQ * b + NQ], start=True, stop=True)
                    mm.then_inc(sem("s_out"), 1)
                if step[0] == "r_turn":
                    h = step[1]
                    pe.wait_ge(sem("ks_saved"), h + 1)
                    if h:
                        pe.wait_ge(sem("s_os"), h)
                    for a, x in ((0, k_s), (1, i_s)):
                        mm = pe.transpose(BP[0:DECB, P * a:P * a + P], x[:, h, :], ident[:])
                    mm.then_inc(sem("s_turned"), 1)
                if step[0] == "r_outer":
                    h = step[1]
                    pe.wait_ge(sem("s_ib"), h + 1)
                    if h == 0:
                        pe.wait_ge(sem("s_mixed"), 1)
                    for a, b in ((0, BS), (1, BO)):
                        mm = pe.matmul(b, ki[:, 0, :], ib[:, 4 * a:4 * a + 4, :], start=True, stop=True)
                    mm.then_inc(sem("s_outer"), 1)
                if step[0] == "r_o":
                    h = step[1]
                    pe.wait_ge(sem("s_state"), 2 * h + 2)
                    for b in range(DECB):
                        mm = pe.matmul(BP[:, b:b + 1], st[:, b, :], q_s[:, h, b:b + 1], start=True, stop=True)
                    mm.then_inc(sem("s_o"), 1)
                if step[0] == "r_rows":
                    pe.wait_ge(sem("s_os"), NREC)
                    pe.transpose(BP[0:NREC * DECB, 0:P], o_s[:].rearrange("p h b -> p (h b)"), ident[:]).then_inc(sem("so_turned"), 1)
                if step[0] == "r_cols":
                    n = NREC * DECB
                    pe.wait_ge(sem("so_norm"), 1)
                    pe.transpose(BP[:, 0:n], px[0:n, :], ident[0:n, 0:n]).then_inc(sem("so_cols"), 1)
        def cols_to_rows(i, out, out_sem):
            r, w = rows_of(i)
            for m in range(KT):
                mm = pe.transpose(out[0:w, m // 4, P * (m % 4):P * (m % 4) + P], mix[:, m, r:r + w], ident[:])
            mm.then_inc(sem(out_sem), 1)

        for slot in range(SLOTS):
            for step, i in row_steps(slot):
                if step == "out":
                    pe.wait_ge(sem("unit_act"), UNITS + NOUT * (BACK.index(rows_of(back_row(i))[0] // CW) + 1))
                    if i:
                        pe.wait_ge(sem("p_t"), i)
                    cols_to_rows(back_row(i), pair[2], "p_tr")
                if step == "in":
                    pe.wait_ge(sem("h2_rows"), i + 1)
                    rows_to_cols(tr[0:rows_of(back_row(i))[1], i % 2, :], i, bank[6:8], "h2_tr", "h2_lo", back_row(i))
            if slot < 24:
                m, c = slot % NOUT, BACK[slot // NOUT]
                n, u = NIN + m, UNITS + slot
                if slot < NOUT:
                    pe.wait_ge(sem("w_split"), n + 1)
                pe.wait_ge(sem("unit_act"), u - 1)
                if slot < 2:
                    pe.wait_ge(sem("th_read"), units_before(SILU, UNITS - 1 + slot))
                if m == 0:
                    pe.wait_ge(sem("mix_lo"), 2 * (slot // NOUT) + 2)
                products(J[u % 2][:, 0:CW], w_tiles(n), c, 0, KT).then_inc(sem("unit"), 1)
            else:
                q, k = (slot - 24) // 2, slot % 2
                c, j = BACK[q // 2], q % 2
                if j == 0 and k == 0:
                    pe.wait_ge(sem("h2_lo"), 2 * (back_row(CW * c // P) + 1))
                if q < 2:
                    pe.wait_ge(sem("w_split"), N12 + 2 * j + k + 1)
                if q < 2 and k == 0:
                    pe.wait_ge(sem("unit_act"), UNITS + 24)
                if q >= 2:
                    pe.wait_ge(sem(("gate_done", "hf_done")[k]), q - 1)
                s4 = (N12 + 2 * j + k) % 4
                products(bank[2 * k + q % 2][:, 0:CW], (w_hi[:, s4], w_lo[:, s4]), c, 0, KT).then_inc(sem(("gate_mm", "up_mm")[k]), 1)

        def up(g):
            for j in range(2):
                for c in range(CH):
                    q = 6 * g + 3 * j + c
                    e = (3 * j + c) % 2
                    for k in range(2):
                        if c == 0:
                            pe.wait_ge(sem("w_split"), 4 * g + (N12 + 2 * j + k + 1))
                        pe.wait_ge(sem(("gate_done", "hf_done")[k]), q - 1)
                        s4 = (N12 + 2 * j + k) % 4
                        products(bank[2 * k + e][:, 0:CW], (w_hi[:, s4], w_lo[:, s4]), c, 0, KT)\
                            .then_inc(sem(("gate_mm", "up_mm")[k]), 1)

        def down(g, first, last):
            pe.wait_ge(sem("d_split"), 2 * g + 2)
            for c, (c0, cw) in enumerate(LAST_CHUNKS if last else CHUNKS[::-1] if first else CHUNKS):
                pe.wait_ge(sem("h_lo_done"), 2 * c + 2 if first else 6 * g + (4 + min(c, CH - 1)))
                for m in range(KT):
                    v = KT * c + m
                    if not (first and v < 4):
                        pe.wait_ge(sem("acc_done"), 24 * g + (v - 3))
                    for j in range(2):
                        for s, (a, b) in enumerate(((d_hi, h_hi), (d_hi, h_lo), (d_lo, h_hi))):
                            mm = pe.matmul(bank[4 + v % 4][:, 0:cw], a[:, j, P * m:P * m + P], b[:, j, c0:c0 + cw],
                                           start=(j == 0 and s == 0), stop=(j == 1 and s == 2))
                    mm.then_inc(sem("down_mm"), 1)
                    if last and v in LAST_ROWS:
                        last_rows(LAST_ROWS.index(v))

        def last_rows(i):
            r, w = rows_of(i)
            pe.wait_ge(sem("acc_done"), 24 * (GROUPS - 1) + KT * (1 + max(c for c, (c0, _) in enumerate(LAST_CHUNKS) if c0 < r + w)))
            if i >= 2:
                pe.wait_ge(sem("y_t"), i - 1)
            cols_to_rows(i, pair[i % 2], "y_tr")

        down(0, True, False)
        with pe.Fori(1, GROUPS - 1) as g:
            up(g)
            down(g, False, False)
        up(GROUPS - 1)
        down(GROUPS - 1, False, True)
        for i in range(len(LAST_ROWS), RT):
            last_rows(i)

    @blk.vector
    def _(dve):
        chain = [0]

        def then(ins):
            chain[0] += 1
            ins.then_inc(sem("dve_chain"), 1)
            dve.wait_ge(sem("dve_chain"), chain[0])

        dve.memset(eps[:], EPS).then_inc(sem("eps_set"), 1)

        def norm_rows(i):
            r, w = rows_of(i)
            dve.wait_ge(sem("n_std"), i + 1)
            then(dve.reciprocal(rstd[0:w, 0, i:i + 1], std[0:w, 0, i:i + 1]))
            if i == 0:
                dve.wait_ge(sem("g_in"), 16)
            dve.scalar_tensor_tensor(out=hr_first(i), in0=xr_first(i), scalar=rstd[0:w, 0, i:i + 1],
                                     in1=gb0[0:w, :], op0=ALU.mult, op1=ALU.mult).then_inc(sem("h_rows"), 1)

        def low(i, hi_sem, lo_sem, banks, tile=None):
            r, w = rows_of(i if tile is None else tile)
            for kk in range(2):
                q = 2 * i + kk
                dve.wait_ge(sem(hi_sem), q + 1)
                dve.tensor_tensor(act_lo[:, 4 * kk:4 * kk + 4, r:r + w],
                                  banks[q % len(banks)].rearrange("p (k r) -> p k r", k=4)[:, :, 0:w],
                                  act_hi[:, 4 * kk:4 * kk + 4, r:r + w].bitcast(F32), ALU.subtract).then_inc(sem(lo_sem), 1)

        norm_rows(0)
        norm_rows(1)

        def lower_bound():
            dve.wait_ge(sem("const_in"), NCONST)
            then(dve.tensor_tensor(lbt[:, 4, :], lbl[:, 0, :], lbl[:, 1, :], ALU.max))
            dve.tensor_tensor(lbt[:, 0, :], lbl[:, 0, :], lbt[:, 4, :], ALU.subtract)
            dve.tensor_tensor(lbt[:, 1, :], lbl[:, 1, :], lbt[:, 4, :], ALU.subtract).then_inc(sem("lb_in"), 1)
            then(dve.tensor_scalar(nsink[:], sink[:], -1.0, None, ALU.mult))
            dve.wait_ge(sem("lb_exp"), 1)
            then(dve.tensor_tensor(lbt[:, 5, :], lbt[:, 2, :], lbt[:, 3, :], ALU.add))
            then(dve.reciprocal(lbt[:, 6, :], lbt[:, 5, :]))
            then(dve.tensor_tensor(lbt[:, 4, :], lbt[:, 2, :], lbt[:, 6, :], ALU.mult))
            then(dve.tensor_scalar(lbt[:, 5, :], lbt[:, 4, :], -0.5, 0.5, ALU.mult, ALU.add))
            then(dve.tensor_tensor(lbt[:, 6, :], lbt[:, 4, :], lbt[:, 5, :], ALU.add))

        f_scale, f_shift = lbt[:, 5, :], lbt[:, 6, :]

        def rope(r):
            kind, m, c = unit_of(ROPE_UNITS[r])
            if r == 0:
                dve.wait_ge(sem("rot_in"), 32)
            dve.wait_ge(sem("unit_act"), ROPE_UNITS[r] + 1)
            x = kraw[:, cols(c)] if kind == "k" else mix[:, m, cols(c)]
            tmp = sm_rope[:, 0:CW]
            if r:
                dve.wait_ge(sem("rope"), r)
            then(dve.stream_shuffle(tmp, x, ROT_MASK))
            dve.tensor_tensor(x, x, cos[:, cols(c)], ALU.mult)
            then(dve.tensor_tensor(tmp, tmp, sin[:, cols(c)], ALU.mult))
            dve.tensor_tensor(x, x, tmp, ALU.add).then_inc(sem("rope"), 1)

        def keys_low(c):
            dve.wait_ge(sem("k_high"), c + 1)
            for g in range(NKV):
                h = slice(HD * g, HD * g + HD)
                ins = dve.tensor_tensor(k_lo[h, g, cols(c)], kraw[h, cols(c)], k_hi[h, g, cols(c)].bitcast(F32), ALU.subtract)
            ins.then_inc(sem("k_low"), 1)

        sm_rope = hk

        def unit_read(u):
            kind, m, c = unit_of(u)
            src = J[u % 2][:, 0:CW]
            if kind == "ri":
                if c == CH - 1:
                    dve.wait_ge(sem("unit_act"), u + 1)
                    dve.tensor_copy(i_s[:, m, :], r_i[:, SEQ:ROWS]).then_inc(sem("s_saved"), 1)
            if kind not in SILU:
                return
            s = units_before(SILU, u)
            dve.wait_ge(sem("unit_act"), u + 1)
            if kind == "rf":
                if m and c == 0:
                    dve.wait_ge(sem("g_prod"), LEVELS * (m - 1) + 1)
                dve.tensor_scalar(r_f[:, cols(c)], th[:, s % 2, :], f_scale[:, m:m + 1], f_shift[:, m:m + 1],
                                  ALU.mult, ALU.add).then_inc(sem("th_read"), 1)
                dve.wait_ge(sem("th_read"), s + 1)
                if c == CH - 1:
                    dve.tensor_copy(f_s[:, m, :], r_f[:, SEQ:ROWS]).then_inc(sem("f_done"), 1)
                    dve.tensor_scalar(k_s[:, m, :], r_f[:, SEQ:ROWS], -1.0, 1.0, ALU.mult, ALU.add).then_inc(sem("ks_saved"), 1)
            elif kind == "rq":
                if m and c == 0:
                    dve.wait_ge(sem("diag_mm"), m)
                dve.scalar_tensor_tensor(out=r_q[:, cols(c)], in0=th[:, s % 2, :], scalar=1.0, in1=src,
                                         op0=ALU.add, op1=ALU.mult).then_inc(sem("th_read"), 1)
                if c == CH - 1:
                    dve.wait_ge(sem("th_read"), s + 1)
                    then(dve.tensor_copy(q_s[:, m, :], r_q[:, SEQ:ROWS]))
            else:
                w = CW if c < CH - 1 else CW - DECB
                dve.scalar_tensor_tensor(out=th[:, s % 2, :], in0=th[:, s % 2, :], scalar=1.0, in1=src,
                                         op0=ALU.add, op1=ALU.mult).then_inc(sem("g_gate"), 1)
                dve.wait_ge(sem("g_gate"), units_before(("rg",), u) + 1)
                dve.wait_ge(sem("o_cols"), 2 * (m + 1))
                dst = mix[:, 4 + m, CW * c:CW * c + w]
                if c == CH - 1:
                    then(dve.tensor_copy(g_s[:, m, :], th[:, s % 2, w:CW]))
                dve.tensor_tensor(dst, dst, th[:, s % 2, 0:w], ALU.mult).then_inc(sem("th_read"), 1)

        def decay(h, n):
            hs = 1 << n
            g = r_f[:, 0:SEQ] if n == 0 else g_level(n)
            gv = g.rearrange("p (b e) -> p b e", e=2)
            qv = hq[:].rearrange("p (b e s) -> p b e s", e=2, s=hs)
            kv = hk[:].rearrange("p (b e s) -> p b e s", e=2, s=hs)
            nb = SEQ // (2 * hs)
            if n:
                dve.wait_ge(sem("g_prod"), LEVELS * h + n)
            dve.tensor_tensor(qv[:, :, 1, :], qv[:, :, 1, :], bc(gv[:, :, 0].unsqueeze(2), [P, nb, hs]), ALU.mult)
            dve.tensor_tensor(kv[:, :, 0, :], kv[:, :, 0, :], bc(gv[:, :, 1].unsqueeze(2), [P, nb, hs]), ALU.mult)\
                .then_inc(sem("hq_step"), 1)

        def mix_low(i):
            c = BACK[i]
            for kk in range(2):
                dve.wait_ge(sem("mix_hi"), 2 * i + kk + 1)
                dve.tensor_tensor(act_lo[:, 4 * kk:4 * kk + 4, cols(c)], mix[:, 4 * kk:4 * kk + 4, cols(c)],
                                  act_hi[:, 4 * kk:4 * kk + 4, cols(c)].bitcast(F32), ALU.subtract).then_inc(sem("mix_lo"), 1)

        for tick in range(TICKS):
            for i in NORM_ROWS.get(tick // 2, ()) if tick % 2 == 0 else ():
                if i == 2:
                    low(i, "n_hi", "n_lo", NB)
                if 2 <= i + 1 < RT:
                    norm_rows(i + 1)
                if i != 2:
                    low(i, "n_hi", "n_lo", NB)
            if tick == AT0:
                lower_bound()
            for step in rot_steps(tick):
                if step[0] == "rot":
                    rope(step[1])
                if step[0] == "k_low":
                    keys_low(step[1])
            for step, i in attention_steps(tick):
                t, j, e = i // NBLK, i % NBLK, i % 2
                k0 = WIN if j == 0 else 0
                if step == "Q":
                    dve.wait_ge(sem("q_high"), i + 1)
                    dve.tensor_tensor(q_lo[:, e, :], mix[:, t, P * j:P * j + P], q_hi[:, e, :].bitcast(F32), ALU.subtract)\
                        .then_inc(sem("q_low"), 1)
                elif step == "S":
                    dve.wait_ge(sem("at_s"), i + 1)
                    if i:
                        dve.wait_ge(sem("at_exp"), i)
                    for g in range(NKV):
                        ins = dve.tensor_tensor_reduce(sm[:, g, k0:], BS[:, 2 * WIN * g + k0:2 * WIN * (g + 1)], amask[:, k0:],
                                                       1.0, -3.0e38, ALU.add, ALU.max, mx[:, e, g:g + 1])
                    then(ins)
                    then(dve.scalar_tensor_tensor(out=negm[:, e, :], in0=mx[:, e, :], scalar=-SCALE, in1=nsink[:, t:t + GRP + 1:GRP],
                                                  op0=ALU.mult, op1=ALU.min))
                    dve.tensor_tensor(tsum[:, e, :], sink[:, t:t + GRP + 1:GRP], negm[:, e, :], ALU.add).then_inc(sem("at_max"), 1)
                elif step == "PT":
                    dve.wait_ge(sem("at_exp"), i + 1)
                    then(dve.tensor_tensor(den[:, e, :], den[:, e, :], esk[:, e, :], ALU.add))
                    then(dve.reciprocal(rden[:, e, :], den[:, e, :]))
                elif step == "PV":
                    dve.wait_ge(sem("at_pv"), i + 1)
                    if i:
                        dve.wait_ge(sem("at_ot"), i)
                    dve.tensor_tensor(orow[:], BO[:, 0:P].rearrange("p (g d) -> p g d", g=2),
                                      bc(rden[:, e, :].unsqueeze(2), [P, 2, HD]), ALU.mult).then_inc(sem("at_or"), 1)
            for step in recurrence_steps(tick):
                h = step[1]
                if step[0] == "prep":
                    dve.wait_ge(sem("f_done"), h + 1)
                    if h:
                        dve.wait_ge(sem("o_turned"), 2 * h)
                    dve.tensor_tensor(hq[:], r_q[:, 0:SEQ], r_f[:, 0:SEQ], ALU.mult)
                    dve.tensor_scalar(hk[:], r_f[:, 0:SEQ], -1.0, 1.0, ALU.mult, ALU.add).then_inc(sem("hq_prep"), 1)
                if step[0] == "diag":
                    dve.wait_ge(sem("diag_mm"), h + 1)
                    if h == 0:
                        dve.wait_ge(sem("stored"), 32)
                    else:
                        dve.wait_ge(sem("o_ss"), h)
                    for a in range(2):
                        ins = dve.tensor_tensor(ast[:, 4 * a:4 * a + 4, :], BL[a].rearrange("p (b t) -> p b t", b=4),
                                                bc(ident[:].unsqueeze(1), [P, 4, P]), ALU.mult)
                    ins.then_inc(sem("diag_read"), 1)
                    dve.wait_ge(sem("diag_read"), h + 1)
                if step[0] == "level":
                    n = step[2]
                    dve.wait_ge(sem("level_mm"), LEVELS * h + n + 1)
                    if n == 0 and h == 0:
                        dve.wait_ge(sem("lmask_done"), 1)
                    decay(h, n)
                    nb, hs = P // (2 << n), 1 << n
                    av = ast[:].rearrange("p c (b e s) -> p c b e s", e=2, s=hs)
                    mv = lmask[:, n, :].rearrange("p (b e s) -> p b e s", e=2, s=hs)[:, :, 1, :]
                    k = P - hs
                    dve.copy_predicated(av[0:k, :, :, 1, :], bc(mv[0:k].unsqueeze(1), [k, NBLK, nb, hs]),
                                        BL[n % 2][0:k, :].rearrange("p (c b s) -> p c b s", c=NBLK, s=hs)).then_inc(sem("level_read"), 1)
                    dve.wait_ge(sem("level_read"), LEVELS * h + n + 1)
                if step[0] == "u":
                    dve.wait_ge(sem("u_mm"), h + 1)
                    dve.wait_ge(sem("g_prod"), LEVELS * (h + 1))
                    if h:
                        dve.wait_ge(sem("stp_out"), 16 * h)
                    gl = g_level(LEVELS)
                    for c in range(NBLK):
                        u_c = BL[c // 4][:, P * (c % 4):P * (c % 4) + P]
                        if c == 0:
                            ins = dve.tensor_copy(states[:, 1, :], u_c)
                        else:
                            ins = dve.scalar_tensor_tensor(out=states[:, c + 1, :], in0=states[:, c, :], scalar=gl[:, c:c + 1],
                                                           in1=u_c, op0=ALU.mult, op1=ALU.add)
                        ins.then_inc(sem("chain"), 1)
                        dve.wait_ge(sem("chain"), NBLK * h + c + 1)
                if step[0] == "o":
                    dve.wait_ge(sem("o_std"), h + 1)
                    then(dve.reciprocal(orstd[:], ostd[:]))
                    then(dve.tensor_scalar(orstd[:], orstd[:], 0.25, None, ALU.mult))
                    for a in range(2):
                        ins = dve.tensor_tensor(orn[:, 4 * P * a:4 * P * a + 4 * P].rearrange("p (b t) -> p b t", b=4),
                                                BL[a].rearrange("p (b t) -> p b t", b=4),
                                                bc(orstd[:, 4 * a:4 * a + 4].unsqueeze(2), [P, 4, P]), ALU.mult)
                    ins.then_inc(sem("o_norm"), 1)
                if step[0] == "ot":
                    for a in range(2):
                        dve.wait_ge(sem("o_turned"), 2 * h + a + 1)
                        dve.tensor_scalar(mix[:, 4 + h, 4 * P * a:4 * P * a + 4 * P], BL[a], rnorm[:, h:h + 1], None, ALU.mult)\
                            .then_inc(sem("o_cols"), 1)
            for step in sample_steps(tick):
                n = DECB * NQ
                if step[0] == "ks_t":
                    dve.wait_ge(sem("qp_zero"), 1)
                    dve.wait_ge(sem("at_out"), NITEM)
                    for g in range(NKV):
                        ins = dve.tensor_copy(qp[HD * g:HD * g + HD, :, GRP * g:GRP * g + GRP].rearrange("p b t -> p t b"),
                                              mix[HD * g:HD * g + HD, 0:GRP, SEQ:ROWS])
                    ins.then_inc(sem("qp_done"), 1)
                if step[0] == "s_turn":
                    dve.wait_ge(sem("s_turn"), 1)
                    then(dve.tensor_reduce(sst[0:n, 0:1], BP[0:n, 0:P], AX.X, ALU.max))
                    then(dve.tensor_scalar(sst[0:n, 0:1], sst[0:n, 0:1], SCALE, sinkc[:, 0:1], ALU.mult, ALU.max))
                    then(dve.tensor_scalar(sst[0:n, 1:2], sst[0:n, 0:1], -1.0, None, ALU.mult))
                    dve.tensor_tensor(sst[0:n, 2:3], sinkc[:, 0:1], sst[0:n, 1:2], ALU.add).then_inc(sem("s_max"), 1)
                    dve.wait_ge(sem("s_exp"), 1)
                    then(dve.tensor_tensor(sst[0:n, 3:4], sst[0:n, 3:4], sst[0:n, 4:5], ALU.add))
                    then(dve.reciprocal(sst[0:n, 4:5], sst[0:n, 3:4]))
                    dve.tensor_scalar(px[:], px[:], sst[0:n, 4:5], None, ALU.mult).then_inc(sem("s_prob"), 1)
                if step[0] == "s_out":
                    dve.wait_ge(sem("s_out"), 1)
                    for g in range(NKV):
                        ov = BO[HD * g:HD * g + HD, 0:n].rearrange("p (b t) -> p t b", t=NQ)
                        ins = dve.tensor_copy(mix[HD * g:HD * g + HD, 0:GRP, SEQ:ROWS], ov[:, GRP * g:GRP * g + GRP, :])
                    ins.then_inc(sem("s_mixed"), 1)
                if step[0] == "r_turn":
                    h = step[1]
                    dve.wait_ge(sem("s_ki"), h + 1)
                    if h == 0:
                        dve.wait_ge(sem("stored"), 64)
                    dve.tensor_tensor(ib[:], bc(ki[:, 1, :].unsqueeze(1), [DECB, DECB, P]),
                                      bc(ident[0:DECB, 0:DECB].unsqueeze(2), [DECB, DECB, P]), ALU.mult).then_inc(sem("s_ib"), 1)
                if step[0] == "r_outer":
                    h = step[1]
                    dve.wait_ge(sem("s_outer"), h + 1)
                    dve.wait_ge(sem("st_scaled"), h + 1)
                    for a, b in ((0, BS), (1, BO)):
                        dve.tensor_tensor(st[:, 4 * a:4 * a + 4, :], st[:, 4 * a:4 * a + 4, :], b.rearrange("p (b d) -> p b d", b=4),
                                          ALU.add).then_inc(sem("s_state"), 1)
                if step[0] == "r_o":
                    h = step[1]
                    dve.wait_ge(sem("s_o"), h + 1)
                    dve.tensor_copy(o_s[:, h, :], BP[:, 0:DECB]).then_inc(sem("s_os"), 1)
                if step[0] == "r_rows":
                    n = NREC * DECB
                    dve.wait_ge(sem("so_std"), 1)
                    then(dve.reciprocal(sst[0:n, 7:8], sst[0:n, 6:7]))
                    dve.tensor_scalar(px[0:n, :], BP[0:n, 0:P], sst[0:n, 7:8], 0.25, ALU.mult, ALU.mult).then_inc(sem("so_norm"), 1)
                if step[0] == "r_cols":
                    n = NREC * DECB
                    dve.wait_ge(sem("so_cols"), 1)
                    then(dve.tensor_tensor(o_s[:], BP[:, 0:n].rearrange("p (h b) -> p h b", h=NREC),
                                           bc(rnorm[:].unsqueeze(2), [P, NREC, DECB]), ALU.mult))
            if tick % 2:
                unit_read(tick // 2)
                i = tick // 2 - (UNITS - CH)
                if i >= 0 and BACK[i] == CH - 1:
                    dve.tensor_tensor(mix[:, 4:8, SEQ:ROWS], o_s[:], g_s[:], ALU.mult).then_inc(sem("mix_done"), 1)
                if i >= 0:
                    mix_low(i)

        def hidden(q, e, first=False):
            dve.wait_ge(sem("up_mm"), q + 1)
            dve.wait_ge(sem("gate_done"), q + 1)
            if not first:
                dve.wait_ge(sem("h_lo_done"), q - 1)
            dve.tensor_tensor(hf[:, e, :], bank[2 + e][:, 0:CW], sg[:, e, :], ALU.mult).then_inc(sem("hf_done"), 1)

        for slot in range(SLOTS):
            for step, i in row_steps(slot):
                w = rows_of(back_row(i))[1]
                if step == "out":
                    dve.wait_ge(sem("p_std"), i + 1)
                    then(dve.reciprocal(rstd[0:w, 0, i:i + 1], std[0:w, 0, i:i + 1]))
                    if i == 0:
                        dve.wait_ge(sem("g_in"), 48)
                    dve.scalar_tensor_tensor(out=tr[0:w, i % 2, :].rearrange("p (a b) -> p a b", a=2), in0=pair[2][0:w, :, :],
                                             scalar=rstd[0:w, 0, i:i + 1], in1=gbl[0:w, :].rearrange("p (a b) -> p a b", a=2),
                                             op0=ALU.mult, op1=ALU.mult).then_inc(sem("p_t"), 1)
                    if i in X2_VECTOR:
                        add_x(dve, i)
                if step == "mid":
                    dve.wait_ge(sem("q_std"), i + 1)
                    then(dve.reciprocal(rstd[0:w, 1, i:i + 1], std[0:w, 1, i:i + 1]))
                    dve.scalar_tensor_tensor(out=tr[0:w, i % 2, :], in0=x2r[0:w, i % 2, :], scalar=rstd[0:w, 1, i:i + 1],
                                             in1=gb2[0:w, :], op0=ALU.mult, op1=ALU.mult).then_inc(sem("h2_rows"), 1)
                if step == "in":
                    low(i, "h2_hi", "h2_lo", bank[6:8], back_row(i))
            if slot >= 24 and slot % 2:
                q = (slot - 24) // 2
                hidden(q, q % 2, q < 2)

        def last_rows(i):
            r, w = rows_of(i)
            dve.wait_ge(sem("y_std"), i + 1)
            then(dve.reciprocal(rstd[0:w, 1, i:i + 1], std[0:w, 1, i:i + 1]))
            if i == 0:
                dve.wait_ge(sem("g_in"), 64)
            dve.scalar_tensor_tensor(out=ty[0:w, i % 4, :].rearrange("p (a b) -> p a b", a=2), in0=pair[i % 2][0:w, :, :],
                                     scalar=rstd[0:w, 1, i:i + 1], in1=gbl[0:w, :].rearrange("p (a b) -> p a b", a=2),
                                     op0=ALU.mult, op1=ALU.mult).then_inc(sem("y_t"), 1)
            if i in Y_VECTOR:
                dve.wait_ge(sem("y_t"), i + 1)
                dve.wait_ge(*x2_back(i))
                dve.tensor_tensor(x2b[0:w, i, :], ty[0:w, i % 4, :], x2b[0:w, i, :], ALU.add).then_inc(sem("y_vector"), 1)

        def up(g):
            for j in range(2):
                for c in range(CH):
                    hidden(6 * g + (3 * j + c), (3 * j + c) % 2)

        def down(g, first=False, last=False):
            if not first:
                dve.wait_ge(sem("acc_done"), 24 * g)
            for c, (c0, cw) in enumerate(LAST_CHUNKS if last else CHUNKS[::-1] if first else CHUNKS):
                for m in range(KT):
                    v = KT * c + m
                    dve.wait_ge(sem("down_mm"), 24 * g + (v + 1))
                    src, acc = bank[4 + v % 4][:, 0:cw], mix[:, m, c0:c0 + cw]
                    if first:
                        dve.tensor_copy(acc, src).then_inc(sem("acc_done"), 1)
                    else:
                        dve.tensor_tensor(acc, acc, src, ALU.add).then_inc(sem("acc_done"), 1)
                    if last and v - 2 in LAST_ROWS:
                        last_rows(LAST_ROWS.index(v - 2))

        down(0, True)
        with dve.Fori(1, GROUPS - 1) as g:
            up(g)
            down(g)
        up(GROUPS - 1)
        down(GROUPS - 1, False, True)
        for i in range(len(LAST_ROWS), RT):
            last_rows(i)

    block.__exit__(None, None, None)


_OUTS = [("y_prompt", (1, SEQ, DM)), ("y_sample", (DECB, 1, DM)), ("k_p", (1, 1, WIN, NKV, HD)), ("v_p", (1, 1, WIN, NKV, HD)),
         ("st_p", (1, 1, NREC, RD, RD)), ("k_s", (1, DECB, WIN, NKV, HD)), ("v_s", (1, DECB, WIN, NKV, HD)),
         ("st_s", (1, DECB, NREC, RD, RD))]


def kernel(**inputs):
    import concourse.bacc as bacc
    from concourse.bass_utils import run_bass_kernel_spmd

    nc = bacc.Bacc("TRN2", target_bir_lowering=False, num_devices=1)
    arrays = {name: np.ascontiguousarray(a) for name, a in inputs.items()}
    arrays.update(shape_constants())
    t_in = {name: nc.dram_tensor(f"{name}_dram", a.shape, mybir.dt.from_np(a.dtype), kind="ExternalInput").ap()
            for name, a in arrays.items()}
    t_out = {name: nc.dram_tensor(f"{name}_out", shape, F32, kind="ExternalOutput").ap() for name, shape in _OUTS}
    build(nc, t_in, t_out)
    r = run_bass_kernel_spmd(nc, [{f"{name}_dram": a for name, a in arrays.items()}], core_ids=[0])
    return tuple(r.results[0][f"{name}_out"] for name, _ in _OUTS)
```
